# Optimizing a Trainium2 kernel written in Bass

```python
import jax, jax.numpy as jnp
from jax import lax
import numpy as np

D_MODEL = 1024
BATCH = 1
SEQ = 256
DEPTH = 2

HEAD_DIM = 64
ATT_HEADS = (D_MODEL // 2) // HEAD_DIM
ATT_WIDTH = ATT_HEADS * HEAD_DIM
DILATED_BRANCHES = ((128, 1), (512, 4), (2048, 16))
ATT_BLOCK = 128
CONV_WIDTH = D_MODEL // 4
CONV_K = 3
GLA_HEADS = 4
GLA_VAL_WIDTH = D_MODEL // 4
GLA_KEY_WIDTH = GLA_VAL_WIDTH // 2
GLA_DV = GLA_VAL_WIDTH // GLA_HEADS
GLA_DK = GLA_KEY_WIDTH // GLA_HEADS
GLA_GATE_RANK = 16
GLA_GATE_TAU = 16.0
GLA_CHUNK = 32
MIX_WIDTH = ATT_WIDTH + CONV_WIDTH + GLA_VAL_WIDTH
IN_WIDTHS = (ATT_WIDTH, ATT_WIDTH, ATT_WIDTH,
             CONV_WIDTH, CONV_WIDTH, CONV_WIDTH,
             GLA_KEY_WIDTH, GLA_KEY_WIDTH,
             GLA_VAL_WIDTH, GLA_VAL_WIDTH,
             GLA_GATE_RANK)
IN_TOTAL = sum(IN_WIDTHS)
D_FF_DENSE = 2816
N_EXPERTS = 8
TOP_K = 2
D_FF_EXPERT = 3584
ROPE_THETA = 10000.0
EPS = 1e-6
NEG = -1e30

kernel_name = "hybrid_dilated_conv_gla_moe_trunk"

def rmsnorm(x, g):
    xf = x.astype(jnp.float32)
    y = xf * lax.rsqrt(jnp.mean(xf * xf, axis=-1, keepdims=True) + EPS)
    return (y * g.astype(jnp.float32)).astype(x.dtype)

def rope_tables(seq, dim):
    inv = 1.0 / (ROPE_THETA ** (jnp.arange(0, dim, 2, dtype=jnp.float32) / dim))
    ang = jnp.arange(seq, dtype=jnp.float32)[:, None] * inv[None, :]
    return jnp.cos(ang), jnp.sin(ang)

def apply_rope(x, cos, sin):
    x1, x2 = jnp.split(x.astype(jnp.float32), 2, axis=-1)
    c = cos[None, :, None, :]
    s = sin[None, :, None, :]
    return jnp.concatenate([x1 * c - x2 * s, x1 * s + x2 * c], axis=-1)

def dilated_branch(q, k, v, window, dilation):
    b, s, h, d = q.shape
    n_back = window // dilation
    assert n_back <= ATT_BLOCK
    L = s // dilation
    nb = -(-L // ATT_BLOCK)
    Lp = nb * ATT_BLOCK

    def to_strided(t):
        t = t.reshape(b, L, dilation, h, d).transpose(0, 2, 3, 1, 4)
        t = jnp.pad(t, ((0, 0), (0, 0), (0, 0), (0, Lp - L), (0, 0)))
        return t.reshape(b, dilation, h, nb, ATT_BLOCK, d)

    def with_prev(t):
        prev = jnp.pad(t, ((0, 0), (0, 0), (0, 0), (1, 0), (0, 0), (0, 0)))[:, :, :, :-1]
        return jnp.concatenate([prev, t], axis=4)

    qs = to_strided(q)
    kk = with_prev(to_strided(k))
    vv = with_prev(to_strided(v))
    scores = jnp.einsum('brhnqd,brhnkd->brhnqk', qs, kk) * (d ** -0.5)
    blk = jnp.arange(nb)[:, None, None]
    qi = blk * ATT_BLOCK + jnp.arange(ATT_BLOCK)[None, :, None]
    ki = (blk - 1) * ATT_BLOCK + jnp.arange(2 * ATT_BLOCK)[None, None, :]
    diff = qi - ki
    valid = (diff >= 0) & (diff <= n_back) & (ki >= 0)
    scores = jnp.where(valid, scores, NEG)
    mx = jnp.max(scores, axis=-1)
    p = jnp.where(valid, jnp.exp(scores - mx[..., None]), 0.0)
    den = jnp.sum(p, axis=-1)
    num = jnp.einsum('brhnqk,brhnkd->brhnqd', p, vv)

    def from_strided(t):
        tail = t.shape[5:]
        t = t.reshape((b, dilation, h, Lp) + tail)[:, :, :, :L]
        perm = (0, 3, 1, 2) + tuple(range(4, t.ndim))
        return t.transpose(perm).reshape((b, s, h) + tail)

    return from_strided(num), from_strided(den), from_strided(mx)

def dilated_attention(q, k, v):
    outs = [dilated_branch(q, k, v, w, dl) for (w, dl) in DILATED_BRANCHES]
    m_all = jnp.max(jnp.stack([o[2] for o in outs]), axis=0)
    num = 0.0
    den = 0.0
    for n_i, d_i, m_i in outs:
        w_i = jnp.exp(m_i - m_all)
        num = num + w_i[..., None] * n_i
        den = den + w_i * d_i
    return num / den[..., None]

def short_gated_conv(gate_b, gate_c, hin, conv_w):
    u = gate_c * hin
    y = lax.conv_general_dilated(u, conv_w[:, None, :].astype(u.dtype), window_strides=(1,),
                                 padding=[(CONV_K - 1, 0)],
                                 dimension_numbers=('NWC', 'WIO', 'NWC'),
                                 feature_group_count=u.shape[-1])
    return gate_b * y

def gla(q, k, v, log_a, out_gate, norm_g):
    f32 = jnp.float32
    b, s, h, dk = q.shape
    dv = v.shape[-1]
    C = GLA_CHUNK
    n = s // C

    def chunk(t):
        return t.astype(f32).reshape(b, n, C, h, -1).transpose(0, 3, 1, 2, 4)

    qc = chunk(q) * (dk ** -0.5)
    kc, vc, ac = chunk(k), chunk(v), chunk(log_a)
    bcum = jnp.cumsum(ac, axis=3)
    causal = jnp.tril(jnp.ones((C, C), dtype=bool))[..., None]
    diff = bcum[:, :, :, :, None, :] - bcum[:, :, :, None, :, :]
    decay = jnp.where(causal, jnp.exp(jnp.minimum(diff, 0.0)), 0.0)
    attn = jnp.einsum('bhntk,bhnsk,bhntsk->bhnts', qc, kc, decay)
    o_intra = jnp.einsum('bhnts,bhnsv->bhntv', attn, vc)
    b_last = bcum[:, :, :, -1, :]
    k_to_end = kc * jnp.exp(b_last[:, :, :, None, :] - bcum)
    chunk_state = jnp.einsum('bhnsk,bhnsv->bhnkv', k_to_end, vc)

    def step(state, inp):
        a_last, upd = inp
        return jnp.exp(a_last)[..., None] * state + upd, state

    init = jnp.zeros((b, h, dk, dv), f32)
    _, s_prev = lax.scan(step, init, (jnp.moveaxis(b_last, 2, 0), jnp.moveaxis(chunk_state, 2, 0)))
    s_prev = jnp.moveaxis(s_prev, 0, 2)
    o_inter = jnp.einsum('bhntk,bhnkv->bhntv', qc * jnp.exp(bcum), s_prev)
    o = (o_intra + o_inter).transpose(0, 2, 3, 1, 4).reshape(b, s, h, dv)
    o = o * lax.rsqrt(jnp.mean(o * o, axis=-1, keepdims=True) + EPS)
    return o.reshape(b, s, h * dv) * norm_g.astype(f32) * jax.nn.silu(out_gate.astype(f32))

def hybrid_mixer(hn, w_in, w_gate_lr, b_gate_lr, conv_w, gla_norm, w_out, cos, sin):
    b, s, _ = hn.shape
    split_pts = [int(p) for p in np.cumsum(IN_WIDTHS)[:-1]]
    proj = hn @ w_in
    (q_a, k_a, v_a, c_b, c_c, c_h, g_q, g_k, g_v, g_o, g_z) = jnp.split(proj, split_pts, axis=-1)
    qa = apply_rope(q_a.reshape(b, s, ATT_HEADS, HEAD_DIM), cos, sin)
    ka = apply_rope(k_a.reshape(b, s, ATT_HEADS, HEAD_DIM), cos, sin)
    va = v_a.reshape(b, s, ATT_HEADS, HEAD_DIM).astype(jnp.float32)
    att = dilated_attention(qa, ka, va).reshape(b, s, ATT_WIDTH)
    cv = short_gated_conv(c_b, c_c, c_h, conv_w)
    log_a = jax.nn.log_sigmoid((g_z @ w_gate_lr + b_gate_lr).astype(jnp.float32)) / GLA_GATE_TAU
    gl = gla(g_q.reshape(b, s, GLA_HEADS, GLA_DK), g_k.reshape(b, s, GLA_HEADS, GLA_DK),
             g_v.reshape(b, s, GLA_HEADS, GLA_DV), log_a.reshape(b, s, GLA_HEADS, GLA_DK),
             g_o, gla_norm)
    mix = jnp.concatenate([att.astype(hn.dtype), cv.astype(hn.dtype), gl.astype(hn.dtype)], axis=-1)
    return mix @ w_out

def swiglu(h, wg, wu, wd):
    return (jax.nn.silu(h @ wg) * (h @ wu)) @ wd

def moe_swiglu(h, router, eg, eu, ed):
    b, s, d = h.shape
    t = h.reshape(b * s, d)
    logits = (t @ router).astype(jnp.float32)
    top_v, top_i = lax.top_k(logits, TOP_K)
    top_w = jax.nn.softmax(top_v, axis=-1)
    combine = jnp.sum(jax.nn.one_hot(top_i, N_EXPERTS, dtype=jnp.float32) * top_w[..., None], axis=1)
    out = jnp.zeros((b * s, d), jnp.float32)
    for e in range(N_EXPERTS):
        out = out + combine[:, e:e + 1] * swiglu(t, eg[e], eu[e], ed[e]).astype(jnp.float32)
    return out.astype(h.dtype).reshape(b, s, d)

def setup_inputs(seed: int = 0) -> dict:
    key = jax.random.key(seed)
    ks = jax.random.split(key, 20)
    n_dense = (DEPTH + 1) // 2
    n_moe = DEPTH // 2
    nrm = jax.random.normal
    f32 = jnp.float32
    return {
        "x": nrm(ks[0], (BATCH, SEQ, D_MODEL), f32),
        "mix_norm": 1.0 + 0.02 * nrm(ks[1], (DEPTH, D_MODEL), f32),
        "w_in": nrm(ks[2], (DEPTH, D_MODEL, IN_TOTAL), f32) * D_MODEL ** -0.5,
        "w_gate_lr": nrm(ks[3], (DEPTH, GLA_GATE_RANK, GLA_KEY_WIDTH), f32) * GLA_GATE_RANK ** -0.5,
        "b_gate_lr": 0.1 * nrm(ks[4], (DEPTH, GLA_KEY_WIDTH), f32),
        "conv_w": nrm(ks[5], (DEPTH, CONV_K, CONV_WIDTH), f32) * CONV_K ** -0.5,
        "gla_norm": 1.0 + 0.02 * nrm(ks[6], (DEPTH, GLA_VAL_WIDTH), f32),
        "w_out": nrm(ks[7], (DEPTH, MIX_WIDTH, D_MODEL), f32) * MIX_WIDTH ** -0.5,
        "ffn_norm": 1.0 + 0.02 * nrm(ks[8], (DEPTH, D_MODEL), f32),
        "dense_w_gate": nrm(ks[9], (n_dense, D_MODEL, D_FF_DENSE), f32) * D_MODEL ** -0.5,
        "dense_w_up": nrm(ks[10], (n_dense, D_MODEL, D_FF_DENSE), f32) * D_MODEL ** -0.5,
        "dense_w_down": nrm(ks[11], (n_dense, D_FF_DENSE, D_MODEL), f32) * D_FF_DENSE ** -0.5,
        "router": nrm(ks[12], (n_moe, D_MODEL, N_EXPERTS), f32) * D_MODEL ** -0.5,
        "exp_w_gate": nrm(ks[13], (n_moe, N_EXPERTS, D_MODEL, D_FF_EXPERT), f32) * D_MODEL ** -0.5,
        "exp_w_up": nrm(ks[14], (n_moe, N_EXPERTS, D_MODEL, D_FF_EXPERT), f32) * D_MODEL ** -0.5,
        "exp_w_down": nrm(ks[15], (n_moe, N_EXPERTS, D_FF_EXPERT, D_MODEL), f32) * D_FF_EXPERT ** -0.5,
        "final_norm": 1.0 + 0.02 * nrm(ks[16], (D_MODEL,), f32),
    }

def reference(x, mix_norm, w_in, w_gate_lr, b_gate_lr, conv_w, gla_norm, w_out, ffn_norm,
              dense_w_gate, dense_w_up, dense_w_down, router, exp_w_gate, exp_w_up, exp_w_down,
              final_norm):
    cos, sin = rope_tables(x.shape[1], HEAD_DIM)
    h = x
    for i in range(DEPTH):
        hn = rmsnorm(h, mix_norm[i])
        h = h + hybrid_mixer(hn, w_in[i], w_gate_lr[i], b_gate_lr[i], conv_w[i], gla_norm[i],
                             w_out[i], cos, sin)
        hn = rmsnorm(h, ffn_norm[i])
        j = i // 2
        if i % 2 == 0:
            h = h + swiglu(hn, dense_w_gate[j], dense_w_up[j], dense_w_down[j])
        else:
            h = h + moe_swiglu(hn, router[j], exp_w_gate[j], exp_w_up[j], exp_w_down[j])
    return rmsnorm(h, final_norm)


_drawn_inputs = setup_inputs


def setup_inputs(seed=0):
    import zlib

    import numpy as np

    out = dict(_drawn_inputs(seed))
    spreads = {}
    factors = {'gla_norm': 3.219, 'final_norm': 2.866}
    for name, (base, spread) in spreads.items():
        noise = np.random.default_rng([zlib.crc32(name.encode()), seed]).standard_normal(out[name].shape)
        drawn = base * np.exp(spread * noise) if base else spread * noise
        out[name] = __import__('jax').numpy.asarray(drawn.astype(out[name].dtype))
    for name, factor in factors.items():
        out[name] = (out[name] * factor).astype(out[name].dtype)
    return out
```

```python
from contextlib import ExitStack

import numpy as np

import concourse.bass as bass
from concourse import mybir

F32 = mybir.dt.float32
F32R = mybir.dt.float32r
I32 = mybir.dt.int32
U32 = mybir.dt.uint32
U8 = mybir.dt.uint8
ALU = mybir.AluOpType
ACT = mybir.ActivationFunctionType
AX_X = mybir.AxisListType.X

P = 128
D = 1024
SEQ = 256
TT = SEQ // P
KT = D // P
DEPTH = 2
EPS = 1e-6
NEG = -1e30
HEADS = 8
HD = 64
BRANCHES = ((128, 1), (512, 4), (2048, 16))
ROPE_THETA = 10000.0
GH = 4
GK = 32
GV = 64
TAU = 16.0
RANK = 16
F_DENSE = 2816
N_EXP = 8
F_EXP = 3584
FB = 256

UNIT = 2048
RAW = 6
SPLIT = 3
MIX_UNITS = 16
DENSE_BLOCKS = F_DENSE // FB
EXP_BLOCKS = F_EXP // FB
DENSE_UNITS = 3 * DENSE_BLOCKS
EXP_UNITS = 3 * EXP_BLOCKS
BASE_MIX = (0, MIX_UNITS + DENSE_UNITS)
BASE_DENSE = MIX_UNITS
BASE_MOE = 2 * MIX_UNITS + DENSE_UNITS
ALL_UNITS = BASE_MOE + N_EXP * EXP_UNITS
assert DENSE_BLOCKS % 2 == 1 and EXP_BLOCKS % 2 == 0 and EXP_UNITS % RAW == 0

RS_NORM, RS_GLA = (1, 3, 4, 6, 7), (2, 5)
LEVELS = (128, 64, 32, 16, 8, 4, 2, 1)

C_ID, C_TRI, C_ONES, C_STRI, C_IOTA = 0, 128, 256, 384, 512
C_LNC = 640
C_ROPE = C_LNC + 3 * P
C_E8 = C_ROPE + 2 * TT * HD
C_ALL = C_E8 + 8


def shape_constants():
    c = np.zeros((P, C_ALL), np.float32)
    i = np.arange(P)
    c[:, C_ID:C_ID + P] = np.eye(P)
    c[:, C_TRI:C_TRI + P] = i[:, None] <= i[None, :]
    c[:, C_ONES:C_ONES + P] = 1.0
    c[:, C_STRI:C_STRI + P] = i[:, None] < i[None, :]
    c[:, C_IOTA:C_IOTA + P] = i[None, :]
    t = np.arange(SEQ)
    diff = t[:, None] - t[None, :]
    count = np.zeros((SEQ, SEQ))
    for window, step in BRANCHES:
        count += (diff >= 0) & (diff % step == 0) & (diff // step <= window // step)
    lnc = np.where(count > 0, np.log(np.maximum(count, 1)), NEG)
    c[:, C_LNC:C_LNC + P] = lnc[:P, :P]
    c[:, C_LNC + P:C_LNC + 3 * P] = lnc[P:]
    inv = (1.0 / (np.float32(ROPE_THETA) ** (np.arange(0, HD, 2, dtype=np.float32) / np.float32(HD)))).astype(np.float32)
    ang = (t.astype(np.float32)[:, None] * inv[None, :]).astype(np.float32).astype(np.float64)
    cos = np.concatenate([np.cos(ang), np.cos(ang)], 1)
    sin = np.concatenate([-np.sin(ang), np.sin(ang)], 1)
    rope = np.stack([cos, sin])
    c[:, C_ROPE:C_E8] = rope.reshape(2, TT, P, HD).transpose(2, 0, 1, 3).reshape(P, -1)
    c[:, C_E8:C_E8 + 8] = np.arange(8)
    m = np.zeros((P, len(LEVELS), P), np.float32)
    for n, half in enumerate(LEVELS[1:]):
        same = i[:, None] // (2 * half) == i[None, :] // (2 * half)
        m[:, n] = same & (i[:, None] % (2 * half) < half) & (i[None, :] % (2 * half) >= half)
    m[:, -1] = np.eye(P)
    return c, m


def build(nc, x, stream, w_z, w_gate, conv_w, gla_gain, gains, router, consts, masks, out):
    with ExitStack() as ctx:
        def sb(name, shape, dt=F32):
            return ctx.enter_context(nc.sbuf_tensor(name, shape, dt))

        def sem(name):
            return ctx.enter_context(nc.semaphore(name))

        ps = ctx.enter_context(nc.psum_tensor("ps", [P, 8, 512], F32))

        raw = sb("raw", [P, RAW, UNIT])
        w_hi = sb("w_hi", [P, SPLIT, UNIT], F32R)
        w_lo = sb("w_lo", [P, SPLIT, UNIT], F32R)
        h = sb("h", [P, TT, D])
        xT_hi = sb("xT_hi", [P, KT, SEQ], F32R)
        xT_lo = sb("xT_lo", [P, KT, SEQ], F32R)
        mix_hi = sb("mix_hi", [P, KT * SEQ], F32R)
        mix_lo = sb("mix_lo", [P, KT * SEQ], F32R)
        mixT_hi = mix_hi[:, :].rearrange("p (k t) -> p k t", k=KT)
        mixT_lo = mix_lo[:, :].rearrange("p (k t) -> p k t", k=KT)
        tok_hi = mix_hi[:, :].rearrange("p (t d) -> p t d", t=TT)
        tok_lo = mix_lo[:, :].rearrange("p (t d) -> p t d", t=TT)
        big = sb("big", [P, 8 * D])
        work = sb("work", [P, 2 * D])
        small = sb("small", [P, 2 * D])
        cst = sb("cst", [P, C_ALL])
        msk = sb("msk", [P, len(LEVELS), P], U8)
        gain = sb("gain", [P, D])
        gate_x = sb("gate_x", [P, 2, FB])
        act_x = sb("act_x", [P, 2, FB])
        aT_hi = sb("aT_hi", [P, 2, 2, P], F32R)
        aT_lo = sb("aT_lo", [P, 2, 2, P], F32R)
        wz = sb("wz", [P, KT, RANK])
        wz_hi = sb("wz_hi", [P, KT, RANK], F32R)
        wz_lo = sb("wz_lo", [P, KT, RANK], F32R)
        wg = sb("wg", [RANK + 1, P])
        zT = sb("zT", [RANK + 1, SEQ])
        z_sb = sb("z_sb", [P, TT, RANK])
        cw = sb("cw", [P, DEPTH, 2, 3])
        gg = sb("gg", [P, DEPTH, 2])
        ss = sb("ss", [P, TT])
        rs = sb("rs", [P, 8])
        nwt = sb("nwt", [P, 8])
        mx = sb("mx", [P, 2, 2])
        nmx = sb("nmx", [P, 2, 2])
        den = sb("den", [P, 2, 2])
        rden = sb("rden", [P, 2, 2])
        gss = sb("gss", [P, 8])
        ix8 = sb("ix8", [P, TT, 8], U32)
        zero8 = sb("zero8", [P, 8])
        over_f = sb("over_f", [P, 4])
        over_i = sb("over_i", [P, 4], I32)
        rt = sb("rt", [P, KT, 8])
        rt_hi = sb("rt_hi", [P, KT, 8], F32R)
        rt_lo = sb("rt_lo", [P, KT, 8], F32R)
        w_slot = sb("w_slot", [P, 1])
        disp = sb("disp", [P, TT, P], F32R)

        ident = cst[:, C_ID:C_ID + P]
        tri = cst[:, C_TRI:C_TRI + P]
        tri_ones = cst[:, C_TRI:C_TRI + 2 * P]
        ones = cst[:, C_ONES:C_ONES + P]
        stri = cst[:, C_STRI:C_STRI + P]
        iota = cst[:, C_IOTA:C_IOTA + P]
        lnc = cst[:, C_LNC:C_LNC + 3 * P]
        rope = cst[:, C_ROPE:C_E8].rearrange("p (a t d) -> p a t d", a=2, t=TT)
        iota8 = cst[:, C_E8:C_E8 + 8]

        hn = big[:, 0:2048].rearrange("p (t d) -> p t d", t=TT)
        rope_t1 = big[:, 0:1024].rearrange("p (t n) -> p t n", t=TT)
        rope_t2 = big[:, 1024:2048].rearrange("p (t n) -> p t n", t=TT)
        ke = big[:, 0:2048].rearrange("p (l t) -> p l t", l=8)
        rot_q = big[:, 2048:3072].rearrange("p (t n) -> p t n", t=TT)
        rot_k = big[:, 3072:4096].rearrange("p (t n) -> p t n", t=TT)
        dec = big[:, 2048:4096].rearrange("p (l t) -> p l t", l=8)
        qT = big[:, 4096:5120].rearrange("p (a t) -> p a t", a=4)
        kT = big[:, 5120:6144].rearrange("p (a t) -> p a t", a=4)
        gat = big[:, 4096:5120].rearrange("p (h t q) -> p h t q", h=GH, t=TT)
        gax = big[:, 5120:5632].rearrange("p (h q) -> p h q", h=GH)
        osq = big[:, 5632:6144]
        v_sb = big[:, 6144:7168].rearrange("p (t n) -> p t n", t=TT)
        gvo = big[:, 7168:8192].rearrange("p (t n) -> p t n", t=TT)
        ys = big[:, :].rearrange("p (e d) -> p e d", e=N_EXP)
        qe = work[:, :].rearrange("p (l t) -> p l t", l=8)
        z_abs = work[:, 0:256].rearrange("p (t f) -> p t f", t=TT)
        z_log = work[:, 256:512].rearrange("p (t f) -> p t f", t=TT)
        log_a = work[:, 512:768].rearrange("p (t f) -> p t f", t=TT)
        slotT = work[:, :].rearrange("p (e t) -> p e t", e=N_EXP)
        probs = small[:, 0:768].rearrange("p (b n) -> p b n", b=2)
        probsT = small[:, 768:1536].rearrange("p (b n) -> p b n", b=2)
        cc = small[:, 1536:2048].rearrange("p (f t) -> p f t", f=2)
        g_qk = act_x[:, :, :]
        bcum = work[:, 768:1024]
        cu = gate_x[:, :, :]
        cy = work[:, 1024:1536].rearrange("p (f t) -> p f t", f=2)

        lg = small[:, 0:16].rearrange("p (t e) -> p t e", t=TT)
        mx8 = small[:, 16:32].rearrange("p (t e) -> p t e", t=TT)
        ixf = small[:, 32:36].rearrange("p (t e) -> p t e", t=TT)
        top1 = small[:, 36:52].rearrange("p (t e) -> p t e", t=TT)
        top2 = small[:, 52:68].rearrange("p (t e) -> p t e", t=TT)
        chosen = small[:, 68:84].rearrange("p (t e) -> p t e", t=TT)
        comb = small[:, 84:100].rearrange("p (t e) -> p t e", t=TT)
        slot = small[:, 100:116].rearrange("p (t e) -> p t e", t=TT)
        tw = small[:, 116:124].rearrange("p (t e) -> p t e", t=TT)
        flag = small[:, 124:132]
        cum = small[:, 132:140]
        sel = small[:, 140:148]

        in_x, in_cst, in_mask, in_small, in_gain, in_wz = (sem(n) for n in ("in_x", "in_cst", "in_mask", "in_small", "in_gain", "in_wz"))
        landed = [sem(f"landed{i}") for i in range(RAW)]
        hi_done, lo_done, unit_used = sem("hi_done"), sem("lo_done"), sem("unit_used")
        dve_chain, act_chain, pool_chain = sem("dve_chain"), sem("act_chain"), sem("pool_chain")
        sq_act, hn_done, hnT_ps, hnT_hi, hnT_lo = (sem(n) for n in ("sq_act", "hn_done", "hnT_ps", "hnT_hi", "hnT_lo"))
        mean_done, rs_start = sem("mean_done"), sem("rs_start")
        gain_used, res_done = sem("gain_used"), sem("res_done")
        wz_h, wz_l, z_ps, z_cp, zT_ps, zT_cp, zl_ps = (sem(n) for n in ("wz_h", "wz_l", "z_ps", "z_cp", "zT_ps", "zT_cp", "zl_ps"))
        zlog_done, loga_done, b_ps, b_cp = (sem(n) for n in ("zlog_done", "loga_done", "b_ps", "b_cp"))
        rope_mul, rope_add, qT_ps, kT_ps, qT_cp, kT_cp = (sem(n) for n in ("rope_mul", "rope_add", "qT_ps", "kT_ps", "qT_cp", "kT_cp"))
        v_cp, f_cp, t_cp = sem("v_cp"), sem("f_cp"), sem("t_cp")
        s_ps, s_max, s_exp, s_rden, s_norm, pT_ps, pT_cp, att_ps, att_hi, att_lo = (
            sem(n) for n in ("s_ps", "s_max", "s_exp", "s_rden", "s_norm", "pT_ps", "pT_cp", "att_ps", "att_hi", "att_lo"))
        conv_u, conv_y, conv_out, conv_hi, conv_lo = (sem(n) for n in ("conv_u", "conv_y", "conv_out", "conv_hi", "conv_lo"))
        dec_sub, dec_exp, qe_done, ke_done, lv_ps, lv_cp, o_ps, o_sq, og_exp, o_done, oT_ps, oT_hi, oT_lo = (
            sem(n) for n in ("dec_sub", "dec_exp", "qe_done", "ke_done", "lv_ps", "lv_cp", "o_ps", "o_sq", "og_exp", "o_done",
                             "oT_ps", "oT_hi", "oT_lo"))

        class FfnSems:
            def __init__(self, name):
                self.gu_first = sem(f"{name}_gu_first")
                self.silu = sem(f"{name}_silu")
                self.mul = sem(f"{name}_mul")
                self.aT_ps = sem(f"{name}_aT_ps")
                self.aT_hi = sem(f"{name}_aT_hi")
                self.aT_lo = sem(f"{name}_aT_lo")

        fd, fm = FfnSems("dense"), FfnSems("moe")
        rt_h, rt_l, lg_ps, lg_exp_in, lg_exp, chosen_done, pos_ps, route_done, tok_h, tok_l = (
            sem(n) for n in ("rt_h", "rt_l", "lg_ps", "lg_exp_in", "lg_exp", "chosen_done", "pos_ps", "route_done", "tok_h", "tok_l"))
        disp_done, ga_ps, ga_hi, ga_lo, slot_ps, slot_cp, y_free = (
            sem(n) for n in ("disp_done", "ga_ps", "ga_hi", "ga_lo", "slot_ps", "slot_cp", "y_free"))
        sc_ps, sc_add, ov_ps = sem("sc_ps"), sem("sc_add"), sem("ov_ps")
        fin_done, out_sem = sem("fin_done"), sem("out_sem")

        def load_unit(sp, n, d=0, row=None):
            if n >= RAW:
                sp.wait_ge(lo_done, d * RAW + (n - RAW + 1))
            row = d * RAW + n if row is None else row
            src = stream[row] if isinstance(row, int) else stream[bass.ds(row, 1)].rearrange("a p c -> (a p) c")
            sp.dma_start(raw[:, n % RAW, :], src).then_inc(landed[n % RAW], 16)

        def hi_unit(act, n, d=0):
            act.wait_ge(landed[n % RAW], (d + (n // RAW + 1)) * 16)
            if n >= SPLIT:
                act.wait_ge(unit_used, d * RAW + (n - SPLIT + 1))
            nc.scalar.activation(w_hi[:, n % SPLIT, :], raw[:, n % RAW, :], ACT.Copy).then_inc(hi_done, 1)

        def lo_unit(dve, n, d=0):
            dve.wait_ge(hi_done, d * RAW + (n + 1))
            nc.vector.tensor_tensor(w_lo[:, n % SPLIT, :], raw[:, n % RAW, :], w_hi[:, n % SPLIT, :].bitcast(F32),
                                    ALU.subtract).then_inc(lo_done, 1)

        PASSES = ((0, 0), (1, 0), (0, 1))
        ALL_EXP = N_EXP * EXP_UNITS // RAW

        def w(n, part, a, b):
            return (w_hi, w_lo)[part][:, n % SPLIT, a:b]

        def used(eng, n, d=0):
            eng.wait_ge(unit_used, d * RAW + n)

        block = ctx.enter_context(nc.Block())

        @block.sync
        def _(sp):
            for n in range(RAW):
                if n == 1:
                    sp.dma_start(cst[:, :], consts).then_inc(in_cst, 16)
                if n == 0:
                    sp.dma_start(h[:, :, :], x.rearrange("a (t p) d -> p (a t) d", p=P)).then_inc(in_x, 16)
                load_unit(sp, n)
            for n in range(RAW, MIX_UNITS):
                load_unit(sp, n)
            with sp.Fori(0, DENSE_UNITS // RAW) as i:
                for j in range(RAW):
                    load_unit(sp, BASE_DENSE + j, i)
            for n in range(BASE_MIX[1] - DENSE_UNITS % RAW, BASE_MOE):
                load_unit(sp, n)
            with sp.Fori(0, N_EXP * EXP_UNITS // RAW) as i:
                for j in range(RAW):
                    load_unit(sp, BASE_MOE + j, i)
            sp.wait_ge(route_done, 1)
            n_over = sp.value_load(over_i[0:1, 0:1], min_val=0, max_val=3)
            with sp.If(n_over > 0):
                with sp.Fori(0, n_over) as k:
                    e = sp.value_load(over_i[0:1, bass.ds(k + 1, 1)], min_val=0, max_val=N_EXP - 1)
                    with sp.Fori(0, EXP_UNITS // RAW) as i:
                        for j in range(RAW):
                            load_unit(sp, BASE_MOE + j, k * (EXP_UNITS // RAW) + i + ALL_EXP,
                                      row=e * EXP_UNITS + i * RAW + (BASE_MOE + j))
            sp.wait_ge(fin_done, 2)
            sp.dma_start(out.rearrange("a (t p) d -> p (a t) d", p=P), hn[:, :, :]).then_inc(out_sem, 16)
            sp.wait_ge(out_sem, 16)

        @block.gpsimd
        def _(pool):
            chain = [0]

            def link(ins):
                chain[0] += 1
                ins.then_inc(pool_chain, 1)
                pool.wait_ge(pool_chain, chain[0])

            pool.dma_start(gain[:, :], gains[0:1, :].to_broadcast([P, D])).then_inc(in_gain, 16)
            pool.dma_start(wz[:, :, :], w_z[0]).then_inc(in_wz, 16)
            pool.dma_start(wg[:, :], w_gate[0]).then_inc(in_wz, 16)
            mask_f = big[:, 7168:8192].rearrange("p (n q) -> p n q", n=len(LEVELS))
            pool.dma_start(mask_f, masks).then_inc(in_mask, 16)
            pool.dma_start(cw[:, :, :, :], conv_w).then_inc(in_small, 16)
            pool.dma_start(gg[:, :, :], gla_gain).then_inc(in_small, 16)
            pool.dma_start(rt[:, :, :], router).then_inc(in_small, 16)
            nc.gpsimd.memset(zero8[:, :], 0.0)
            link(nc.gpsimd.memset(zT[:, :], 1.0))
            pool.wait_ge(in_mask, 16)
            link(nc.gpsimd.tensor_copy(msk[:, :, :], mask_f))
            for L in range(DEPTH):
                pool.wait_ge(gain_used, 2 * L + 1)
                pool.dma_start(gain[:, :], gains[2 * L + 1:2 * L + 2, :].to_broadcast([P, D])).then_inc(in_gain, 16)
                for n, rot in enumerate((rot_q, rot_k)):
                    pool.wait_ge(rope_mul, 2 * L + n + 1)
                    nc.gpsimd.tensor_tensor(rot[:, :, :], rope_t1[:, :, :], rope_t2[:, :, :], ALU.add).then_inc(rope_add, 1)
                for hd in range(HEADS):
                    b = hd % 2
                    pool.wait_ge(s_rden, HEADS * L + hd + 1)
                    nc.gpsimd.tensor_scalar(probs[:, b, 0:P], probs[:, b, 0:P], rden[:, b, 0:1], None, ALU.mult)
                    nc.gpsimd.tensor_scalar(probs[:, b, P:3 * P], probs[:, b, P:3 * P], rden[:, b, 1:2], None,
                                            ALU.mult).then_inc(s_norm, 1)
                pool.wait_ge(dec_exp, L + 1)
                pool.wait_ge(f_cp, 3 * L + 2)
                nc.gpsimd.tensor_tensor(ke[:, :, :], dec[:, :, :],
                                        g_qk[:, 1, :].unsqueeze(1).to_broadcast([P, 8, SEQ]), ALU.mult).then_inc(ke_done, 1)
                pool.wait_ge(gain_used, 2 * L + 2)
                if L == 0:
                    pool.dma_start(wz[:, :, :], w_z[1]).then_inc(in_wz, 16)
                    pool.dma_start(wg[:, :], w_gate[1]).then_inc(in_wz, 16)
                pool.dma_start(gain[:, :], gains[2 * L + 2:2 * L + 3, :].to_broadcast([P, D])).then_inc(in_gain, 16)

        @block.scalar
        def _(act):
            chain = [0]

            def link(ins):
                chain[0] += 1
                ins.then_inc(act_chain, 1)
                act.wait_ge(act_chain, chain[0])

            def copy(dst, src, scale=1.0):
                return nc.scalar.activation(dst, src, ACT.Copy, scale=scale)

            def rsqrt_start(src, n, count):
                act.wait_ge(mean_done, count)
                link(nc.scalar.activation(rs[:, 0:n], src, ACT.Ln))
                nc.scalar.activation(rs[:, 0:n], rs[:, 0:n], ACT.Exp, scale=-0.5).then_inc(rs_start, 1)

            def norm(i):
                if i == 0:
                    act.wait_ge(in_x, 16)
                else:
                    act.wait_ge(res_done, i)
                nc.scalar.activation(hn[:, 1, :], h[:, 1, :], ACT.Square, accum_out=ss[:, 1:2]).then_inc(sq_act, 1)
                rsqrt_start(ss[:, :], TT, RS_NORM[i])
                if i < 4:
                    for half in range(2):
                        act.wait_ge(hnT_ps, 2 * i + half + 1)
                        copy(xT_hi[:, 4 * half:4 * half + 4, :],
                             ps[:, 2 * half:2 * half + 2, :].rearrange("p b (k t) -> p (b k) t", k=2)).then_inc(hnT_hi, 1)

            def mixer(L):
                n0 = BASE_MIX[L]
                split = lambda j: hi_unit(act, n0 + j)
                act.wait_ge(in_wz, 32 * (L + 1))
                copy(wz_hi[:, :, :], wz[:, :, :]).then_inc(wz_h, 1)
                norm(2 * L)
                split(2)
                act.wait_ge(z_ps, L + 1)
                copy(z_sb[:, :, :], ps[:, 6, 0:TT * RANK].rearrange("p (t r) -> p t r", t=TT)).then_inc(z_cp, 1)
                split(3)
                act.wait_ge(zT_ps, L + 1)
                if L == 0:
                    act.wait_ge(pool_chain, 2)
                copy(zT[0:RANK, :], ps[0:RANK, 7, 0:SEQ]).then_inc(zT_cp, 1)
                split(4)
                split(5)
                split(6)
                act.wait_ge(zl_ps, L + 1)
                link(nc.scalar.activation(z_abs[:, :, :], ps[:, 6, SEQ:2 * SEQ].rearrange("p (t f) -> p t f", t=TT), ACT.Abs))
                link(nc.scalar.activation(z_log[:, :, :], z_abs[:, :, :], ACT.Exp, scale=-1.0))
                nc.scalar.activation(z_log[:, :, :], z_log[:, :, :], ACT.Ln, bias=1.0).then_inc(zlog_done, 1)
                split(7)
                used(act, n0 + 6)
                copy(v_sb[:, :, :], ps[:, 0:2, :]).then_inc(v_cp, 1)
                split(8)
                act.wait_ge(qT_ps, L + 1)
                copy(qT[:, :, :], ps[:, 4:6, :].rearrange("p b (a t) -> p (b a) t", a=2), HD ** -0.5).then_inc(qT_cp, 1)
                used(act, n0 + 8)
                copy(g_qk[:, 0, :], ps[:, 2, 0:SEQ], GK ** -0.5).then_inc(f_cp, 1)
                copy(g_qk[:, 1, :], ps[:, 2, SEQ:2 * SEQ]).then_inc(f_cp, 1)
                copy(cc[:, :, :], ps[:, 3, :].rearrange("p (f t) -> p f t", f=2)).then_inc(f_cp, 1)
                split(9)
                split(10)
                used(act, n0 + 10)
                copy(gvo[:, :, :], ps[:, 0:2, :]).then_inc(t_cp, 1)
                split(11)
                for step in range(HEADS + 2):
                    if step < HEADS:
                        b = step % 2
                        act.wait_ge(s_max, HEADS * L + step + 1)
                        nc.scalar.activation(probs[:, b, 0:P], probs[:, b, 0:P], ACT.Exp, bias=nmx[:, b, 0:1],
                                             accum_out=den[:, b, 0:1])
                        nc.scalar.activation(probs[:, b, P:3 * P], probs[:, b, P:3 * P], ACT.Exp, bias=nmx[:, b, 1:2],
                                             accum_out=den[:, b, 1:2]).then_inc(s_exp, 1)
                    if 1 <= step <= HEADS:
                        hd = step - 1
                        act.wait_ge(pT_ps, HEADS * L + hd + 1)
                        if hd >= 2:
                            act.wait_ge(att_ps, HEADS * L + hd - 1)
                        copy(probsT[:, hd % 2, :], ps[:, 6 + hd % 2, 0:3 * P]).then_inc(pT_cp, 1)
                    if step == 5:
                        split(12)
                    if step == 7:
                        split(13)
                    if step >= 3 and step % 2 == 1:
                        pair = (step - 3) // 2
                        act.wait_ge(att_ps, HEADS * L + 2 * pair + 2)
                        copy(mixT_hi[:, pair, :], ps[:, pair % 2, pair // 2 * SEQ:(pair // 2 + 1) * SEQ]).then_inc(att_hi, 1)
                split(14)
                act.wait_ge(dec_sub, L + 1)
                link(nc.scalar.activation(dec[:, :, :], dec[:, :, :], ACT.Abs))
                nc.scalar.activation(dec[:, :, :], dec[:, :, :], ACT.Exp, scale=-1.0 / TAU).then_inc(dec_exp, 1)
                act.wait_ge(conv_out, L + 1)
                copy(mixT_hi[:, 4:6, :], cy[:, :, :]).then_inc(conv_hi, 1)
                nc.scalar.activation(cc[:, :, :], gvo[:, :, SEQ:2 * SEQ], ACT.Exp, scale=-1.0).then_inc(og_exp, 1)
                act.wait_ge(o_ps, L + 1)
                nc.scalar.activation(osq, ps[:, 0, :], ACT.Square).then_inc(o_sq, 1)
                rsqrt_start(gss[:, :], 8, RS_GLA[L])
                act.wait_ge(oT_ps, L + 1)
                for f in range(2):
                    copy(mixT_hi[:, 6 + f, :], ps[:, 1 + f, 0:SEQ], gg[:, L, f:f + 1]).then_inc(oT_hi, 1)
                split(15)

            def ffn_block(S, tiles, B, par, n, d=0):
                for t in range(tiles):
                    s = t if tiles == 2 else par
                    if t < tiles - 1:
                        act.wait_ge(S.gu_first, B + 1)
                    else:
                        used(act, n, d)
                    nc.scalar.activation(gate_x[:, s, :], ps[:, 4 + s, 0:FB], ACT.Silu).then_inc(S.silu, 1)

            def ffn_aT(S, tiles, B, par):
                act.wait_ge(S.aT_ps, B + 1)
                if tiles == 2:
                    copy(aT_hi[:, :, :, :], ps[:, 6 + par, :].rearrange("p (t f q) -> p t f q", t=2, f=2)).then_inc(S.aT_hi, 1)
                else:
                    copy(aT_hi[:, par, :, :], ps[:, 6 + par, 0:FB].rearrange("p (f q) -> p f q", f=2)).then_inc(S.aT_hi, 1)

            def expert_start(e, n, d):
                for g in (0, 1):
                    act.wait_ge(ga_ps, e * 4 + (g + 1))
                    copy(xT_hi[:, 4 * g:4 * g + 4, 0:P], ps[:, 2 + g, :].rearrange("p (k s) -> p k s", k=4)).then_inc(ga_hi, 1)
                hi_unit(act, n, d)
                hi_unit(act, n + 1, d)
                hi_unit(act, n + 2, d)
                ffn_block(fm, 1, e * EXP_BLOCKS, 0, n + 2, d)
                hi_unit(act, n + 3, d)

            def expert_middle(e, n, d):
                with act.Fori(0, (EXP_BLOCKS - 2) // 2) as i:
                    for p in range(2):
                        B = e * EXP_BLOCKS + i * 2 + p
                        m = n + 4 + 3 * p
                        hi_unit(act, m, d + i)
                        ffn_aT(fm, 1, B, p)
                        hi_unit(act, m + 1, d + i)
                        ffn_block(fm, 1, B + 1, 1 - p, m, d + i)
                        hi_unit(act, m + 2, d + i)

            def expert_end(e, n, d, follow):
                B = e * EXP_BLOCKS + (EXP_BLOCKS - 2)
                hi_unit(act, n + EXP_UNITS - 2, d)
                ffn_aT(fm, 1, B, 0)
                hi_unit(act, n + EXP_UNITS - 1, d)
                ffn_block(fm, 1, B + 1, 1, n + EXP_UNITS - 2, d)
                if follow:
                    for g in (0, 1):
                        act.wait_ge(ga_ps, (e + 1) * 4 + (g + 1))
                        copy(xT_hi[:, 4 * g:4 * g + 4, 0:P],
                             ps[:, 2 + g, :].rearrange("p (k s) -> p k s", k=4)).then_inc(ga_hi, 1)
                    hi_unit(act, n, d + EXP_UNITS // RAW)
                ffn_aT(fm, 1, B + 1, 1)
                if follow:
                    hi_unit(act, n + 1, d + EXP_UNITS // RAW)

            def expert_out(e, n, d):
                used(act, n + EXP_UNITS, d)
                act.wait_ge(slot_cp, 3 * (e + 1))
                dst = ys[:, e, :] if isinstance(e, int) else ys[:, bass.ds(e, 1), :].rearrange("p a d -> p (a d)")
                copy(dst, ps[:, 0:2, :].rearrange("p a d -> p (a d)"), w_slot[:, 0:1]).then_inc(y_free, 1)

            act.sem_inc(y_free, 1)
            for n in range(2):
                hi_unit(act, n)
            mixer(0)
            n0 = BASE_DENSE
            hi_unit(act, n0)
            hi_unit(act, n0 + 1)
            norm(1)
            hi_unit(act, n0 + 2)
            ffn_block(fd, 2, 0, 0, n0 + 2)
            hi_unit(act, n0 + 3)
            with act.Fori(0, (DENSE_BLOCKS - 1) // 2) as i:
                for p in range(2):
                    B = i * 2 + p
                    m = n0 + 4 + 3 * p
                    hi_unit(act, m, i)
                    ffn_aT(fd, 2, B, p)
                    hi_unit(act, m + 1, i)
                    ffn_block(fd, 2, B + 1, 0, m, i)
                    hi_unit(act, m + 2, i)
            ffn_aT(fd, 2, DENSE_BLOCKS - 1, 0)
            hi_unit(act, BASE_MIX[1] + 1)
            mixer(1)
            act.wait_ge(in_small, 48)
            copy(rt_hi[:, :, :], rt[:, :, :]).then_inc(rt_h, 1)
            norm(3)
            act.wait_ge(hn_done, 8)
            copy(tok_hi[:, :, :], hn[:, :, :]).then_inc(tok_h, 1)
            act.wait_ge(lg_exp_in, 1)
            nc.scalar.activation(tw[:, :, 1:2], tw[:, :, 0:1], ACT.Exp).then_inc(lg_exp, 1)
            expert_start(0, BASE_MOE, 0)
            with act.Fori(0, N_EXP - 1) as e:
                d = e * (EXP_UNITS // RAW)
                expert_middle(e, BASE_MOE, d)
                expert_end(e, BASE_MOE, d + (EXP_UNITS // RAW) * 0, True)
                expert_out(e, BASE_MOE, d)
                hi_unit(act, BASE_MOE + 2, d + EXP_UNITS // RAW)
                ffn_block(fm, 1, (e + 1) * EXP_BLOCKS, 0, BASE_MOE + 2, d + EXP_UNITS // RAW)
                hi_unit(act, BASE_MOE + 3, d + EXP_UNITS // RAW)
            last = N_EXP - 1
            expert_middle(last, BASE_MOE, last * (EXP_UNITS // RAW))
            expert_end(last, BASE_MOE, last * (EXP_UNITS // RAW), False)
            expert_out(last, BASE_MOE, last * (EXP_UNITS // RAW))
            act.wait_ge(route_done, 1)
            n_over = act.value_load(over_i[0:1, 0:1], min_val=0, max_val=3)
            with act.If(n_over > 0):
                with act.Fori(0, n_over) as k:
                    e = k + N_EXP
                    d = k * (EXP_UNITS // RAW) + N_EXP * (EXP_UNITS // RAW)
                    expert_start(e, BASE_MOE, d)
                    expert_middle(e, BASE_MOE, d)
                    expert_end(e, BASE_MOE, d, False)
                    used(act, BASE_MOE + EXP_UNITS, d)
                    act.wait_ge(slot_cp, 3 * (e + 1))
                    copy(ys[:, 0, :], ps[:, 0:2, :].rearrange("p a d -> p (a d)"), w_slot[:, 0:1]).then_inc(y_free, 1)
            norm(4)

        @block.vector
        def _(dve):
            chain = [0]

            def link(ins):
                chain[0] += 1
                ins.then_inc(dve_chain, 1)
                dve.wait_ge(dve_chain, chain[0])

            def rsqrt_mean(src, n, width, count):
                y, t = rs[:, 0:n], nwt[:, 0:n]
                nc.vector.tensor_scalar(src, src, 1.0 / width, EPS, ALU.mult, ALU.add).then_inc(mean_done, 1)
                dve.wait_ge(rs_start, count)
                link(nc.vector.tensor_tensor(t, y, y, ALU.mult))
                link(nc.vector.tensor_tensor(t, t, src, ALU.mult))
                link(nc.vector.tensor_scalar(t, t, -0.5, 1.5, ALU.mult, ALU.add))
                link(nc.vector.tensor_tensor(y, y, t, ALU.mult))

            def norm(i):
                if i == 0:
                    dve.wait_ge(in_x, 16)
                link(nc.vector.tensor_tensor_reduce(out=hn[:, 0, :], in0=h[:, 0, :], in1=h[:, 0, :], scale=1.0, scalar=0.0,
                                                    op0=ALU.mult, op1=ALU.add, accum_out=ss[:, 0:1]))
                dve.wait_ge(sq_act, i + 1)
                rsqrt_mean(ss[:, :], TT, D, RS_NORM[i])
                dve.wait_ge(in_gain, 16 * (i + 1))
                for t in range(TT):
                    ins = nc.vector.scalar_tensor_tensor(out=hn[:, t, :], in0=h[:, t, :], scalar=rs[:, t:t + 1],
                                                         in1=gain[:, :], op0=ALU.mult, op1=ALU.mult)
                    ins.then_inc(fin_done if i == 4 else hn_done, 1)
                if i < 4:
                    dve.wait_ge(hn_done, 2 * (i + 1))
                    dve.sem_inc(gain_used, 1)
                    for half in range(2):
                        dve.wait_ge(hnT_hi, 2 * i + half + 1)
                        nc.vector.tensor_tensor(xT_lo[:, 4 * half:4 * half + 4, :],
                                                ps[:, 2 * half:2 * half + 2, :].rearrange("p b (k t) -> p (b k) t", k=2),
                                                xT_hi[:, 4 * half:4 * half + 4, :].bitcast(F32),
                                                ALU.subtract).then_inc(hnT_lo, 1)

            def rope_mults(first):
                x = ps[:, first:first + 2, :].rearrange("p t (h d) -> p t h d", h=HEADS)
                t1 = rope_t1[:, :, :].rearrange("p t (h d) -> p t h d", h=HEADS)
                t2 = rope_t2[:, :, :].rearrange("p t (h d) -> p t h d", h=HEADS)
                c = rope[:, 0].unsqueeze(2).to_broadcast([P, TT, HEADS, HD])
                s = rope[:, 1].unsqueeze(2).to_broadcast([P, TT, HEADS, HD])
                half = HD // 2
                nc.vector.tensor_tensor(t1, x, c, ALU.mult)
                nc.vector.tensor_tensor(t2[:, :, :, 0:half], x[:, :, :, half:HD], s[:, :, :, 0:half], ALU.mult)
                nc.vector.tensor_tensor(t2[:, :, :, half:HD], x[:, :, :, 0:half], s[:, :, :, half:HD],
                                        ALU.mult).then_inc(rope_mul, 1)

            def residual(n):
                used(dve, n)
                for t in range(TT):
                    for half in range(2):
                        ins = nc.vector.tensor_tensor(h[:, t, half * 512:(half + 1) * 512], h[:, t, half * 512:(half + 1) * 512],
                                                      ps[:, 2 * t + half, :], ALU.add)
                link(ins)
                dve.sem_inc(res_done, 1)

            def mixer(L):
                n0 = BASE_MIX[L]
                split = lambda j: lo_unit(dve, n0 + j)
                dve.wait_ge(wz_h, L + 1)
                nc.vector.tensor_tensor(wz_lo[:, :, :], wz[:, :, :], wz_hi[:, :, :].bitcast(F32), ALU.subtract).then_inc(wz_l, 1)
                norm(2 * L)
                split(2)
                split(3)
                used(dve, n0 + 2)
                rope_mults(0)
                split(4)
                split(5)
                zl = ps[:, 6, SEQ:2 * SEQ].rearrange("p (t f) -> p t f", t=TT)
                used(dve, n0 + 4)
                dve.wait_ge(rope_add, 2 * L + 1)
                rope_mults(2)
                split(6)
                dve.wait_ge(zlog_done, L + 1)
                nc.vector.scalar_tensor_tensor(out=log_a[:, :, :], in0=zl, scalar=0.0, in1=z_log[:, :, :], op0=ALU.min,
                                               op1=ALU.subtract).then_inc(loga_done, 1)
                split(7)
                split(8)
                dve.wait_ge(b_ps, L + 1)
                nc.vector.tensor_copy(bcum[:, :], ps[:, 7, SEQ:2 * SEQ]).then_inc(b_cp, 1)
                dve.wait_ge(kT_ps, L + 1)
                nc.vector.tensor_copy(kT[:, :, :], ps[:, 6:8, :].rearrange("p b (a t) -> p (b a) t", a=2)).then_inc(kT_cp, 1)
                split(9)
                split(10)
                dve.wait_ge(b_cp, L + 1)
                for n, half in enumerate(LEVELS):
                    b3 = bcum[:, :].rearrange("p (i j) -> p i j", j=2 * half)
                    ref = b3[:, :, half - 1:half].to_broadcast([P, SEQ // (2 * half), 2 * half])
                    ins = nc.vector.tensor_tensor(dec[:, n, :].rearrange("p (i j) -> p i j", j=2 * half), b3, ref, ALU.subtract)
                ins.then_inc(dec_sub, 1)
                split(11)
                for step in range(HEADS + 2):
                    if step < HEADS:
                        b = step % 2
                        dve.wait_ge(s_ps, HEADS * L + step + 1)
                        if step >= 2:
                            dve.wait_ge(pT_ps, HEADS * L + step - 1)
                        nc.vector.tensor_tensor_reduce(out=probs[:, b, 0:P], in0=ps[:, 4 + b, 0:P], in1=lnc[:, 0:P], scale=1.0,
                                                       scalar=-3e38, op0=ALU.add, op1=ALU.max, accum_out=mx[:, b, 0:1])
                        link(nc.vector.tensor_tensor_reduce(out=probs[:, b, P:3 * P], in0=ps[:, 4 + b, P:3 * P],
                                                            in1=lnc[:, P:3 * P], scale=1.0, scalar=-3e38, op0=ALU.add,
                                                            op1=ALU.max, accum_out=mx[:, b, 1:2]))
                        nc.vector.tensor_scalar(nmx[:, b, :], mx[:, b, :], -1.0, None, ALU.mult).then_inc(s_max, 1)
                    if 1 <= step <= HEADS:
                        hd = step - 1
                        dve.wait_ge(s_exp, HEADS * L + hd + 1)
                        nc.vector.reciprocal(rden[:, hd % 2, :], den[:, hd % 2, :]).then_inc(s_rden, 1)
                    if step == 5:
                        split(12)
                    if step == 7:
                        split(13)
                    if step == 6:
                        used(dve, n0 + 12)
                        dve.wait_ge(f_cp, 3 * L + 3)
                        link(nc.vector.tensor_tensor(cu, cc[:, :, :], ps[:, 2, :].rearrange("p (f t) -> p f t", f=2), ALU.mult))
                        for f in range(2):
                            u, y = cu[:, f, :], cy[:, f, :]
                            link(nc.vector.tensor_scalar(y, u, cw[:, L, f, 2:3], None, ALU.mult))
                            link(nc.vector.scalar_tensor_tensor(out=y[:, 1:SEQ], in0=u[:, 0:SEQ - 1], scalar=cw[:, L, f, 1:2],
                                                                in1=y[:, 1:SEQ], op0=ALU.mult, op1=ALU.add))
                            link(nc.vector.scalar_tensor_tensor(out=y[:, 2:SEQ], in0=u[:, 0:SEQ - 2], scalar=cw[:, L, f, 0:1],
                                                                in1=y[:, 2:SEQ], op0=ALU.mult, op1=ALU.add))
                        nc.vector.tensor_tensor(cy, cy, ps[:, 3, :].rearrange("p (f t) -> p f t", f=2),
                                                ALU.mult).then_inc(conv_out, 1)
                    if step >= 3 and step % 2 == 1:
                        pair = (step - 3) // 2
                        dve.wait_ge(att_hi, 4 * L + pair + 1)
                        nc.vector.tensor_tensor(mixT_lo[:, pair, :], ps[:, pair % 2, pair // 2 * SEQ:(pair // 2 + 1) * SEQ],
                                                mixT_hi[:, pair, :].bitcast(F32), ALU.subtract).then_inc(att_lo, 1)
                split(14)
                dve.wait_ge(conv_hi, L + 1)
                nc.vector.tensor_tensor(mixT_lo[:, 4:6, :], cy, mixT_hi[:, 4:6, :].bitcast(F32), ALU.subtract).then_inc(conv_lo, 1)
                dve.wait_ge(dec_exp, L + 1)
                dve.wait_ge(f_cp, 3 * L + 1)
                dve.wait_ge(conv_lo, L + 1)
                nc.vector.tensor_tensor(qe[:, :, :], dec[:, :, :], g_qk[:, 0, :].unsqueeze(1).to_broadcast([P, 8, SEQ]),
                                        ALU.mult).then_inc(qe_done, 1)
                dve.wait_ge(og_exp, L + 1)
                go = gvo[:, :, SEQ:2 * SEQ]
                link(nc.vector.tensor_scalar(cc[:, :, :], cc[:, :, :], 1.0, None, ALU.add))
                link(nc.vector.reciprocal(cc[:, :, :], cc[:, :, :]))
                link(nc.vector.tensor_tensor(go, go, cc[:, :, :], ALU.mult))
                for n in range(9):
                    dve.wait_ge(lv_ps, 9 * L + n + 1)
                    if n:
                        dve.wait_ge(lv_cp, 9 * L + n)
                    b0 = 4 - n % 2 * 4
                    src = ps[:, b0:b0 + 4, 0:SEQ].rearrange("p h (t q) -> p h t q", t=TT)
                    if n == 8:
                        nc.vector.tensor_copy(gax[:, :, :], src[:, :, 0, :]).then_inc(lv_cp, 1)
                        continue
                    for t in range(TT):
                        if n == 0:
                            m = msk[:, 7, :].unsqueeze(1).to_broadcast([P, GH, P])
                            ins = nc.vector.tensor_tensor(gat[:, :, t, :], src[:, :, t, :], m, ALU.mult)
                        else:
                            m = msk[:, n - 1, :].unsqueeze(1).to_broadcast([P, GH, P])
                            ins = nc.vector.copy_predicated(gat[:, :, t, :], m, src[:, :, t, :])
                        if t == 0:
                            continue
                        ins.then_inc(lv_cp, 1)
                dve.wait_ge(o_sq, L + 1)
                link(nc.vector.tensor_reduce(gss[:, :], osq.rearrange("p (g d) -> p g d", d=GV), AX_X, ALU.add))
                rsqrt_mean(gss[:, :], 8, GV, RS_GLA[L])
                og = cc[:, :, :].rearrange("p t (g d) -> p (t g) d", d=GV)
                link(nc.vector.tensor_tensor(og, ps[:, 0, :].rearrange("p (g d) -> p g d", d=GV),
                                             rs[:, :].unsqueeze(2).to_broadcast([P, 8, GV]), ALU.mult))
                nc.vector.tensor_tensor(cc[:, :, :], cc[:, :, :], go, ALU.mult).then_inc(o_done, 1)
                for f in range(2):
                    dve.wait_ge(oT_hi, 2 * L + f + 1)
                    nc.vector.scalar_tensor_tensor(out=mixT_lo[:, 6 + f, :], in0=ps[:, 1 + f, 0:SEQ],
                                                   scalar=gg[:, L, f:f + 1], in1=mixT_hi[:, 6 + f, :].bitcast(F32),
                                                   op0=ALU.mult, op1=ALU.subtract).then_inc(oT_lo, 1)
                split(15)

            def ffn_block(S, tiles, B, par, n, d=0):
                for t in range(tiles):
                    s = t if tiles == 2 else par
                    dve.wait_ge(S.silu, B * tiles + (t + 1))
                    nc.vector.tensor_tensor(act_x[:, s, :], gate_x[:, s, :], ps[:, 4 + s, FB:2 * FB], ALU.mult).then_inc(S.mul, 1)

            def ffn_aT(S, tiles, B, par):
                dve.wait_ge(S.aT_hi, B + 1)
                if tiles == 2:
                    dst, hi = aT_lo[:, :, :, :], aT_hi[:, :, :, :]
                    src = ps[:, 6 + par, :].rearrange("p (t f q) -> p t f q", t=2, f=2)
                else:
                    dst, hi = aT_lo[:, par, :, :], aT_hi[:, par, :, :]
                    src = ps[:, 6 + par, 0:FB].rearrange("p (f q) -> p f q", f=2)
                nc.vector.tensor_tensor(dst, src, hi.bitcast(F32), ALU.subtract).then_inc(S.aT_lo, 1)

            def dispatch(e, over):
                for t in range(TT):
                    s = slot[:, t, e:e + 1] if isinstance(e, int) else slot[:, t, bass.ds(e, 1)]
                    ins = nc.vector.tensor_scalar(disp[:, t, :], iota, 128.0 if over else 0.0, s, ALU.add, ALU.is_equal)
                ins.then_inc(disp_done, 1)

            def gather_lo(e):
                for g in (0, 1):
                    dve.wait_ge(ga_ps, e * 4 + (g + 3))
                    nc.vector.tensor_copy(xT_lo[:, 4 * g:4 * g + 4, 0:P],
                                          ps[:, 2 + g, :].rearrange("p (k s) -> p k s", k=4)).then_inc(ga_lo, 1)

            def slots(e):
                dve.wait_ge(slot_ps, e + 1)
                dst = slotT[:, e, :] if isinstance(e, int) else slotT[:, bass.ds(e, 1), :].rearrange("p a t -> p (a t)")
                nc.vector.tensor_copy(dst, ps[:, 6, SEQ:2 * SEQ]).then_inc(slot_cp, 2)
                dve.wait_ge(y_free, e + 1)
                nc.vector.tensor_copy(w_slot[:, :], ps[:, 7, SEQ:SEQ + 1]).then_inc(slot_cp, 1)

            def expert_start(e, n, d):
                gather_lo(e)
                lo_unit(dve, n, d)
                lo_unit(dve, n + 1, d)
                lo_unit(dve, n + 2, d)
                slots(e)
                ffn_block(fm, 1, e * EXP_BLOCKS, 0, n + 2, d)
                lo_unit(dve, n + 3, d)

            def expert_middle(e, n, d):
                with dve.Fori(0, (EXP_BLOCKS - 2) // 2) as i:
                    for p in range(2):
                        B = e * EXP_BLOCKS + i * 2 + p
                        m = n + 4 + 3 * p
                        lo_unit(dve, m, d + i)
                        ffn_aT(fm, 1, B, p)
                        lo_unit(dve, m + 1, d + i)
                        ffn_block(fm, 1, B + 1, 1 - p, m, d + i)
                        lo_unit(dve, m + 2, d + i)

            def expert_end(e, n, d, follow):
                B = e * EXP_BLOCKS + (EXP_BLOCKS - 2)
                if follow:
                    dve.wait_ge(slot_ps, e + 1)
                    dispatch(e + 1, False)
                lo_unit(dve, n + EXP_UNITS - 2, d)
                ffn_aT(fm, 1, B, 0)
                lo_unit(dve, n + EXP_UNITS - 1, d)
                ffn_block(fm, 1, B + 1, 1, n + EXP_UNITS - 2, d)
                if follow:
                    gather_lo(e + 1)
                    lo_unit(dve, n, d + EXP_UNITS // RAW)
                ffn_aT(fm, 1, B + 1, 1)
                if follow:
                    lo_unit(dve, n + 1, d + EXP_UNITS // RAW)

            for n in range(2):
                lo_unit(dve, n)
            dve.wait_ge(in_cst, 16)
            dve.wait_ge(in_small, 48)
            dve.wait_ge(pool_chain, 2)
            mixer(0)
            n0 = BASE_DENSE
            lo_unit(dve, n0)
            residual(BASE_DENSE)
            lo_unit(dve, n0 + 1)
            norm(1)
            lo_unit(dve, n0 + 2)
            ffn_block(fd, 2, 0, 0, n0 + 2)
            lo_unit(dve, n0 + 3)
            with dve.Fori(0, (DENSE_BLOCKS - 1) // 2) as i:
                for p in range(2):
                    B = i * 2 + p
                    m = n0 + 4 + 3 * p
                    lo_unit(dve, m, i)
                    ffn_aT(fd, 2, B, p)
                    lo_unit(dve, m + 1, i)
                    ffn_block(fd, 2, B + 1, 0, m, i)
                    lo_unit(dve, m + 2, i)
            ffn_aT(fd, 2, DENSE_BLOCKS - 1, 0)
            lo_unit(dve, BASE_MIX[1] + 1)
            residual(BASE_MIX[1])
            mixer(1)
            residual(BASE_MOE)
            dve.wait_ge(rt_h, 1)
            nc.vector.tensor_tensor(rt_lo[:, :, :], rt[:, :, :], rt_hi[:, :, :].bitcast(F32), ALU.subtract).then_inc(rt_l, 1)
            norm(3)
            dve.wait_ge(tok_h, 1)
            nc.vector.tensor_tensor(tok_lo[:, :, :], hn[:, :, :], tok_hi[:, :, :].bitcast(F32), ALU.subtract).then_inc(tok_l, 1)
            dve.wait_ge(lg_ps, 1)
            link(nc.vector.tensor_copy(lg[:, :, :], ps[:, 6, 0:16].rearrange("p (t e) -> p t e", t=TT)))
            for t in range(TT):
                link(nc.vector.max(mx8[:, t, :], lg[:, t, :]))
            for t in range(TT):
                ins = nc.vector.max_index(ix8[:, t, :], mx8[:, t, :], lg[:, t, :])
            link(ins)
            nc.vector.tensor_tensor(tw[:, :, 0:1], mx8[:, :, 1:2], mx8[:, :, 0:1], ALU.subtract).then_inc(lg_exp_in, 1)
            link(nc.vector.tensor_copy(ixf[:, :, :], ix8[:, :, 0:2]))
            for n, top in enumerate((top1, top2)):
                for t in range(TT):
                    ins = nc.vector.tensor_scalar(top[:, t, :], iota8, ixf[:, t, n:n + 1], None, ALU.is_equal)
            link(ins)
            nc.vector.tensor_tensor(chosen[:, :, :], top1[:, :, :], top2[:, :, :], ALU.add).then_inc(chosen_done, 1)
            dve.wait_ge(lg_exp, 1)
            link(nc.vector.tensor_scalar(tw[:, :, 2:3], tw[:, :, 1:2], 1.0, None, ALU.add))
            link(nc.vector.reciprocal(tw[:, :, 2:3], tw[:, :, 2:3]))
            link(nc.vector.tensor_tensor(tw[:, :, 3:4], tw[:, :, 1:2], tw[:, :, 2:3], ALU.mult))
            for t in range(TT):
                ins = nc.vector.tensor_scalar(comb[:, t, :], top1[:, t, :], tw[:, t, 2:3], None, ALU.mult)
            link(ins)
            for t in range(TT):
                ins = nc.vector.scalar_tensor_tensor(out=comb[:, t, :], in0=top2[:, t, :], scalar=tw[:, t, 3:4],
                                                     in1=comb[:, t, :], op0=ALU.mult, op1=ALU.add)
            link(ins)
            dve.wait_ge(chosen_done, 1)
            dve.wait_ge(pos_ps, 1)
            link(nc.vector.scalar_tensor_tensor(out=slot[:, :, :], in0=ps[:, 7, 0:16].rearrange("p (t e) -> p t e", t=TT),
                                                scalar=1.0, in1=chosen[:, :, :], op0=ALU.add, op1=ALU.mult))
            link(nc.vector.tensor_scalar(slot[:, :, :], slot[:, :, :], -1.0, None, ALU.add))
            link(nc.vector.tensor_scalar(flag[:, :], ps[:, 7, 16:24], float(P), None, ALU.is_gt))
            dispatch(0, False)
            link(nc.vector.tensor_tensor_scan(cum[:, :], flag[:, :], zero8[:, :], 0.0, ALU.add, ALU.add))
            link(nc.vector.tensor_copy(over_f[:, 0:1], cum[:, 7:8]))
            for k in range(3):
                link(nc.vector.scalar_tensor_tensor(out=sel[:, :], in0=cum[:, :], scalar=float(k + 1), in1=flag[:, :],
                                                    op0=ALU.is_equal, op1=ALU.mult))
                link(nc.vector.tensor_tensor_reduce(out=sel[:, :], in0=sel[:, :], in1=iota8, scale=1.0, scalar=0.0,
                                                    op0=ALU.mult, op1=ALU.add, accum_out=over_f[:, k + 1:k + 2]))
            nc.vector.tensor_copy(over_i[:, :], over_f[:, :]).then_inc(route_done, 1)
            expert_start(0, BASE_MOE, 0)
            with dve.Fori(0, N_EXP - 1) as e:
                d = e * (EXP_UNITS // RAW)
                expert_middle(e, BASE_MOE, d)
                expert_end(e, BASE_MOE, d, True)
                lo_unit(dve, BASE_MOE + 2, d + EXP_UNITS // RAW)
                slots(e + 1)
                ffn_block(fm, 1, (e + 1) * EXP_BLOCKS, 0, BASE_MOE + 2, d + EXP_UNITS // RAW)
                lo_unit(dve, BASE_MOE + 3, d + EXP_UNITS // RAW)
            last = N_EXP - 1
            expert_middle(last, BASE_MOE, last * (EXP_UNITS // RAW))
            expert_end(last, BASE_MOE, last * (EXP_UNITS // RAW), False)
            for t in range(TT):
                for half in range(2):
                    dve.wait_ge(sc_ps, 2 * t + half + 1)
                    ins = nc.vector.tensor_tensor(h[:, t, half * 512:(half + 1) * 512], h[:, t, half * 512:(half + 1) * 512],
                                                  ps[:, 2 + 2 * t + half, :], ALU.add)
            ins.then_inc(sc_add, 1)
            dve.wait_ge(sc_add, 1)
            dve.wait_ge(route_done, 1)
            n_over = dve.value_load(over_i[0:1, 0:1], min_val=0, max_val=3)
            with dve.If(n_over > 0):
                with dve.Fori(0, n_over) as k:
                    e = k + N_EXP
                    ex = dve.value_load(over_i[0:1, bass.ds(k + 1, 1)], min_val=0, max_val=N_EXP - 1)
                    d = k * (EXP_UNITS // RAW) + N_EXP * (EXP_UNITS // RAW)
                    dve.wait_ge(slot_ps, e)
                    dispatch(ex, True)
                    gather_lo(e)
                    for j in range(3):
                        lo_unit(dve, BASE_MOE + j, d)
                    dve.wait_ge(slot_ps, e + 1)
                    dve.wait_ge(y_free, e + 1)
                    nc.vector.tensor_copy(slotT[:, 0, :], ps[:, 6, SEQ:2 * SEQ]).then_inc(slot_cp, 2)
                    nc.vector.tensor_copy(w_slot[:, :], ps[:, 7, SEQ:SEQ + 1]).then_inc(slot_cp, 1)
                    ffn_block(fm, 1, e * EXP_BLOCKS, 0, BASE_MOE + 2, d)
                    lo_unit(dve, BASE_MOE + 3, d)
                    expert_middle(e, BASE_MOE, d)
                    expert_end(e, BASE_MOE, d, False)
                    dve.wait_ge(ov_ps, k + 1)
                    for t in range(TT):
                        for half in range(2):
                            ins = nc.vector.tensor_tensor(h[:, t, half * 512:(half + 1) * 512],
                                                          h[:, t, half * 512:(half + 1) * 512],
                                                          ps[:, 2 + 2 * t + half, :], ALU.add)
                    ins.then_inc(sc_add, 1)
                    dve.wait_ge(sc_add, k + 2)
            dve.sem_inc(res_done, 1)
            norm(4)

        @block.tensor
        def _(pe):
            def unit_ready(n, d=0):
                pe.wait_ge(lo_done, d * RAW + (n + 1))

            def norm(i):
                pe.wait_ge(hn_done, 2 * (i + 1))
                for half in range(2):
                    for t in range(TT):
                        for kk in range(4):
                            k = 4 * half + kk
                            last = nc.tensor.transpose(ps[:, k // 2, k % 2 * SEQ + t * P:k % 2 * SEQ + (t + 1) * P],
                                                       hn[:, t, k * P:(k + 1) * P], ident)
                    last.then_inc(hnT_ps, 1)

            def tokens_first(n, half, bank):
                unit_ready(n)
                for t in range(TT):
                    for kk in range(4):
                        k = 4 * half + kk
                        for xp, wp in PASSES:
                            last = nc.tensor.matmul(ps[:, bank + t, :], (xT_hi, xT_lo)[xp][:, k, t * P:(t + 1) * P],
                                                    w(n, wp, kk * 512, (kk + 1) * 512),
                                                    start=(k == 0 and xp == wp), stop=(k == KT - 1 and wp == 1))
                last.then_inc(unit_used, 1)

            def features_first(n, half, bank):
                unit_ready(n)
                for kk in range(4):
                    k = 4 * half + kk
                    for f in range(4):
                        for xp, wp in PASSES:
                            last = nc.tensor.matmul(ps[:, bank + f // 2, f % 2 * SEQ:(f % 2 + 1) * SEQ],
                                                    w(n, wp, kk * 512 + f * P, kk * 512 + (f + 1) * P),
                                                    (xT_hi, xT_lo)[xp][:, k, :],
                                                    start=(k == 0 and f % 2 == 0 and xp == wp),
                                                    stop=(k == KT - 1 and wp == 1), skip_group_check=True)
                last.then_inc(unit_used, 1)

            def w_in_block(fn, n, bank):
                fn(n, 0, bank)
                fn(n + 1, 1, bank)

            def scores(L, hd):
                b, r, a = hd % 2, hd % 2 * HD, hd // 2
                if hd >= 2:
                    pe.wait_ge(s_max, HEADS * L + hd - 1)
                for t in range(TT):
                    last = nc.tensor.matmul(ps[:, 4 + b, P * t:P * t + (t + 1) * P], qT[r:r + HD, a, t * P:(t + 1) * P],
                                            kT[r:r + HD, a, 0:(t + 1) * P], start=True, stop=True)
                last.then_inc(s_ps, 1)

            def probs_T(L, hd):
                b = hd % 2
                pe.wait_ge(s_norm, HEADS * L + hd + 1)
                if hd >= 2:
                    pe.wait_ge(pT_cp, HEADS * L + hd - 1)
                for c in range(3):
                    last = nc.tensor.transpose(ps[:, 6 + b, c * P:(c + 1) * P], probs[:, b, c * P:(c + 1) * P], ident)
                last.then_inc(pT_ps, 1)

            def weigh(L, hd):
                b, r, a = hd % 2, hd % 2 * HD, hd // 2
                pe.wait_ge(pT_cp, HEADS * L + hd + 1)
                if a >= 2:
                    pe.wait_ge(att_lo, 4 * L + a - 1)
                o = ps[r:r + HD, a % 2, a // 2 * SEQ:(a // 2 + 1) * SEQ]
                nc.tensor.matmul(o, v_sb[:, 0, hd * HD:(hd + 1) * HD], probsT[:, b, 0:SEQ], start=True, stop=True)
                nc.tensor.matmul(o[:, P:SEQ], v_sb[:, 1, hd * HD:(hd + 1) * HD], probsT[:, b, SEQ:3 * P], start=False,
                                 stop=True, skip_group_check=True).then_inc(att_ps, 1)

            def w_out(n, j):
                unit_ready(n)
                for kk in range(2):
                    k = 2 * j + kk
                    for t in range(TT):
                        for half in range(2):
                            for xp, wp in PASSES:
                                last = nc.tensor.matmul(ps[:, 2 * t + half, :], (mixT_hi, mixT_lo)[xp][:, k, t * P:(t + 1) * P],
                                                        w(n, wp, kk * D + half * 512, kk * D + (half + 1) * 512),
                                                        start=(k == 0 and xp == wp), stop=(k == KT - 1 and wp == 1))
                last.then_inc(unit_used, 1)

            def mixer(L):
                n0 = BASE_MIX[L]
                norm(2 * L)
                pe.wait_ge(hnT_lo, 4 * L + 2)
                pe.wait_ge(wz_l, L + 1)
                for t in range(TT):
                    for k in range(KT):
                        for xp, wp in PASSES:
                            last = nc.tensor.matmul(ps[:, 6, t * RANK:(t + 1) * RANK],
                                                    (xT_hi, xT_lo)[xp][:, k, t * P:(t + 1) * P], (wz_hi, wz_lo)[wp][:, k, :],
                                                    start=(k == 0 and xp == wp), stop=(k == KT - 1 and wp == 1))
                last.then_inc(z_ps, 1)
                w_in_block(tokens_first, n0, 0)
                pe.wait_ge(z_cp, L + 1)
                for t in range(TT):
                    last = nc.tensor.transpose(ps[0:RANK, 7, t * P:(t + 1) * P], z_sb[:, t, :], ident)
                last.then_inc(zT_ps, 1)
                w_in_block(tokens_first, n0 + 2, 2)
                pe.wait_ge(zT_cp, L + 1)
                for t in range(TT):
                    last = nc.tensor.matmul(ps[:, 6, SEQ + t * P:SEQ + (t + 1) * P], zT[:, t * P:(t + 1) * P], wg[:, :],
                                            start=True, stop=True)
                last.then_inc(zl_ps, 1)
                pe.wait_ge(rope_mul, 2 * L + 1)
                w_in_block(tokens_first, n0 + 4, 0)
                pe.wait_ge(loga_done, L + 1)
                nc.tensor.matmul(ps[:, 7, SEQ:2 * SEQ], log_a[:, 0, :], tri_ones, start=True, stop=True)
                nc.tensor.matmul(ps[:, 7, SEQ + P:2 * SEQ], log_a[:, 1, :], tri, start=False, stop=True,
                                 skip_group_check=True).then_inc(b_ps, 1)
                pe.wait_ge(rope_mul, 2 * L + 2)
                w_in_block(features_first, n0 + 6, 2)
                for n, (rot, bank, done) in enumerate(((rot_q, 4, qT_ps), (rot_k, 6, kT_ps))):
                    pe.wait_ge(rope_add, 2 * L + n + 1)
                    if n:
                        pe.wait_ge(b_cp, L + 1)
                    for a in range(4):
                        for t in range(TT):
                            last = nc.tensor.transpose(ps[:, bank + a // 2, a % 2 * SEQ + t * P:a % 2 * SEQ + (t + 1) * P],
                                                       rot[:, t, a * P:(a + 1) * P], ident)
                    last.then_inc(done, 1)
                pe.wait_ge(v_cp, L + 1)
                w_in_block(tokens_first, n0 + 8, 0)
                pe.wait_ge(qT_cp, L + 1)
                pe.wait_ge(kT_cp, L + 1)
                for step in range(HEADS + 2):
                    if step < HEADS:
                        scores(L, step)
                    if step == 1:
                        pe.wait_ge(f_cp, 3 * (L + 1))
                        features_first(n0 + 10, 0, 2)
                    if step == 3:
                        features_first(n0 + 11, 1, 2)
                    if 1 <= step <= HEADS:
                        probs_T(L, step - 1)
                    if step >= 2:
                        if step == 2:
                            pe.wait_ge(t_cp, L + 1)
                        weigh(L, step - 2)
                for n in range(9):
                    if n == 0:
                        pe.wait_ge(pT_cp, HEADS * (L + 1))
                        pe.wait_ge(f_cp, 3 * L + 2)
                    if n == 1:
                        pe.wait_ge(att_lo, 4 * (L + 1))
                        pe.wait_ge(conv_out, L + 1)
                        pe.wait_ge(qe_done, L + 1)
                        pe.wait_ge(ke_done, L + 1)
                    if n >= 2:
                        pe.wait_ge(lv_cp, 9 * L + n - 1)
                    for hh in range(GH):
                        r = slice(GK * hh, GK * (hh + 1))
                        for t in range(1 if n == 8 else TT):
                            if n == 0:
                                lhsT, rhs = g_qk[r, 1, t * P:(t + 1) * P], g_qk[r, 0, t * P:(t + 1) * P]
                            elif n == 8:
                                lhsT, rhs = ke[r, 0, 0:P], qe[r, 0, P:2 * P]
                            else:
                                lhsT, rhs = ke[r, n, t * P:(t + 1) * P], qe[r, n, t * P:(t + 1) * P]
                            last = nc.tensor.matmul(ps[:, 4 - n % 2 * 4 + hh, t * P:(t + 1) * P], lhsT, rhs, start=True, stop=True,
                                                    tile_position=(GK * hh, 0))
                    last.then_inc(lv_ps, 1)
                pe.wait_ge(lv_cp, 9 * (L + 1))
                for t in range(TT):
                    for hh in range(GH):
                        o = ps[:, 0, t * SEQ + hh * GV:t * SEQ + (hh + 1) * GV]
                        last = nc.tensor.matmul(o, gat[:, hh, t, :], gvo[:, t, hh * GV:(hh + 1) * GV], start=True, stop=(t == 0))
                        if t == 1:
                            last = nc.tensor.matmul(o, gax[:, hh, :], gvo[:, 0, hh * GV:(hh + 1) * GV], start=False, stop=True)
                last.then_inc(o_ps, 1)
                pe.wait_ge(o_done, L + 1)
                for f in range(2):
                    for t in range(TT):
                        last = nc.tensor.transpose(ps[:, 1 + f, t * P:(t + 1) * P], cc[:, t, f * P:(f + 1) * P], ident)
                last.then_inc(oT_ps, 1)
                pe.wait_ge(oT_lo, 2 * (L + 1))
                pe.wait_ge(conv_lo, L + 1)
                for j in range(4):
                    w_out(n0 + 12 + j, j)

            def gate_up(S, tiles, B, par, n, d, wait_mul=True):
                for half in range(2):
                    unit_ready(n + half, d)
                    for t in range(tiles):
                        s = t if tiles == 2 else par
                        if half == 0 and wait_mul:
                            pe.wait_ge(S.mul, (B - 1) * 2 + (t + 1) if tiles == 2 else B - 1)
                        for kk in range(4):
                            k = 4 * half + kk
                            for xp, wp in PASSES:
                                last = nc.tensor.matmul(ps[:, 4 + s, :], (xT_hi, xT_lo)[xp][:, k, t * P:(t + 1) * P],
                                                        w((n + half), wp, kk * 512, (kk + 1) * 512),
                                                        start=(k == 0 and xp == wp), stop=(k == KT - 1 and wp == 1))
                        if half == 1 and t < tiles - 1:
                            last.then_inc(S.gu_first, 1)
                    last.then_inc(unit_used, 1)
                    if half == 0:
                        yield

            def act_T(S, tiles, B, par):
                pe.wait_ge(S.mul, (B + 1) * tiles)
                for t in range(tiles):
                    s = t if tiles == 2 else par
                    for f in range(2):
                        c = t * FB + f * P
                        last = nc.tensor.transpose(ps[:, 6 + par, c:c + P], act_x[:, s, f * P:(f + 1) * P], ident)
                last.then_inc(S.aT_ps, 1)

            def down(S, tiles, B, par, n, d, first, final):
                unit_ready(n, d)
                pe.wait_ge(S.aT_lo, B + 1)
                for f in range(2):
                    for t in range(tiles):
                        s = t if tiles == 2 else par
                        for half in range(2):
                            for xp, wp in PASSES:
                                last = nc.tensor.matmul(ps[:, 2 * t + half, :], (aT_hi, aT_lo)[xp][:, s, f, :],
                                                        w(n, wp, f * D + half * 512, f * D + (half + 1) * 512),
                                                        start=(first and f == 0 and xp == wp),
                                                        stop=(final and f == 1 and wp == 1), skip_group_check=True)
                last.then_inc(unit_used, 1)

            def step(S, tiles, B, p, n, d, first, final=False, wait_mul=True):
                gu = gate_up(S, tiles, B + 1, 1 - p, n, d, wait_mul)
                next(gu)
                act_T(S, tiles, B, p)
                for _ in gu:
                    pass
                down(S, tiles, B, p, n + 2, d, first, final)

            def gather(e):
                pe.wait_ge(disp_done, e + 1)
                for g in range(4):
                    if g >= 2:
                        pe.wait_ge(ga_hi, e * 2 + (g - 1))
                    src = tok_hi if g < 2 else tok_lo
                    for kk in range(4):
                        k = g % 2 * 4 + kk
                        for t in range(TT):
                            last = nc.tensor.matmul(ps[:, 2 + g % 2, kk * P:(kk + 1) * P], src[:, t, k * P:(k + 1) * P],
                                                    disp[:, t, :], start=(t == 0), stop=(t == TT - 1))
                    last.then_inc(ga_ps, 1)

            def slot_tables(e, col):
                for t in range(TT):
                    nc.tensor.transpose(ps[:, 6, SEQ + t * P:SEQ + (t + 1) * P], disp[:, t, :].bitcast(F32), ident)
                for t in range(TT):
                    c = comb[:, t, col:col + 1] if isinstance(col, int) else comb[:, t, bass.ds(col, 1)]
                    last = nc.tensor.matmul(ps[:, 7, SEQ:SEQ + 1], disp[:, t, :].bitcast(F32), c, start=(t == 0),
                                            stop=(t == TT - 1))
                last.then_inc(slot_ps, 1)

            def expert_start(e, col, n, d):
                gather(e)
                slot_tables(e, col)
                pe.wait_ge(ga_lo, e * 2 + 2)
                for _ in gate_up(fm, 1, e * EXP_BLOCKS, 0, n, d, wait_mul=False):
                    pass

            def expert_steps(e, n, d, y_wait):
                if y_wait:
                    pe.wait_ge(y_free, e + 1)
                pe.wait_ge(slot_cp, 3 * e + 3)
                B0 = e * EXP_BLOCKS
                step(fm, 1, B0, 0, n + 2, d, True, wait_mul=False)
                step(fm, 1, B0 + 1, 1, n + 5, d, False)
                with pe.Fori(1, (EXP_BLOCKS - 2) // 2) as i:
                    for p in range(2):
                        step(fm, 1, B0 + i * 2 + p, p, n + 2 + 3 * p, d + i, False)
                step(fm, 1, B0 + (EXP_BLOCKS - 2), 0, n + EXP_UNITS - 4, d, False)

            def expert_last(e, n, d):
                B = e * EXP_BLOCKS + (EXP_BLOCKS - 1)
                act_T(fm, 1, B, 1)
                down(fm, 1, B, 1, n + EXP_UNITS - 1, d, False, True)

            pe.wait_ge(in_cst, 16)
            mixer(0)
            n0 = BASE_DENSE
            norm(1)
            pe.wait_ge(hnT_lo, 4)
            for _ in gate_up(fd, 2, 0, 0, n0, 0, wait_mul=False):
                pass
            step(fd, 2, 0, 0, n0 + 2, 0, True)
            step(fd, 2, 1, 1, n0 + 5, 0, False)
            with pe.Fori(1, (DENSE_BLOCKS - 1) // 2) as i:
                for p in range(2):
                    step(fd, 2, i * 2 + p, p, n0 + 2 + 3 * p, i, False)
            act_T(fd, 2, DENSE_BLOCKS - 1, 0)
            down(fd, 2, DENSE_BLOCKS - 1, 0, n0 + DENSE_UNITS - 1, 0, False, True)
            mixer(1)
            norm(3)
            pe.wait_ge(hnT_lo, 8)
            pe.wait_ge(rt_l, 1)
            for t in range(TT):
                for k in range(KT):
                    for xp, wp in PASSES:
                        last = nc.tensor.matmul(ps[:, 6, t * 8:(t + 1) * 8], (xT_hi, xT_lo)[xp][:, k, t * P:(t + 1) * P],
                                                (rt_hi, rt_lo)[wp][:, k, :], start=(k == 0 and xp == wp),
                                                stop=(k == KT - 1 and wp == 1))
            last.then_inc(lg_ps, 1)
            pe.wait_ge(chosen_done, 1)
            nc.tensor.matmul(ps[:, 7, 0:8], stri, chosen[:, 0, :], start=True, stop=True)
            nc.tensor.matmul(ps[:, 7, 8:16], ones, chosen[:, 0, :], start=True, stop=False)
            nc.tensor.matmul(ps[:, 7, 8:16], stri, chosen[:, 1, :], start=False, stop=True)
            nc.tensor.matmul(ps[:, 7, 16:24], ones, chosen[:, 0, :], start=True, stop=False)
            nc.tensor.matmul(ps[:, 7, 16:24], ones, chosen[:, 1, :], start=False, stop=True).then_inc(pos_ps, 1)
            pe.wait_ge(tok_l, 1)
            expert_start(0, 0, BASE_MOE, 0)
            with pe.Fori(0, N_EXP - 1) as e:
                d = e * (EXP_UNITS // RAW)
                expert_steps(e, BASE_MOE, d, True)
                gather(e + 1)
                expert_last(e, BASE_MOE, d)
                slot_tables(e + 1, e + 1)
                pe.wait_ge(ga_lo, e * 2 + 4)
                for _ in gate_up(fm, 1, (e + 1) * EXP_BLOCKS, 0, BASE_MOE, d + EXP_UNITS // RAW, wait_mul=False):
                    pass
            last_e = N_EXP - 1
            expert_steps(last_e, BASE_MOE, last_e * (EXP_UNITS // RAW), True)
            expert_last(last_e, BASE_MOE, last_e * (EXP_UNITS // RAW))
            pe.wait_ge(y_free, N_EXP + 1)
            pe.wait_ge(slot_cp, 3 * N_EXP)
            for t in range(TT):
                for half in range(2):
                    for e in range(N_EXP):
                        last = nc.tensor.matmul(ps[:, 2 + 2 * t + half, :], slotT[:, e, t * P:(t + 1) * P],
                                                ys[:, e, half * 512:(half + 1) * 512], start=(e == 0), stop=(e == N_EXP - 1))
                    last.then_inc(sc_ps, 1)
            pe.wait_ge(route_done, 1)
            n_over = pe.value_load(over_i[0:1, 0:1], min_val=0, max_val=3)
            with pe.If(n_over > 0):
                with pe.Fori(0, n_over) as k:
                    e = k + N_EXP
                    ex = pe.value_load(over_i[0:1, bass.ds(k + 1, 1)], min_val=0, max_val=N_EXP - 1)
                    d = k * (EXP_UNITS // RAW) + N_EXP * (EXP_UNITS // RAW)
                    pe.wait_ge(sc_add, k + 1)
                    expert_start(e, ex, BASE_MOE, d)
                    expert_steps(e, BASE_MOE, d, False)
                    expert_last(e, BASE_MOE, d)
                    pe.wait_ge(y_free, e + 2)
                    for t in range(TT):
                        for half in range(2):
                            last = nc.tensor.matmul(ps[:, 2 + 2 * t + half, :], slotT[:, 0, t * P:(t + 1) * P],
                                                    ys[:, 0, half * 512:(half + 1) * 512], start=True, stop=True)
                    last.then_inc(ov_ps, 1)


def lay_out(inp):
    a = {k: np.asarray(v) for k, v in inp.items()}

    def by_unit(m, width):
        rows = UNIT // width
        k = m.shape[0] // (P * rows)
        u = m.reshape(k, rows, P, m.shape[1] // width, width).transpose(3, 0, 2, 1, 4)
        return u.reshape(-1, P, UNIT)

    def ffn(g, u, d):
        nb = g.shape[1] // FB
        gu = np.stack([g.reshape(D, nb, FB), u.reshape(D, nb, FB)], 2).reshape(D, nb * 2 * FB)
        gu = by_unit(gu, 2 * FB).reshape(nb, 2, P, UNIT)
        dn = by_unit(d, D)
        out = [gu[0]]
        for b in range(1, nb):
            out += [gu[b], dn[b - 1:b]]
        return out + [dn[nb - 1:nb]]

    order = ((0, 1536), (2304, 2560), (1792, 2048), (2560, 3072), (2048, 2304), (1536, 1792))
    units = []
    for L in range(DEPTH):
        w_in = np.concatenate([a["w_in"][L][:, s:e] for s, e in order], 1)
        units += [by_unit(w_in, 512), by_unit(a["w_out"][L], D)]
        if L % 2 == 0:
            units += ffn(a["dense_w_gate"][L // 2], a["dense_w_up"][L // 2], a["dense_w_down"][L // 2])
        else:
            for e in range(N_EXP):
                units += ffn(a["exp_w_gate"][L // 2, e], a["exp_w_up"][L // 2, e], a["exp_w_down"][L // 2, e])
    consts, masks = shape_constants()
    z = a["w_in"][:, :, 3072:].reshape(DEPTH, KT, P, RANK).transpose(0, 2, 1, 3)
    gate = np.concatenate([a["w_gate_lr"], a["b_gate_lr"][:, None, :]], 1)
    conv = a["conv_w"].reshape(DEPTH, 3, 2, P).transpose(3, 0, 2, 1)
    gla_gain = a["gla_norm"].reshape(DEPTH, 2, P).transpose(2, 0, 1)
    gains = np.stack([a["mix_norm"][0], a["ffn_norm"][0], a["mix_norm"][1], a["ffn_norm"][1], a["final_norm"]])
    router = a["router"][0].reshape(KT, P, N_EXP).transpose(1, 0, 2)
    return {"x": a["x"], "stream": np.concatenate(units, 0), "w_z": z, "w_gate": gate, "conv_w": conv, "gla_gain": gla_gain,
            "gains": gains, "router": router, "consts": consts, "masks": masks}


def kernel(**inputs):
    import concourse.bacc as bacc
    from concourse.bass_utils import run_bass_kernel_spmd

    nc = bacc.Bacc("TRN2", target_bir_lowering=False, num_devices=1)
    arrays, args = {}, []
    for name, v in lay_out(inputs).items():
        v = np.ascontiguousarray(v)
        arrays[f"in_{name}"] = v
        args.append(nc.dram_tensor(f"in_{name}", v.shape, mybir.dt.from_np(v.dtype), kind="ExternalInput").ap())
    out = nc.dram_tensor("out_0", (1, SEQ, D), F32, kind="ExternalOutput").ap()
    build(nc, *args, out)
    r = run_bass_kernel_spmd(nc, [arrays], core_ids=[0])
    return r.results[0]["out_0"]
```

```python
from contextlib import ExitStack

import numpy as np

import concourse.bass as bass
from concourse import mybir

F32 = mybir.dt.float32
F32R = mybir.dt.float32r
I32 = mybir.dt.int32
U32 = mybir.dt.uint32
U8 = mybir.dt.uint8
ALU = mybir.AluOpType
ACT = mybir.ActivationFunctionType
AX_X = mybir.AxisListType.X

P = 128
D = 1024
SEQ = 256
TT = SEQ // P
KT = D // P
DEPTH = 2
EPS = 1e-6
NEG = -1e30
HEADS = 8
HD = 64
BRANCHES = ((128, 1), (512, 4), (2048, 16))
ROPE_THETA = 10000.0
GH = 4
GK = 32
GV = 64
TAU = 16.0
RANK = 16
F_DENSE = 2816
N_EXP = 8
F_EXP = 3584
FB = 256

UNIT = 2048
RAW = 6
SPLIT = 3
MIX_UNITS = 16
DENSE_BLOCKS = F_DENSE // FB
EXP_BLOCKS = F_EXP // FB
DENSE_UNITS = 3 * DENSE_BLOCKS
EXP_UNITS = 3 * EXP_BLOCKS
BASE_MIX = (0, MIX_UNITS + DENSE_UNITS)
BASE_DENSE = MIX_UNITS
BASE_MOE = 2 * MIX_UNITS + DENSE_UNITS
ALL_UNITS = BASE_MOE + N_EXP * EXP_UNITS
assert DENSE_BLOCKS % 2 == 1 and EXP_BLOCKS % 2 == 0 and EXP_UNITS % RAW == 0

RSQRT_BITS = float(0x5F3759DF)
LEVELS = (128, 64, 32, 16, 8, 4, 2, 1)

C_ID, C_TRI, C_ONES, C_STRI, C_IOTA = 0, 128, 256, 384, 512
C_LNC = 640
C_ROPE = C_LNC + 3 * P
C_E8 = C_ROPE + 2 * TT * HD
C_ALL = C_E8 + 8


def shape_constants():
    c = np.zeros((P, C_ALL), np.float32)
    i = np.arange(P)
    c[:, C_ID:C_ID + P] = np.eye(P)
    c[:, C_TRI:C_TRI + P] = i[:, None] <= i[None, :]
    c[:, C_ONES:C_ONES + P] = 1.0
    c[:, C_STRI:C_STRI + P] = i[:, None] < i[None, :]
    c[:, C_IOTA:C_IOTA + P] = i[None, :]
    t = np.arange(SEQ)
    diff = t[:, None] - t[None, :]
    count = np.zeros((SEQ, SEQ))
    for window, step in BRANCHES:
        count += (diff >= 0) & (diff % step == 0) & (diff // step <= window // step)
    lnc = np.where(count > 0, np.log(np.maximum(count, 1)), NEG)
    c[:, C_LNC:C_LNC + P] = lnc[:P, :P]
    c[:, C_LNC + P:C_LNC + 3 * P] = lnc[P:]
    inv = (1.0 / (np.float32(ROPE_THETA) ** (np.arange(0, HD, 2, dtype=np.float32) / np.float32(HD)))).astype(np.float32)
    ang = (t.astype(np.float32)[:, None] * inv[None, :]).astype(np.float32).astype(np.float64)
    cos = np.concatenate([np.cos(ang), np.cos(ang)], 1)
    sin = np.concatenate([-np.sin(ang), np.sin(ang)], 1)
    rope = np.stack([cos, sin])
    c[:, C_ROPE:C_E8] = rope.reshape(2, TT, P, HD).transpose(2, 0, 1, 3).reshape(P, -1)
    c[:, C_E8:C_E8 + 8] = np.arange(8)
    m = np.zeros((P, len(LEVELS), P), np.float32)
    for n, half in enumerate(LEVELS[1:]):
        same = i[:, None] // (2 * half) == i[None, :] // (2 * half)
        m[:, n] = same & (i[:, None] % (2 * half) < half) & (i[None, :] % (2 * half) >= half)
    m[:, -1] = np.eye(P)
    return c, m


def build(nc, x, stream, w_z, w_gate, conv_w, gla_gain, gains, router, consts, masks, out):
    with ExitStack() as ctx:
        def sb(name, shape, dt=F32):
            return ctx.enter_context(nc.sbuf_tensor(name, shape, dt))

        def sem(name):
            return ctx.enter_context(nc.semaphore(name))

        ps = ctx.enter_context(nc.psum_tensor("ps", [P, 8, 512], F32))

        raw = sb("raw", [P, RAW, UNIT])
        w_hi = sb("w_hi", [P, SPLIT, UNIT], F32R)
        w_lo = sb("w_lo", [P, SPLIT, UNIT], F32R)
        h = sb("h", [P, TT, D])
        xT_hi = sb("xT_hi", [P, KT, SEQ], F32R)
        xT_lo = sb("xT_lo", [P, KT, SEQ], F32R)
        mix_hi = sb("mix_hi", [P, KT * SEQ], F32R)
        mix_lo = sb("mix_lo", [P, KT * SEQ], F32R)
        mixT_hi = mix_hi[:, :].rearrange("p (k t) -> p k t", k=KT)
        mixT_lo = mix_lo[:, :].rearrange("p (k t) -> p k t", k=KT)
        tok_hi = mix_hi[:, :].rearrange("p (t d) -> p t d", t=TT)
        tok_lo = mix_lo[:, :].rearrange("p (t d) -> p t d", t=TT)
        big = sb("big", [P, 8 * D])
        work = sb("work", [P, 2 * D])
        small = sb("small", [P, 2 * D])
        cst = sb("cst", [P, C_ALL])
        msk = sb("msk", [P, len(LEVELS), P], U8)
        gain = sb("gain", [P, D])
        gate_x = sb("gate_x", [P, 2, FB])
        act_x = sb("act_x", [P, 2, FB])
        aT_hi = sb("aT_hi", [P, 2, 2, P], F32R)
        aT_lo = sb("aT_lo", [P, 2, 2, P], F32R)
        wz = sb("wz", [P, KT, RANK])
        wz_hi = sb("wz_hi", [P, KT, RANK], F32R)
        wz_lo = sb("wz_lo", [P, KT, RANK], F32R)
        wg = sb("wg", [RANK + 1, P])
        zT = sb("zT", [RANK + 1, SEQ])
        cw = sb("cw", [P, DEPTH, 2, 3])
        gg = sb("gg", [P, DEPTH, 2])
        ss = sb("ss", [P, TT])
        rs = sb("rs", [P, 8])
        nwt = sb("nwt", [P, 8])
        mx = sb("mx", [P, 2, 2])
        nmx = sb("nmx", [P, 2, 2])
        den = sb("den", [P, 2, 2])
        rden = sb("rden", [P, 2, 2])
        gss = sb("gss", [P, 8])
        ix8 = sb("ix8", [P, TT, 8], U32)
        zero8 = sb("zero8", [P, 8])
        over_f = sb("over_f", [P, 4])
        over_i = sb("over_i", [P, 4], I32)
        rt = sb("rt", [P, KT, 8])
        rt_hi = sb("rt_hi", [P, KT, 8], F32R)
        rt_lo = sb("rt_lo", [P, KT, 8], F32R)
        w_slot = sb("w_slot", [P, 1])
        disp = sb("disp", [P, TT, P], F32R)

        ident = cst[:, C_ID:C_ID + P]
        tri = cst[:, C_TRI:C_TRI + P]
        tri_ones = cst[:, C_TRI:C_TRI + 2 * P]
        ones = cst[:, C_ONES:C_ONES + P]
        stri = cst[:, C_STRI:C_STRI + P]
        iota = cst[:, C_IOTA:C_IOTA + P]
        lnc = cst[:, C_LNC:C_LNC + 3 * P]
        rope = cst[:, C_ROPE:C_E8].rearrange("p (a t d) -> p a t d", a=2, t=TT)
        iota8 = cst[:, C_E8:C_E8 + 8]

        hn = big[:, 0:2048].rearrange("p (t d) -> p t d", t=TT)
        rope_t1 = big[:, 0:1024].rearrange("p (t n) -> p t n", t=TT)
        rope_t2 = big[:, 1024:2048].rearrange("p (t n) -> p t n", t=TT)
        ke = big[:, 0:2048].rearrange("p (l t) -> p l t", l=8)
        rot_q = big[:, 2048:3072].rearrange("p (t n) -> p t n", t=TT)
        rot_k = big[:, 3072:4096].rearrange("p (t n) -> p t n", t=TT)
        dec = big[:, 2048:4096].rearrange("p (l t) -> p l t", l=8)
        qT = big[:, 4096:5120].rearrange("p (a t) -> p a t", a=4)
        kT = big[:, 5120:6144].rearrange("p (a t) -> p a t", a=4)
        gat = big[:, 4096:5120].rearrange("p (h t q) -> p h t q", h=GH, t=TT)
        gax = big[:, 5120:5632].rearrange("p (h q) -> p h q", h=GH)
        osq = big[:, 5632:6144]
        v_sb = big[:, 6144:7168].rearrange("p (t n) -> p t n", t=TT)
        gvo = big[:, 7168:8192].rearrange("p (t n) -> p t n", t=TT)
        ys = big[:, :].rearrange("p (e d) -> p e d", e=N_EXP)
        qe = work[:, :].rearrange("p (l t) -> p l t", l=8)
        z_abs = work[:, 0:256].rearrange("p (t f) -> p t f", t=TT)
        z_log = work[:, 256:512].rearrange("p (t f) -> p t f", t=TT)
        log_a = work[:, 512:768].rearrange("p (t f) -> p t f", t=TT)
        slotT = work[:, :].rearrange("p (e t) -> p e t", e=N_EXP)
        probs = (small[:, 0:3 * P], small[:, 3 * P:6 * P], gain[:, 0:3 * P])
        probsT = small[:, 768:1536].rearrange("p (b n) -> p b n", b=2)
        cc = small[:, 1536:2048].rearrange("p (f t) -> p f t", f=2)
        g_qk = act_x[:, :, :]
        bcum = work[:, 768:1024]
        cu = gate_x[:, :, :]
        cy = gain[:, 512:1024].rearrange("p (f t) -> p f t", f=2)

        gath = small[:, D:2 * D].rearrange("p (b n) -> p b n", b=2)
        lg = small[:, 0:16].rearrange("p (t e) -> p t e", t=TT)
        mx8 = small[:, 16:32].rearrange("p (t e) -> p t e", t=TT)
        ixf = small[:, 32:36].rearrange("p (t e) -> p t e", t=TT)
        top1 = small[:, 36:52].rearrange("p (t e) -> p t e", t=TT)
        top2 = small[:, 52:68].rearrange("p (t e) -> p t e", t=TT)
        chosen = small[:, 68:84].rearrange("p (t e) -> p t e", t=TT)
        comb = small[:, 84:100].rearrange("p (t e) -> p t e", t=TT)
        slot = small[:, 100:116].rearrange("p (t e) -> p t e", t=TT)
        tw = small[:, 116:124].rearrange("p (t e) -> p t e", t=TT)
        flag = small[:, 124:132]
        cum = small[:, 132:140]
        sel = small[:, 140:148]
        lgT = small[0:N_EXP, 256:512]

        in_x, in_gain0, in_cst, in_mask, in_small, in_gain, in_wz = (sem(n) for n in ("in_x", "in_gain0", "in_cst", "in_mask", "in_small", "in_gain", "in_wz"))
        landed = [sem(f"landed{i}") for i in range(RAW)]
        hi_done, lo_done, unit_used = sem("hi_done"), sem("lo_done"), sem("unit_used")
        dve_chain, act_chain, pool_chain = sem("dve_chain"), sem("act_chain"), sem("pool_chain")
        sq_act, hn_done, hnT_ps, hnT_hi, hnT_lo = (sem(n) for n in ("sq_act", "hn_done", "hnT_ps", "hnT_hi", "hnT_lo"))
        gain_used, res_done = sem("gain_used"), sem("res_done")
        wz_h, wz_l, zT_ps, zT_cp, zl_ps = (sem(n) for n in ("wz_h", "wz_l", "zT_ps", "zT_cp", "zl_ps"))
        zlog_done, loga_done, b_ps, b_cp = (sem(n) for n in ("zlog_done", "loga_done", "b_ps", "b_cp"))
        rope_mul, rope_add, qT_ps, kT_ps, qT_cp, kT_cp = (sem(n) for n in ("rope_mul", "rope_add", "qT_ps", "kT_ps", "qT_cp", "kT_cp"))
        v_cp, f_cp, t_cp = sem("v_cp"), sem("f_cp"), sem("t_cp")
        s_ps, s_max, s_exp, s_norm, pT_ps, pT_cp, att_ps, att_hi, att_lo = (
            sem(n) for n in ("s_ps", "s_max", "s_exp", "s_norm", "pT_ps", "pT_cp", "att_ps", "att_hi", "att_lo"))
        conv_u, conv_y, conv_out, conv_hi, conv_lo = (sem(n) for n in ("conv_u", "conv_y", "conv_out", "conv_hi", "conv_lo"))
        dec_sub, dec_exp, qe_done, ke_done, lv_ps, lv_cp, o_ps, o_sq, o_done, oT_ps, oT_hi, oT_lo = (
            sem(n) for n in ("dec_sub", "dec_exp", "qe_done", "ke_done", "lv_ps", "lv_cp", "o_ps", "o_sq", "o_done",
                             "oT_ps", "oT_hi", "oT_lo"))

        class FfnSems:
            def __init__(self, name):
                self.gu_first = sem(f"{name}_gu_first")
                self.silu = sem(f"{name}_silu")
                self.mul = sem(f"{name}_mul")
                self.aT_ps = sem(f"{name}_aT_ps")
                self.aT_hi = sem(f"{name}_aT_hi")
                self.aT_lo = sem(f"{name}_aT_lo")

        fd, fm = FfnSems("dense"), FfnSems("moe")
        rt_h, rt_l, lgT_ps, lgT_cp, lg_ps, lg_exp_in, lg_exp, chosen_done, pos_ps, route_done, tok_h, tok_l = (
            sem(n) for n in ("rt_h", "rt_l", "lgT_ps", "lgT_cp", "lg_ps", "lg_exp_in", "lg_exp", "chosen_done", "pos_ps", "route_done", "tok_h", "tok_l"))
        disp_done, ga_ps, ga_act, ga_dve, gaT_ps, ga_hi, ga_lo, slot_ps, slot_cp, y_free = (
            sem(n) for n in ("disp_done", "ga_ps", "ga_act", "ga_dve", "gaT_ps", "ga_hi", "ga_lo", "slot_ps", "slot_cp", "y_free"))
        sc_ps, sc_add, ov_ps = sem("sc_ps"), sem("sc_add"), sem("ov_ps")
        fin_done, out_sem = sem("fin_done"), sem("out_sem")

        def load_unit(sp, n, d=0, row=None):
            if n >= RAW:
                sp.wait_ge(lo_done, d * RAW + (n - RAW + 1))
            row = d * RAW + n if row is None else row
            src = stream[row] if isinstance(row, int) else stream[bass.ds(row, 1)].rearrange("a p c -> (a p) c")
            sp.dma_start(raw[:, n % RAW, :], src).then_inc(landed[n % RAW], 16)

        def hi_unit(act, n, d=0):
            act.wait_ge(landed[n % RAW], (d + (n // RAW + 1)) * 16)
            if n >= SPLIT:
                act.wait_ge(unit_used, d * RAW + (n - SPLIT + 1))
            nc.scalar.activation(w_hi[:, n % SPLIT, :], raw[:, n % RAW, :], ACT.Copy).then_inc(hi_done, 1)

        def lo_unit(dve, n, d=0):
            dve.wait_ge(hi_done, d * RAW + (n + 1))
            nc.vector.tensor_tensor(w_lo[:, n % SPLIT, :], raw[:, n % RAW, :], w_hi[:, n % SPLIT, :].bitcast(F32),
                                    ALU.subtract).then_inc(lo_done, 1)

        PASSES = ((0, 0), (1, 0), (0, 1))
        ALL_EXP = N_EXP * EXP_UNITS // RAW

        def w(n, part, a, b):
            return (w_hi, w_lo)[part][:, n % SPLIT, a:b]

        def used(eng, n, d=0):
            eng.wait_ge(unit_used, d * RAW + n)

        block = ctx.enter_context(nc.Block())

        @block.sync
        def _(sp):
            sp.dma_start(h[:, :, :], x.rearrange("a (t p) d -> p (a t) d", p=P)).then_inc(in_x, 16)
            sp.dma_start(gain[:, :], gains[0:1, :].to_broadcast([P, D])).then_inc(in_gain0, 16)
            sp.dma_start(cst[:, :], consts).then_inc(in_cst, 16)
            for n in range(RAW):
                load_unit(sp, n)
            for n in range(RAW, MIX_UNITS):
                load_unit(sp, n)
            with sp.Fori(0, DENSE_UNITS // RAW) as i:
                for j in range(RAW):
                    load_unit(sp, BASE_DENSE + j, i)
            for n in range(BASE_MIX[1] - DENSE_UNITS % RAW, BASE_MOE):
                load_unit(sp, n)
            with sp.Fori(0, N_EXP * EXP_UNITS // RAW) as i:
                for j in range(RAW):
                    load_unit(sp, BASE_MOE + j, i)
            sp.wait_ge(route_done, 1)
            n_over = sp.value_load(over_i[0:1, 0:1], min_val=0, max_val=3)
            with sp.If(n_over > 0):
                with sp.Fori(0, n_over) as k:
                    e = sp.value_load(over_i[0:1, bass.ds(k + 1, 1)], min_val=0, max_val=N_EXP - 1)
                    with sp.Fori(0, EXP_UNITS // RAW) as i:
                        for j in range(RAW):
                            load_unit(sp, BASE_MOE + j, k * (EXP_UNITS // RAW) + i + ALL_EXP,
                                      row=e * EXP_UNITS + i * RAW + (BASE_MOE + j))
            sp.wait_ge(fin_done, 2)
            sp.dma_start(out.rearrange("a (t p) d -> p (a t) d", p=P), hn[:, :, :]).then_inc(out_sem, 16)
            sp.wait_ge(out_sem, 16)

        @block.gpsimd
        def _(pool):
            chain = [0]

            def link(ins):
                chain[0] += 1
                ins.then_inc(pool_chain, 1)
                pool.wait_ge(pool_chain, chain[0])

            pool.dma_start(wz[:, :, :], w_z[0]).then_inc(in_wz, 16)
            pool.dma_start(wg[:, :], w_gate[0]).then_inc(in_wz, 16)
            mask_f = big[:, 7168:8192].rearrange("p (n q) -> p n q", n=len(LEVELS))
            pool.dma_start(mask_f, masks).then_inc(in_mask, 16)
            pool.dma_start(cw[:, :, :, :], conv_w).then_inc(in_small, 16)
            pool.dma_start(gg[:, :, :], gla_gain).then_inc(in_small, 16)
            pool.dma_start(rt[:, :, :], router).then_inc(in_small, 16)
            nc.gpsimd.memset(zero8[:, :], 0.0)
            link(nc.gpsimd.memset(zT[:, :], 1.0))
            pool.wait_ge(in_mask, 16)
            link(nc.gpsimd.tensor_copy(msk[:, :, :], mask_f))
            for L in range(DEPTH):
                for n, rot in enumerate((rot_q, rot_k)):
                    pool.wait_ge(rope_mul, 2 * L + n + 1)
                    nc.gpsimd.tensor_tensor(rot[:, :, :], rope_t1[:, :, :], rope_t2[:, :, :], ALU.add).then_inc(rope_add, 1)
                pool.wait_ge(dec_exp, L + 1)
                pool.wait_ge(f_cp, 3 * L + 2)
                nc.gpsimd.tensor_tensor(ke[:, :, :], dec[:, :, :],
                                        g_qk[:, 1, :].unsqueeze(1).to_broadcast([P, 8, SEQ]), ALU.mult).then_inc(ke_done, 1)
                pool.wait_ge(pT_ps, HEADS * (L + 1))
                pool.wait_ge(conv_lo, L + 1)
                pool.dma_start(gain[:, :], gains[2 * L + 1:2 * L + 2, :].to_broadcast([P, D])).then_inc(in_gain, 16)
                pool.wait_ge(gain_used, 2 * L + 2)
                if L == 0:
                    pool.dma_start(wz[:, :, :], w_z[1]).then_inc(in_wz, 16)
                    pool.dma_start(wg[:, :], w_gate[1]).then_inc(in_wz, 16)
                pool.dma_start(gain[:, :], gains[2 * L + 2:2 * L + 3, :].to_broadcast([P, D])).then_inc(in_gain, 16)

        @block.scalar
        def _(act):
            chain = [0]

            def link(ins):
                chain[0] += 1
                ins.then_inc(act_chain, 1)
                act.wait_ge(act_chain, chain[0])

            def copy(dst, src, scale=1.0):
                return nc.scalar.activation(dst, src, ACT.Copy, scale=scale)

            def norm(i):
                if i == 0:
                    act.wait_ge(in_x, 16)
                else:
                    act.wait_ge(res_done, i)
                nc.scalar.activation(hn[:, 1, :], h[:, 1, :], ACT.Square, accum_out=ss[:, 1:2]).then_inc(sq_act, 1)
                if i < 4:
                    for half in range(2):
                        act.wait_ge(hnT_ps, 2 * i + half + 1)
                        copy(xT_hi[:, 4 * half:4 * half + 4, :],
                             ps[:, 2 * half:2 * half + 2, :].rearrange("p b (k t) -> p (b k) t", k=2)).then_inc(hnT_hi, 1)

            def mixer(L):
                n0 = BASE_MIX[L]
                split = lambda j: hi_unit(act, n0 + j)
                if L == 0:
                    norm(0)
                act.wait_ge(in_wz, 32 * (L + 1))
                copy(wz_hi[:, :, :], wz[:, :, :]).then_inc(wz_h, 1)
                if L == 0:
                    split(0)
                    split(1)
                else:
                    norm(2)
                split(2)
                act.wait_ge(zT_ps, L + 1)
                if L == 0:
                    act.wait_ge(pool_chain, 1)
                copy(zT[0:RANK, :], ps[0:RANK, 7, 0:SEQ]).then_inc(zT_cp, 1)
                split(3)
                split(4)
                split(5)
                split(6)
                act.wait_ge(zl_ps, L + 1)
                link(nc.scalar.activation(z_abs[:, :, :], ps[:, 6, SEQ:2 * SEQ].rearrange("p (t f) -> p t f", t=TT), ACT.Abs))
                link(nc.scalar.activation(z_log[:, :, :], z_abs[:, :, :], ACT.Exp, scale=-1.0))
                nc.scalar.activation(z_log[:, :, :], z_log[:, :, :], ACT.Ln, bias=1.0).then_inc(zlog_done, 1)
                split(7)
                used(act, n0 + 6)
                copy(v_sb[:, :, :], ps[:, 0:2, :]).then_inc(v_cp, 1)
                split(8)
                act.wait_ge(qT_ps, L + 1)
                copy(qT[:, :, :], ps[:, 4:6, :].rearrange("p b (a t) -> p (b a) t", a=2), HD ** -0.5).then_inc(qT_cp, 1)
                used(act, n0 + 8)
                copy(g_qk[:, 0, :], ps[:, 2, 0:SEQ], GK ** -0.5).then_inc(f_cp, 1)
                copy(g_qk[:, 1, :], ps[:, 2, SEQ:2 * SEQ]).then_inc(f_cp, 1)
                copy(cc[:, :, :], ps[:, 3, :].rearrange("p (f t) -> p f t", f=2)).then_inc(f_cp, 1)
                split(9)
                split(10)
                act.wait_ge(dec_sub, L + 1)
                link(nc.scalar.activation(dec[:, :, :], dec[:, :, :], ACT.Abs))
                nc.scalar.activation(dec[:, :, :], dec[:, :, :], ACT.Exp, scale=-1.0 / TAU).then_inc(dec_exp, 1)
                used(act, n0 + 10)
                copy(gvo[:, :, 0:SEQ], ps[:, 0:2, 0:SEQ]).then_inc(t_cp, 1)
                nc.scalar.activation(gvo[:, :, SEQ:2 * SEQ], ps[:, 0:2, SEQ:2 * SEQ], ACT.Silu).then_inc(t_cp, 1)
                split(11)
                for step in range(HEADS + 4):
                    if step < HEADS:
                        b, pr = step % 2, probs[step % 3]
                        act.wait_ge(s_max, HEADS * L + step + 1)
                        nc.scalar.activation(pr[:, 0:P], pr[:, 0:P], ACT.Exp, bias=nmx[:, b, 0:1], accum_out=den[:, b, 0:1])
                        nc.scalar.activation(pr[:, P:3 * P], pr[:, P:3 * P], ACT.Exp, bias=nmx[:, b, 1:2],
                                             accum_out=den[:, b, 1:2]).then_inc(s_exp, 1)
                    if 2 <= step <= HEADS + 1:
                        hd = step - 2
                        act.wait_ge(pT_ps, HEADS * L + hd + 1)
                        if hd >= 2:
                            act.wait_ge(att_ps, HEADS * L + hd - 1)
                        copy(probsT[:, hd % 2, :], ps[:, 6 + hd % 2, 0:3 * P]).then_inc(pT_cp, 1)
                    if step in (3, 6, 8):
                        split({3: 12, 6: 13, 8: 14}[step])
                    if step >= 5 and step % 2 == 1:
                        pair = (step - 5) // 2
                        act.wait_ge(att_ps, HEADS * L + 2 * pair + 2)
                        copy(mixT_hi[:, pair, :], ps[:, pair % 2, pair // 2 * SEQ:(pair // 2 + 1) * SEQ]).then_inc(att_hi, 1)
                act.wait_ge(conv_out, L + 1)
                copy(mixT_hi[:, 4:6, :], cy[:, :, :]).then_inc(conv_hi, 1)
                act.wait_ge(o_ps, L + 1)
                nc.scalar.activation(osq, ps[:, 4, :], ACT.Square).then_inc(o_sq, 1)
                split(15)
                act.wait_ge(oT_ps, L + 1)
                for f in range(2):
                    copy(mixT_hi[:, 6 + f, :], ps[:, 5 + f, 0:SEQ], gg[:, L, f:f + 1]).then_inc(oT_hi, 1)

            def ffn_block(S, tiles, B, par, n, d=0):
                for t in range(tiles):
                    s = t if tiles == 2 else par
                    if t < tiles - 1:
                        act.wait_ge(S.gu_first, B + 1)
                    else:
                        used(act, n, d)
                    nc.scalar.activation(gate_x[:, s, :], ps[:, 4 + s, 0:FB], ACT.Silu).then_inc(S.silu, 1)

            def ffn_aT(S, tiles, B, par):
                act.wait_ge(S.aT_ps, B + 1)
                if tiles == 2:
                    copy(aT_hi[:, :, :, :], ps[:, 6 + par, :].rearrange("p (t f q) -> p t f q", t=2, f=2)).then_inc(S.aT_hi, 1)
                else:
                    copy(aT_hi[:, par, :, :], ps[:, 6 + par, 0:FB].rearrange("p (f q) -> p f q", f=2)).then_inc(S.aT_hi, 1)

            def gathered(e):
                act.wait_ge(ga_ps, e + 1)
                copy(gath[:, 0, :], ps[:, 2, :]).then_inc(ga_act, 1)

            def gather_hi(e, g):
                act.wait_ge(gaT_ps, e * 2 + (g + 1))
                copy(xT_hi[:, 4 * g:4 * g + 4, 0:P], ps[:, 2 + g, :].rearrange("p (k s) -> p k s", k=4)).then_inc(ga_hi, 1)

            def expert_start(e, n, d):
                gathered(e)
                for g in (0, 1):
                    gather_hi(e, g)
                    hi_unit(act, n + g, d)
                hi_unit(act, n + 2, d)
                ffn_block(fm, 1, e * EXP_BLOCKS, 0, n + 2, d)
                hi_unit(act, n + 3, d)

            def expert_middle(e, n, d):
                with act.Fori(0, (EXP_BLOCKS - 2) // 2) as i:
                    for p in range(2):
                        B = e * EXP_BLOCKS + i * 2 + p
                        m = n + 4 + 3 * p
                        hi_unit(act, m, d + i)
                        ffn_aT(fm, 1, B, p)
                        hi_unit(act, m + 1, d + i)
                        ffn_block(fm, 1, B + 1, 1 - p, m, d + i)
                        hi_unit(act, m + 2, d + i)

            def expert_end(e, n, d, follow):
                B = e * EXP_BLOCKS + (EXP_BLOCKS - 2)
                hi_unit(act, n + EXP_UNITS - 2, d)
                ffn_aT(fm, 1, B, 0)
                hi_unit(act, n + EXP_UNITS - 1, d)
                if follow:
                    gathered(e + 1)
                ffn_block(fm, 1, B + 1, 1, n + EXP_UNITS - 2, d)
                ffn_aT(fm, 1, B + 1, 1)
                if follow:
                    for g in (0, 1):
                        gather_hi(e + 1, g)
                        hi_unit(act, n + g, d + EXP_UNITS // RAW)

            def expert_out(e, n, d):
                used(act, n + EXP_UNITS, d)
                act.wait_ge(slot_cp, 3 * (e + 1))
                dst = ys[:, e, :] if isinstance(e, int) else ys[:, bass.ds(e, 1), :].rearrange("p a d -> p (a d)")
                copy(dst, ps[:, 0:2, :].rearrange("p a d -> p (a d)"), w_slot[:, 0:1]).then_inc(y_free, 1)

            act.sem_inc(y_free, 1)
            mixer(0)
            n0 = BASE_DENSE
            hi_unit(act, n0)
            hi_unit(act, n0 + 1)
            norm(1)
            hi_unit(act, n0 + 2)
            ffn_block(fd, 2, 0, 0, n0 + 2)
            hi_unit(act, n0 + 3)
            with act.Fori(0, (DENSE_BLOCKS - 1) // 2) as i:
                for p in range(2):
                    B = i * 2 + p
                    m = n0 + 4 + 3 * p
                    hi_unit(act, m, i)
                    ffn_aT(fd, 2, B, p)
                    hi_unit(act, m + 1, i)
                    ffn_block(fd, 2, B + 1, 0, m, i)
                    hi_unit(act, m + 2, i)
            ffn_aT(fd, 2, DENSE_BLOCKS - 1, 0)
            hi_unit(act, BASE_MIX[1] + 1)
            mixer(1)
            act.wait_ge(in_small, 48)
            copy(rt_hi[:, :, :], rt[:, :, :]).then_inc(rt_h, 1)
            norm(3)
            act.wait_ge(hn_done, 8)
            copy(tok_hi[:, :, :], hn[:, :, :]).then_inc(tok_h, 1)
            act.wait_ge(lg_exp_in, 1)
            nc.scalar.activation(tw[:, :, 1:2], tw[:, :, 0:1], ACT.Exp).then_inc(lg_exp, 1)
            expert_start(0, BASE_MOE, 0)
            with act.Fori(0, N_EXP - 1) as e:
                d = e * (EXP_UNITS // RAW)
                expert_middle(e, BASE_MOE, d)
                expert_end(e, BASE_MOE, d + (EXP_UNITS // RAW) * 0, True)
                expert_out(e, BASE_MOE, d)
                hi_unit(act, BASE_MOE + 2, d + EXP_UNITS // RAW)
                ffn_block(fm, 1, (e + 1) * EXP_BLOCKS, 0, BASE_MOE + 2, d + EXP_UNITS // RAW)
                hi_unit(act, BASE_MOE + 3, d + EXP_UNITS // RAW)
            last = N_EXP - 1
            expert_middle(last, BASE_MOE, last * (EXP_UNITS // RAW))
            expert_end(last, BASE_MOE, last * (EXP_UNITS // RAW), False)
            expert_out(last, BASE_MOE, last * (EXP_UNITS // RAW))
            act.wait_ge(route_done, 1)
            n_over = act.value_load(over_i[0:1, 0:1], min_val=0, max_val=3)
            with act.If(n_over > 0):
                with act.Fori(0, n_over) as k:
                    e = k + N_EXP
                    d = k * (EXP_UNITS // RAW) + N_EXP * (EXP_UNITS // RAW)
                    expert_start(e, BASE_MOE, d)
                    expert_middle(e, BASE_MOE, d)
                    expert_end(e, BASE_MOE, d, False)
                    used(act, BASE_MOE + EXP_UNITS, d)
                    act.wait_ge(slot_cp, 3 * (e + 1))
                    copy(ys[:, 0, :], ps[:, 0:2, :].rearrange("p a d -> p (a d)"), w_slot[:, 0:1]).then_inc(y_free, 1)
            norm(4)

        @block.vector
        def _(dve):
            chain = [0]

            def link(ins):
                chain[0] += 1
                ins.then_inc(dve_chain, 1)
                dve.wait_ge(dve_chain, chain[0])

            def rsqrt_mean(src, n, width, y):
                t = nwt[:, 0:n]
                link(nc.vector.tensor_scalar(src, src, 1.0 / width, EPS, ALU.mult, ALU.add))
                link(nc.vector.tensor_scalar(y.bitcast(I32), src.bitcast(I32), -0.5, RSQRT_BITS, ALU.mult, ALU.add))
                for _ in range(3):
                    link(nc.vector.scalar_tensor_tensor(out=t, in0=y, scalar=-0.5, in1=y, op0=ALU.mult, op1=ALU.mult))
                    link(nc.vector.tensor_tensor(t, t, src, ALU.mult))
                    link(nc.vector.scalar_tensor_tensor(out=y, in0=t, scalar=1.5, in1=y, op0=ALU.add, op1=ALU.mult))

            def norm(i):
                if i == 0:
                    dve.wait_ge(in_x, 16)
                link(nc.vector.tensor_tensor_reduce(out=hn[:, 0, :], in0=h[:, 0, :], in1=h[:, 0, :], scale=1.0, scalar=0.0,
                                                    op0=ALU.mult, op1=ALU.add, accum_out=ss[:, 0:1]))
                dve.wait_ge(sq_act, i + 1)
                rsqrt_mean(ss[:, :], TT, D, rs[:, 0:TT])
                if i == 0:
                    dve.wait_ge(in_gain0, 16)
                else:
                    dve.wait_ge(in_gain, 16 * i)
                for t in range(TT):
                    ins = nc.vector.scalar_tensor_tensor(out=hn[:, t, :], in0=h[:, t, :], scalar=rs[:, t:t + 1],
                                                         in1=gain[:, :], op0=ALU.mult, op1=ALU.mult)
                    ins.then_inc(fin_done if i == 4 else hn_done, 1)
                if i < 4:
                    dve.wait_ge(hn_done, 2 * (i + 1))
                    dve.sem_inc(gain_used, 1)
                    for half in range(2):
                        dve.wait_ge(hnT_hi, 2 * i + half + 1)
                        nc.vector.tensor_tensor(xT_lo[:, 4 * half:4 * half + 4, :],
                                                ps[:, 2 * half:2 * half + 2, :].rearrange("p b (k t) -> p (b k) t", k=2),
                                                xT_hi[:, 4 * half:4 * half + 4, :].bitcast(F32),
                                                ALU.subtract).then_inc(hnT_lo, 1)

            def rope_mults(first):
                x = ps[:, first:first + 2, :].rearrange("p t (h d) -> p t h d", h=HEADS)
                t1 = rope_t1[:, :, :].rearrange("p t (h d) -> p t h d", h=HEADS)
                t2 = rope_t2[:, :, :].rearrange("p t (h d) -> p t h d", h=HEADS)
                c = rope[:, 0].unsqueeze(2).to_broadcast([P, TT, HEADS, HD])
                s = rope[:, 1].unsqueeze(2).to_broadcast([P, TT, HEADS, HD])
                half = HD // 2
                nc.vector.tensor_tensor(t1, x, c, ALU.mult)
                nc.vector.tensor_tensor(t2[:, :, :, 0:half], x[:, :, :, half:HD], s[:, :, :, 0:half], ALU.mult)
                nc.vector.tensor_tensor(t2[:, :, :, half:HD], x[:, :, :, 0:half], s[:, :, :, half:HD],
                                        ALU.mult).then_inc(rope_mul, 1)

            def residual(n):
                used(dve, n)
                for t in range(TT):
                    for half in range(2):
                        ins = nc.vector.tensor_tensor(h[:, t, half * 512:(half + 1) * 512], h[:, t, half * 512:(half + 1) * 512],
                                                      ps[:, 2 * t + half, :], ALU.add)
                link(ins)
                dve.sem_inc(res_done, 1)

            def mixer(L):
                n0 = BASE_MIX[L]
                split = lambda j: lo_unit(dve, n0 + j)
                if L == 0:
                    norm(0)
                dve.wait_ge(wz_h, L + 1)
                nc.vector.tensor_tensor(wz_lo[:, :, :], wz[:, :, :], wz_hi[:, :, :].bitcast(F32), ALU.subtract).then_inc(wz_l, 1)
                if L == 0:
                    split(0)
                    split(1)
                    dve.wait_ge(in_cst, 16)
                    dve.wait_ge(in_small, 48)
                else:
                    norm(2)
                split(2)
                split(3)
                used(dve, n0 + 2)
                rope_mults(0)
                split(4)
                split(5)
                zl = ps[:, 6, SEQ:2 * SEQ].rearrange("p (t f) -> p t f", t=TT)
                used(dve, n0 + 4)
                dve.wait_ge(rope_add, 2 * L + 1)
                rope_mults(2)
                split(6)
                dve.wait_ge(zlog_done, L + 1)
                nc.vector.scalar_tensor_tensor(out=log_a[:, :, :], in0=zl, scalar=0.0, in1=z_log[:, :, :], op0=ALU.min,
                                               op1=ALU.subtract).then_inc(loga_done, 1)
                split(7)
                split(8)
                dve.wait_ge(b_ps, L + 1)
                nc.vector.tensor_copy(bcum[:, :], ps[:, 7, SEQ:2 * SEQ]).then_inc(b_cp, 1)
                dve.wait_ge(kT_ps, L + 1)
                nc.vector.tensor_copy(kT[:, :, :], ps[:, 6:8, :].rearrange("p b (a t) -> p (b a) t", a=2)).then_inc(kT_cp, 1)
                split(9)
                split(10)
                dve.wait_ge(b_cp, L + 1)
                for n, half in enumerate(LEVELS):
                    b3 = bcum[:, :].rearrange("p (i j) -> p i j", j=2 * half)
                    ref = b3[:, :, half - 1:half].to_broadcast([P, SEQ // (2 * half), 2 * half])
                    ins = nc.vector.tensor_tensor(dec[:, n, :].rearrange("p (i j) -> p i j", j=2 * half), b3, ref, ALU.subtract)
                ins.then_inc(dec_sub, 1)
                split(11)
                dve.wait_ge(dec_exp, L + 1)
                dve.wait_ge(f_cp, 3 * L + 1)
                nc.vector.tensor_tensor(qe[:, :, :], dec[:, :, :], g_qk[:, 0, :].unsqueeze(1).to_broadcast([P, 8, SEQ]),
                                        ALU.mult).then_inc(qe_done, 1)
                for step in range(HEADS + 4):
                    if step < HEADS:
                        b, pr = step % 2, probs[step % 3]
                        dve.wait_ge(s_ps, HEADS * L + step + 1)
                        if step >= 3:
                            dve.wait_ge(pT_ps, HEADS * L + step - 2)
                        nc.vector.tensor_tensor_reduce(out=pr[:, 0:P], in0=ps[:, 4 + b, 0:P], in1=lnc[:, 0:P], scale=1.0,
                                                       scalar=-3e38, op0=ALU.add, op1=ALU.max, accum_out=mx[:, b, 0:1])
                        link(nc.vector.tensor_tensor_reduce(out=pr[:, P:3 * P], in0=ps[:, 4 + b, P:3 * P],
                                                            in1=lnc[:, P:3 * P], scale=1.0, scalar=-3e38, op0=ALU.add,
                                                            op1=ALU.max, accum_out=mx[:, b, 1:2]))
                        nc.vector.tensor_scalar(nmx[:, b, :], mx[:, b, :], -1.0, None, ALU.mult).then_inc(s_max, 1)
                    if 1 <= step <= HEADS:
                        hd = step - 1
                        b, pr = hd % 2, probs[hd % 3]
                        dve.wait_ge(s_exp, HEADS * L + hd + 1)
                        link(nc.vector.reciprocal(rden[:, b, :], den[:, b, :]))
                        nc.vector.tensor_scalar(pr[:, 0:P], pr[:, 0:P], rden[:, b, 0:1], None, ALU.mult)
                        nc.vector.tensor_scalar(pr[:, P:3 * P], pr[:, P:3 * P], rden[:, b, 1:2], None,
                                                ALU.mult).then_inc(s_norm, 1)
                    if step in (3, 6, 8):
                        split({3: 12, 6: 13, 8: 14}[step])
                    if step == 9:
                        used(dve, n0 + 12)
                        dve.wait_ge(f_cp, 3 * L + 3)
                        link(nc.vector.tensor_tensor(cu, cc[:, :, :], ps[:, 2, :].rearrange("p (f t) -> p f t", f=2), ALU.mult))
                        for f in range(2):
                            u, y = cu[:, f, :], cy[:, f, :]
                            link(nc.vector.tensor_scalar(y, u, cw[:, L, f, 2:3], None, ALU.mult))
                            link(nc.vector.scalar_tensor_tensor(out=y[:, 1:SEQ], in0=u[:, 0:SEQ - 1], scalar=cw[:, L, f, 1:2],
                                                                in1=y[:, 1:SEQ], op0=ALU.mult, op1=ALU.add))
                            link(nc.vector.scalar_tensor_tensor(out=y[:, 2:SEQ], in0=u[:, 0:SEQ - 2], scalar=cw[:, L, f, 0:1],
                                                                in1=y[:, 2:SEQ], op0=ALU.mult, op1=ALU.add))
                        nc.vector.tensor_tensor(cy, cy, ps[:, 3, :].rearrange("p (f t) -> p f t", f=2),
                                                ALU.mult).then_inc(conv_out, 1)
                    if step >= 5 and step % 2 == 1:
                        pair = (step - 5) // 2
                        dve.wait_ge(att_hi, 4 * L + pair + 1)
                        nc.vector.tensor_tensor(mixT_lo[:, pair, :], ps[:, pair % 2, pair // 2 * SEQ:(pair // 2 + 1) * SEQ],
                                                mixT_hi[:, pair, :].bitcast(F32), ALU.subtract).then_inc(att_lo, 1)
                dve.wait_ge(conv_hi, L + 1)
                nc.vector.tensor_tensor(mixT_lo[:, 4:6, :], cy, mixT_hi[:, 4:6, :].bitcast(F32), ALU.subtract).then_inc(conv_lo, 1)
                dve.wait_ge(pool_chain, 2)
                for n in range(9):
                    dve.wait_ge(lv_ps, 9 * L + n + 1)
                    if n:
                        dve.wait_ge(lv_cp, 9 * L + n)
                    b0 = 4 - n % 2 * 4
                    src = ps[:, b0:b0 + 4, 0:SEQ].rearrange("p h (t q) -> p h t q", t=TT)
                    if n == 8:
                        nc.vector.tensor_copy(gax[:, :, :], src[:, :, 0, :]).then_inc(lv_cp, 1)
                        continue
                    for t in range(TT):
                        if n == 0:
                            m = msk[:, 7, :].unsqueeze(1).to_broadcast([P, GH, P])
                            ins = nc.vector.tensor_tensor(gat[:, :, t, :], src[:, :, t, :], m, ALU.mult)
                        else:
                            m = msk[:, n - 1, :].unsqueeze(1).to_broadcast([P, GH, P])
                            ins = nc.vector.copy_predicated(gat[:, :, t, :], m, src[:, :, t, :])
                        if t == 0:
                            continue
                        ins.then_inc(lv_cp, 1)
                dve.wait_ge(o_sq, L + 1)
                link(nc.vector.tensor_reduce(gss[:, :], osq.rearrange("p (g d) -> p g d", d=GV), AX_X, ALU.add))
                rsqrt_mean(gss[:, :], 8, GV, rs[:, :])
                og = cc[:, :, :].rearrange("p t (g d) -> p (t g) d", d=GV)
                link(nc.vector.tensor_tensor(og, ps[:, 4, :].rearrange("p (g d) -> p g d", d=GV),
                                             rs[:, :].unsqueeze(2).to_broadcast([P, 8, GV]), ALU.mult))
                dve.wait_ge(t_cp, 2 * (L + 1))
                nc.vector.tensor_tensor(cc[:, :, :], cc[:, :, :], gvo[:, :, SEQ:2 * SEQ], ALU.mult).then_inc(o_done, 1)
                split(15)
                for f in range(2):
                    dve.wait_ge(oT_hi, 2 * L + f + 1)
                    nc.vector.scalar_tensor_tensor(out=mixT_lo[:, 6 + f, :], in0=ps[:, 5 + f, 0:SEQ],
                                                   scalar=gg[:, L, f:f + 1], in1=mixT_hi[:, 6 + f, :].bitcast(F32),
                                                   op0=ALU.mult, op1=ALU.subtract).then_inc(oT_lo, 1)

            def ffn_block(S, tiles, B, par, n, d=0):
                for t in range(tiles):
                    s = t if tiles == 2 else par
                    dve.wait_ge(S.silu, B * tiles + (t + 1))
                    nc.vector.tensor_tensor(act_x[:, s, :], gate_x[:, s, :], ps[:, 4 + s, FB:2 * FB], ALU.mult).then_inc(S.mul, 1)

            def ffn_aT(S, tiles, B, par):
                dve.wait_ge(S.aT_hi, B + 1)
                if tiles == 2:
                    dst, hi = aT_lo[:, :, :, :], aT_hi[:, :, :, :]
                    src = ps[:, 6 + par, :].rearrange("p (t f q) -> p t f q", t=2, f=2)
                else:
                    dst, hi = aT_lo[:, par, :, :], aT_hi[:, par, :, :]
                    src = ps[:, 6 + par, 0:FB].rearrange("p (f q) -> p f q", f=2)
                nc.vector.tensor_tensor(dst, src, hi.bitcast(F32), ALU.subtract).then_inc(S.aT_lo, 1)

            def dispatch(e, over):
                for t in range(TT):
                    s = slot[:, t, e:e + 1] if isinstance(e, int) else slot[:, t, bass.ds(e, 1)]
                    ins = nc.vector.tensor_scalar(disp[:, t, :], iota, 128.0 if over else 0.0, s, ALU.add, ALU.is_equal)
                ins.then_inc(disp_done, 1)

            def gathered(e):
                dve.wait_ge(ga_ps, e + 1)
                nc.vector.tensor_copy(gath[:, 1, :], ps[:, 3, :]).then_inc(ga_dve, 1)

            def gather_lo(e, g):
                dve.wait_ge(ga_hi, e * 2 + (g + 1))
                nc.vector.tensor_tensor(xT_lo[:, 4 * g:4 * g + 4, 0:P], ps[:, 2 + g, :].rearrange("p (k s) -> p k s", k=4),
                                        xT_hi[:, 4 * g:4 * g + 4, 0:P].bitcast(F32), ALU.subtract).then_inc(ga_lo, 1)

            def slots(e):
                dve.wait_ge(slot_ps, e + 1)
                dst = slotT[:, e, :] if isinstance(e, int) else slotT[:, bass.ds(e, 1), :].rearrange("p a t -> p (a t)")
                nc.vector.tensor_copy(dst, ps[:, 6, SEQ:2 * SEQ]).then_inc(slot_cp, 2)
                dve.wait_ge(y_free, e + 1)
                nc.vector.tensor_copy(w_slot[:, :], ps[:, 7, SEQ:SEQ + 1]).then_inc(slot_cp, 1)

            def expert_start(e, n, d):
                gathered(e)
                for g in (0, 1):
                    gather_lo(e, g)
                    lo_unit(dve, n + g, d)
                lo_unit(dve, n + 2, d)
                slots(e)
                ffn_block(fm, 1, e * EXP_BLOCKS, 0, n + 2, d)
                lo_unit(dve, n + 3, d)

            def expert_middle(e, n, d):
                with dve.Fori(0, (EXP_BLOCKS - 2) // 2) as i:
                    for p in range(2):
                        B = e * EXP_BLOCKS + i * 2 + p
                        m = n + 4 + 3 * p
                        lo_unit(dve, m, d + i)
                        ffn_aT(fm, 1, B, p)
                        lo_unit(dve, m + 1, d + i)
                        ffn_block(fm, 1, B + 1, 1 - p, m, d + i)
                        lo_unit(dve, m + 2, d + i)

            def expert_end(e, n, d, follow):
                B = e * EXP_BLOCKS + (EXP_BLOCKS - 2)
                if follow:
                    dve.wait_ge(slot_ps, e + 1)
                    dispatch(e + 1, False)
                lo_unit(dve, n + EXP_UNITS - 2, d)
                ffn_aT(fm, 1, B, 0)
                lo_unit(dve, n + EXP_UNITS - 1, d)
                if follow:
                    gathered(e + 1)
                ffn_block(fm, 1, B + 1, 1, n + EXP_UNITS - 2, d)
                ffn_aT(fm, 1, B + 1, 1)
                if follow:
                    for g in (0, 1):
                        gather_lo(e + 1, g)
                        lo_unit(dve, n + g, d + EXP_UNITS // RAW)

            mixer(0)
            n0 = BASE_DENSE
            lo_unit(dve, n0)
            residual(BASE_DENSE)
            lo_unit(dve, n0 + 1)
            norm(1)
            lo_unit(dve, n0 + 2)
            ffn_block(fd, 2, 0, 0, n0 + 2)
            lo_unit(dve, n0 + 3)
            with dve.Fori(0, (DENSE_BLOCKS - 1) // 2) as i:
                for p in range(2):
                    B = i * 2 + p
                    m = n0 + 4 + 3 * p
                    lo_unit(dve, m, i)
                    ffn_aT(fd, 2, B, p)
                    lo_unit(dve, m + 1, i)
                    ffn_block(fd, 2, B + 1, 0, m, i)
                    lo_unit(dve, m + 2, i)
            ffn_aT(fd, 2, DENSE_BLOCKS - 1, 0)
            lo_unit(dve, BASE_MIX[1] + 1)
            residual(BASE_MIX[1])
            mixer(1)
            residual(BASE_MOE)
            dve.wait_ge(rt_h, 1)
            nc.vector.tensor_tensor(rt_lo[:, :, :], rt[:, :, :], rt_hi[:, :, :].bitcast(F32), ALU.subtract).then_inc(rt_l, 1)
            norm(3)
            dve.wait_ge(tok_h, 1)
            nc.vector.tensor_tensor(tok_lo[:, :, :], hn[:, :, :], tok_hi[:, :, :].bitcast(F32), ALU.subtract).then_inc(tok_l, 1)
            dve.wait_ge(lgT_ps, 1)
            nc.vector.tensor_copy(lgT, ps[0:N_EXP, 7, 0:SEQ]).then_inc(lgT_cp, 1)
            dve.wait_ge(lg_ps, 1)
            link(nc.vector.tensor_copy(lg[:, :, :], ps[:, 6, 0:16].rearrange("p (t e) -> p t e", t=TT)))
            for t in range(TT):
                link(nc.vector.max(mx8[:, t, :], lg[:, t, :]))
            for t in range(TT):
                ins = nc.vector.max_index(ix8[:, t, :], mx8[:, t, :], lg[:, t, :])
            link(ins)
            nc.vector.tensor_tensor(tw[:, :, 0:1], mx8[:, :, 1:2], mx8[:, :, 0:1], ALU.subtract).then_inc(lg_exp_in, 1)
            link(nc.vector.tensor_copy(ixf[:, :, :], ix8[:, :, 0:2]))
            for n, top in enumerate((top1, top2)):
                for t in range(TT):
                    ins = nc.vector.tensor_scalar(top[:, t, :], iota8, ixf[:, t, n:n + 1], None, ALU.is_equal)
            link(ins)
            nc.vector.tensor_tensor(chosen[:, :, :], top1[:, :, :], top2[:, :, :], ALU.add).then_inc(chosen_done, 1)
            dve.wait_ge(lg_exp, 1)
            link(nc.vector.tensor_scalar(tw[:, :, 2:3], tw[:, :, 1:2], 1.0, None, ALU.add))
            link(nc.vector.reciprocal(tw[:, :, 2:3], tw[:, :, 2:3]))
            link(nc.vector.tensor_tensor(tw[:, :, 3:4], tw[:, :, 1:2], tw[:, :, 2:3], ALU.mult))
            for t in range(TT):
                ins = nc.vector.tensor_scalar(comb[:, t, :], top1[:, t, :], tw[:, t, 2:3], None, ALU.mult)
            link(ins)
            for t in range(TT):
                ins = nc.vector.scalar_tensor_tensor(out=comb[:, t, :], in0=top2[:, t, :], scalar=tw[:, t, 3:4],
                                                     in1=comb[:, t, :], op0=ALU.mult, op1=ALU.add)
            link(ins)
            dve.wait_ge(chosen_done, 1)
            dve.wait_ge(pos_ps, 1)
            link(nc.vector.scalar_tensor_tensor(out=slot[:, :, :], in0=ps[:, 7, 0:16].rearrange("p (t e) -> p t e", t=TT),
                                                scalar=1.0, in1=chosen[:, :, :], op0=ALU.add, op1=ALU.mult))
            link(nc.vector.tensor_scalar(slot[:, :, :], slot[:, :, :], -1.0, None, ALU.add))
            link(nc.vector.tensor_scalar(flag[:, :], ps[:, 7, 16:24], float(P), None, ALU.is_gt))
            dispatch(0, False)
            link(nc.vector.tensor_tensor_scan(cum[:, :], flag[:, :], zero8[:, :], 0.0, ALU.add, ALU.add))
            link(nc.vector.tensor_copy(over_f[:, 0:1], cum[:, 7:8]))
            for k in range(3):
                link(nc.vector.scalar_tensor_tensor(out=sel[:, :], in0=cum[:, :], scalar=float(k + 1), in1=flag[:, :],
                                                    op0=ALU.is_equal, op1=ALU.mult))
                link(nc.vector.tensor_tensor_reduce(out=sel[:, :], in0=sel[:, :], in1=iota8, scale=1.0, scalar=0.0,
                                                    op0=ALU.mult, op1=ALU.add, accum_out=over_f[:, k + 1:k + 2]))
            nc.vector.tensor_copy(over_i[:, :], over_f[:, :]).then_inc(route_done, 1)
            expert_start(0, BASE_MOE, 0)
            with dve.Fori(0, N_EXP - 1) as e:
                d = e * (EXP_UNITS // RAW)
                expert_middle(e, BASE_MOE, d)
                expert_end(e, BASE_MOE, d, True)
                lo_unit(dve, BASE_MOE + 2, d + EXP_UNITS // RAW)
                slots(e + 1)
                ffn_block(fm, 1, (e + 1) * EXP_BLOCKS, 0, BASE_MOE + 2, d + EXP_UNITS // RAW)
                lo_unit(dve, BASE_MOE + 3, d + EXP_UNITS // RAW)
            last = N_EXP - 1
            expert_middle(last, BASE_MOE, last * (EXP_UNITS // RAW))
            expert_end(last, BASE_MOE, last * (EXP_UNITS // RAW), False)
            for t in range(TT):
                for half in range(2):
                    dve.wait_ge(sc_ps, 2 * t + half + 1)
                    ins = nc.vector.tensor_tensor(h[:, t, half * 512:(half + 1) * 512], h[:, t, half * 512:(half + 1) * 512],
                                                  ps[:, 2 + 2 * t + half, :], ALU.add)
            ins.then_inc(sc_add, 1)
            dve.wait_ge(sc_add, 1)
            dve.wait_ge(route_done, 1)
            n_over = dve.value_load(over_i[0:1, 0:1], min_val=0, max_val=3)
            with dve.If(n_over > 0):
                with dve.Fori(0, n_over) as k:
                    e = k + N_EXP
                    ex = dve.value_load(over_i[0:1, bass.ds(k + 1, 1)], min_val=0, max_val=N_EXP - 1)
                    d = k * (EXP_UNITS // RAW) + N_EXP * (EXP_UNITS // RAW)
                    dve.wait_ge(slot_ps, e)
                    dispatch(ex, True)
                    gathered(e)
                    for g in (0, 1):
                        gather_lo(e, g)
                        lo_unit(dve, BASE_MOE + g, d)
                    lo_unit(dve, BASE_MOE + 2, d)
                    dve.wait_ge(slot_ps, e + 1)
                    dve.wait_ge(y_free, e + 1)
                    nc.vector.tensor_copy(slotT[:, 0, :], ps[:, 6, SEQ:2 * SEQ]).then_inc(slot_cp, 2)
                    nc.vector.tensor_copy(w_slot[:, :], ps[:, 7, SEQ:SEQ + 1]).then_inc(slot_cp, 1)
                    ffn_block(fm, 1, e * EXP_BLOCKS, 0, BASE_MOE + 2, d)
                    lo_unit(dve, BASE_MOE + 3, d)
                    expert_middle(e, BASE_MOE, d)
                    expert_end(e, BASE_MOE, d, False)
                    dve.wait_ge(ov_ps, k + 1)
                    for t in range(TT):
                        for half in range(2):
                            ins = nc.vector.tensor_tensor(h[:, t, half * 512:(half + 1) * 512],
                                                          h[:, t, half * 512:(half + 1) * 512],
                                                          ps[:, 2 + 2 * t + half, :], ALU.add)
                    ins.then_inc(sc_add, 1)
                    dve.wait_ge(sc_add, k + 2)
            dve.sem_inc(res_done, 1)
            norm(4)

        @block.tensor
        def _(pe):
            def unit_ready(n, d=0):
                pe.wait_ge(lo_done, d * RAW + (n + 1))

            def norm(i):
                pe.wait_ge(hn_done, 2 * (i + 1))
                for half in range(2):
                    for t in range(TT):
                        for kk in range(4):
                            k = 4 * half + kk
                            last = nc.tensor.transpose(ps[:, k // 2, k % 2 * SEQ + t * P:k % 2 * SEQ + (t + 1) * P],
                                                       hn[:, t, k * P:(k + 1) * P], ident)
                    last.then_inc(hnT_ps, 1)

            def narrow(dst, hi, lo):
                for k in range(KT):
                    for xp, wp in PASSES:
                        last = nc.tensor.matmul(dst, (hi, lo)[wp][:, k, :], (xT_hi, xT_lo)[xp][:, k, :],
                                                start=(k == 0 and xp == wp), stop=(k == KT - 1 and wp == 1))
                return last

            def tokens_first(n, half, bank):
                unit_ready(n)
                for t in range(TT):
                    for kk in range(4):
                        k = 4 * half + kk
                        for xp, wp in PASSES:
                            last = nc.tensor.matmul(ps[:, bank + t, :], (xT_hi, xT_lo)[xp][:, k, t * P:(t + 1) * P],
                                                    w(n, wp, kk * 512, (kk + 1) * 512),
                                                    start=(k == 0 and xp == wp), stop=(k == KT - 1 and wp == 1))
                last.then_inc(unit_used, 1)

            def features_first(n, half, bank):
                unit_ready(n)
                for kk in range(4):
                    k = 4 * half + kk
                    for f in range(4):
                        for xp, wp in PASSES:
                            last = nc.tensor.matmul(ps[:, bank + f // 2, f % 2 * SEQ:(f % 2 + 1) * SEQ],
                                                    w(n, wp, kk * 512 + f * P, kk * 512 + (f + 1) * P),
                                                    (xT_hi, xT_lo)[xp][:, k, :],
                                                    start=(k == 0 and f % 2 == 0 and xp == wp),
                                                    stop=(k == KT - 1 and wp == 1), skip_group_check=True)
                last.then_inc(unit_used, 1)

            def w_in_block(fn, n, bank):
                fn(n, 0, bank)
                fn(n + 1, 1, bank)

            def scores(L, hd):
                b, r, a = hd % 2, hd % 2 * HD, hd // 2
                if hd >= 2:
                    pe.wait_ge(s_max, HEADS * L + hd - 1)
                for t in range(TT):
                    last = nc.tensor.matmul(ps[:, 4 + b, P * t:P * t + (t + 1) * P], qT[r:r + HD, a, t * P:(t + 1) * P],
                                            kT[r:r + HD, a, 0:(t + 1) * P], start=True, stop=True)
                last.then_inc(s_ps, 1)

            def probs_T(L, hd):
                b, pr = hd % 2, probs[hd % 3]
                pe.wait_ge(s_norm, HEADS * L + hd + 1)
                if hd >= 2:
                    pe.wait_ge(pT_cp, HEADS * L + hd - 1)
                for c in range(3):
                    last = nc.tensor.transpose(ps[:, 6 + b, c * P:(c + 1) * P], pr[:, c * P:(c + 1) * P], ident)
                last.then_inc(pT_ps, 1)

            def weigh(L, hd):
                b, r, a = hd % 2, hd % 2 * HD, hd // 2
                pe.wait_ge(pT_cp, HEADS * L + hd + 1)
                if a >= 2:
                    pe.wait_ge(att_lo, 4 * L + a - 1)
                o = ps[r:r + HD, a % 2, a // 2 * SEQ:(a // 2 + 1) * SEQ]
                nc.tensor.matmul(o, v_sb[:, 0, hd * HD:(hd + 1) * HD], probsT[:, b, 0:SEQ], start=True, stop=True)
                nc.tensor.matmul(o[:, P:SEQ], v_sb[:, 1, hd * HD:(hd + 1) * HD], probsT[:, b, SEQ:3 * P], start=False,
                                 stop=True, skip_group_check=True).then_inc(att_ps, 1)

            def w_out(n, j):
                unit_ready(n)
                for kk in range(2):
                    k = 2 * j + kk
                    for t in range(TT):
                        for half in range(2):
                            for xp, wp in PASSES:
                                last = nc.tensor.matmul(ps[:, 2 * t + half, :], (mixT_hi, mixT_lo)[xp][:, k, t * P:(t + 1) * P],
                                                        w(n, wp, kk * D + half * 512, kk * D + (half + 1) * 512),
                                                        start=(k == 0 and xp == wp), stop=(k == KT - 1 and wp == 1))
                last.then_inc(unit_used, 1)

            def mixer(L):
                n0 = BASE_MIX[L]
                norm(2 * L)
                pe.wait_ge(hnT_lo, 4 * L + 2)
                pe.wait_ge(wz_l, L + 1)
                narrow(ps[0:RANK, 7, 0:SEQ], wz_hi, wz_lo).then_inc(zT_ps, 1)
                w_in_block(tokens_first, n0, 0)
                w_in_block(tokens_first, n0 + 2, 2)
                pe.wait_ge(zT_cp, L + 1)
                for t in range(TT):
                    last = nc.tensor.matmul(ps[:, 6, SEQ + t * P:SEQ + (t + 1) * P], zT[:, t * P:(t + 1) * P], wg[:, :],
                                            start=True, stop=True)
                last.then_inc(zl_ps, 1)
                pe.wait_ge(rope_mul, 2 * L + 1)
                w_in_block(tokens_first, n0 + 4, 0)
                pe.wait_ge(loga_done, L + 1)
                nc.tensor.matmul(ps[:, 7, SEQ:2 * SEQ], log_a[:, 0, :], tri_ones, start=True, stop=True)
                nc.tensor.matmul(ps[:, 7, SEQ + P:2 * SEQ], log_a[:, 1, :], tri, start=False, stop=True,
                                 skip_group_check=True).then_inc(b_ps, 1)
                pe.wait_ge(rope_mul, 2 * L + 2)
                w_in_block(features_first, n0 + 6, 2)
                for n, (rot, bank, done) in enumerate(((rot_q, 4, qT_ps), (rot_k, 6, kT_ps))):
                    pe.wait_ge(rope_add, 2 * L + n + 1)
                    if n:
                        pe.wait_ge(b_cp, L + 1)
                    for a in range(4):
                        for t in range(TT):
                            last = nc.tensor.transpose(ps[:, bank + a // 2, a % 2 * SEQ + t * P:a % 2 * SEQ + (t + 1) * P],
                                                       rot[:, t, a * P:(a + 1) * P], ident)
                    last.then_inc(done, 1)
                pe.wait_ge(v_cp, L + 1)
                w_in_block(tokens_first, n0 + 8, 0)
                pe.wait_ge(qT_cp, L + 1)
                pe.wait_ge(kT_cp, L + 1)
                for step in range(HEADS + 3):
                    if step < HEADS:
                        scores(L, step)
                    if step == 1:
                        pe.wait_ge(f_cp, 3 * (L + 1))
                        features_first(n0 + 10, 0, 2)
                    if step == 3:
                        features_first(n0 + 11, 1, 2)
                    if 2 <= step <= HEADS + 1:
                        probs_T(L, step - 2)
                    if step >= 3:
                        if step == 3:
                            pe.wait_ge(t_cp, 2 * (L + 1))
                        weigh(L, step - 3)
                for n in range(9):
                    if n == 0:
                        pe.wait_ge(pT_cp, HEADS * (L + 1))
                        pe.wait_ge(f_cp, 3 * L + 2)
                    if n == 1:
                        pe.wait_ge(att_lo, 4 * (L + 1))
                        pe.wait_ge(conv_out, L + 1)
                        pe.wait_ge(qe_done, L + 1)
                        pe.wait_ge(ke_done, L + 1)
                    if n >= 2:
                        pe.wait_ge(lv_cp, 9 * L + n - 1)
                    for hh in range(GH):
                        r = slice(GK * hh, GK * (hh + 1))
                        for t in range(1 if n == 8 else TT):
                            if n == 0:
                                lhsT, rhs = g_qk[r, 1, t * P:(t + 1) * P], g_qk[r, 0, t * P:(t + 1) * P]
                            elif n == 8:
                                lhsT, rhs = ke[r, 0, 0:P], qe[r, 0, P:2 * P]
                            else:
                                lhsT, rhs = ke[r, n, t * P:(t + 1) * P], qe[r, n, t * P:(t + 1) * P]
                            last = nc.tensor.matmul(ps[:, 4 - n % 2 * 4 + hh, t * P:(t + 1) * P], lhsT, rhs, start=True, stop=True,
                                                    tile_position=(GK * hh, 0))
                    last.then_inc(lv_ps, 1)
                pe.wait_ge(lv_cp, 9 * L + 8)
                w_out(n0 + 12, 0)
                pe.wait_ge(lv_cp, 9 * (L + 1))
                for t in range(TT):
                    for hh in range(GH):
                        o = ps[:, 4, t * SEQ + hh * GV:t * SEQ + (hh + 1) * GV]
                        last = nc.tensor.matmul(o, gat[:, hh, t, :], gvo[:, t, hh * GV:(hh + 1) * GV], start=True, stop=(t == 0))
                        if t == 1:
                            last = nc.tensor.matmul(o, gax[:, hh, :], gvo[:, 0, hh * GV:(hh + 1) * GV], start=False, stop=True)
                last.then_inc(o_ps, 1)
                w_out(n0 + 13, 1)
                pe.wait_ge(o_done, L + 1)
                for f in range(2):
                    for t in range(TT):
                        last = nc.tensor.transpose(ps[:, 5 + f, t * P:(t + 1) * P], cc[:, t, f * P:(f + 1) * P], ident)
                last.then_inc(oT_ps, 1)
                pe.wait_ge(conv_lo, L + 1)
                w_out(n0 + 14, 2)
                pe.wait_ge(oT_lo, 2 * (L + 1))
                w_out(n0 + 15, 3)

            def gate_up(S, tiles, B, par, n, d, wait_mul=True, slots_of=None):
                for half in range(2):
                    if slots_of is not None:
                        pe.wait_ge(ga_lo, slots_of * 2 + (half + 1))
                    unit_ready(n + half, d)
                    for t in range(tiles):
                        s = t if tiles == 2 else par
                        if half == 0 and wait_mul:
                            pe.wait_ge(S.mul, (B - 1) * 2 + (t + 1) if tiles == 2 else B - 1)
                        for kk in range(4):
                            k = 4 * half + kk
                            for xp, wp in PASSES:
                                last = nc.tensor.matmul(ps[:, 4 + s, :], (xT_hi, xT_lo)[xp][:, k, t * P:(t + 1) * P],
                                                        w((n + half), wp, kk * 512, (kk + 1) * 512),
                                                        start=(k == 0 and xp == wp), stop=(k == KT - 1 and wp == 1))
                        if half == 1 and t < tiles - 1:
                            last.then_inc(S.gu_first, 1)
                    last.then_inc(unit_used, 1)
                    if half == 0:
                        yield

            def act_T(S, tiles, B, par):
                pe.wait_ge(S.mul, (B + 1) * tiles)
                for t in range(tiles):
                    s = t if tiles == 2 else par
                    for f in range(2):
                        c = t * FB + f * P
                        last = nc.tensor.transpose(ps[:, 6 + par, c:c + P], act_x[:, s, f * P:(f + 1) * P], ident)
                last.then_inc(S.aT_ps, 1)

            def down(S, tiles, B, par, n, d, first, final):
                unit_ready(n, d)
                pe.wait_ge(S.aT_lo, B + 1)
                for f in range(2):
                    for t in range(tiles):
                        s = t if tiles == 2 else par
                        for half in range(2):
                            for xp, wp in PASSES:
                                last = nc.tensor.matmul(ps[:, 2 * t + half, :], (aT_hi, aT_lo)[xp][:, s, f, :],
                                                        w(n, wp, f * D + half * 512, f * D + (half + 1) * 512),
                                                        start=(first and f == 0 and xp == wp),
                                                        stop=(final and f == 1 and wp == 1), skip_group_check=True)
                last.then_inc(unit_used, 1)

            def step(S, tiles, B, p, n, d, first, final=False, wait_mul=True, gather_for=None):
                gu = gate_up(S, tiles, B + 1, 1 - p, n, d, wait_mul)
                next(gu)
                if gather_for is not None:
                    gather(gather_for)
                act_T(S, tiles, B, p)
                for _ in gu:
                    pass
                down(S, tiles, B, p, n + 2, d, first, final)

            def gather(e):
                pe.wait_ge(disp_done, e + 1)
                for half in range(2):
                    for t in range(TT):
                        for part, src in enumerate((tok_hi, tok_lo)):
                            last = nc.tensor.matmul(ps[:, 2 + half, :], disp[:, t, :], src[:, t, half * 512:(half + 1) * 512],
                                                    start=(t + part == 0), stop=(t + part == TT))
                last.then_inc(ga_ps, 1)

            def gather_T(e):
                pe.wait_ge(ga_act, e + 1)
                pe.wait_ge(ga_dve, e + 1)
                for half in range(2):
                    for kk in range(4):
                        last = nc.tensor.transpose(ps[:, 2 + half, kk * P:(kk + 1) * P], gath[:, half, kk * P:(kk + 1) * P],
                                                   ident)
                    last.then_inc(gaT_ps, 1)

            def slot_tables(e, col):
                for t in range(TT):
                    nc.tensor.transpose(ps[:, 6, SEQ + t * P:SEQ + (t + 1) * P], disp[:, t, :].bitcast(F32), ident)
                for t in range(TT):
                    c = comb[:, t, col:col + 1] if isinstance(col, int) else comb[:, t, bass.ds(col, 1)]
                    last = nc.tensor.matmul(ps[:, 7, SEQ:SEQ + 1], disp[:, t, :].bitcast(F32), c, start=(t == 0),
                                            stop=(t == TT - 1))
                last.then_inc(slot_ps, 1)

            def expert_start(e, col, n, d):
                gather(e)
                slot_tables(e, col)
                gather_T(e)
                for _ in gate_up(fm, 1, e * EXP_BLOCKS, 0, n, d, wait_mul=False, slots_of=e):
                    pass

            def expert_steps(e, n, d, y_wait, follow):
                if y_wait:
                    pe.wait_ge(y_free, e + 1)
                pe.wait_ge(slot_cp, 3 * e + 3)
                B0 = e * EXP_BLOCKS
                step(fm, 1, B0, 0, n + 2, d, True, wait_mul=False)
                step(fm, 1, B0 + 1, 1, n + 5, d, False)
                with pe.Fori(1, (EXP_BLOCKS - 2) // 2) as i:
                    for p in range(2):
                        step(fm, 1, B0 + i * 2 + p, p, n + 2 + 3 * p, d + i, False)
                step(fm, 1, B0 + (EXP_BLOCKS - 2), 0, n + EXP_UNITS - 4, d, False, gather_for=e + 1 if follow else None)

            def expert_last(e, n, d, follow):
                B = e * EXP_BLOCKS + (EXP_BLOCKS - 1)
                act_T(fm, 1, B, 1)
                if follow:
                    gather_T(e + 1)
                down(fm, 1, B, 1, n + EXP_UNITS - 1, d, False, True)

            pe.wait_ge(in_cst, 16)
            mixer(0)
            n0 = BASE_DENSE
            norm(1)
            pe.wait_ge(hnT_lo, 4)
            for _ in gate_up(fd, 2, 0, 0, n0, 0, wait_mul=False):
                pass
            step(fd, 2, 0, 0, n0 + 2, 0, True)
            step(fd, 2, 1, 1, n0 + 5, 0, False)
            with pe.Fori(1, (DENSE_BLOCKS - 1) // 2) as i:
                for p in range(2):
                    step(fd, 2, i * 2 + p, p, n0 + 2 + 3 * p, i, False)
            act_T(fd, 2, DENSE_BLOCKS - 1, 0)
            down(fd, 2, DENSE_BLOCKS - 1, 0, n0 + DENSE_UNITS - 1, 0, False, True)
            mixer(1)
            norm(3)
            pe.wait_ge(hnT_lo, 8)
            pe.wait_ge(rt_l, 1)
            narrow(ps[0:N_EXP, 7, 0:SEQ], rt_hi, rt_lo).then_inc(lgT_ps, 1)
            pe.wait_ge(lgT_cp, 1)
            for t in range(TT):
                last = nc.tensor.transpose(ps[:, 6, t * N_EXP:(t + 1) * N_EXP], lgT[:, t * P:(t + 1) * P], ident[0:N_EXP, 0:N_EXP])
            last.then_inc(lg_ps, 1)
            pe.wait_ge(chosen_done, 1)
            nc.tensor.matmul(ps[:, 7, 0:8], stri, chosen[:, 0, :], start=True, stop=True)
            nc.tensor.matmul(ps[:, 7, 8:16], ones, chosen[:, 0, :], start=True, stop=False)
            nc.tensor.matmul(ps[:, 7, 8:16], stri, chosen[:, 1, :], start=False, stop=True)
            nc.tensor.matmul(ps[:, 7, 16:24], ones, chosen[:, 0, :], start=True, stop=False)
            nc.tensor.matmul(ps[:, 7, 16:24], ones, chosen[:, 1, :], start=False, stop=True).then_inc(pos_ps, 1)
            pe.wait_ge(tok_l, 1)
            expert_start(0, 0, BASE_MOE, 0)
            with pe.Fori(0, N_EXP - 1) as e:
                d = e * (EXP_UNITS // RAW)
                expert_steps(e, BASE_MOE, d, True, True)
                expert_last(e, BASE_MOE, d, True)
                slot_tables(e + 1, e + 1)
                for _ in gate_up(fm, 1, (e + 1) * EXP_BLOCKS, 0, BASE_MOE, d + EXP_UNITS // RAW, wait_mul=False,
                                 slots_of=e + 1):
                    pass
            last_e = N_EXP - 1
            expert_steps(last_e, BASE_MOE, last_e * (EXP_UNITS // RAW), True, False)
            expert_last(last_e, BASE_MOE, last_e * (EXP_UNITS // RAW), False)
            pe.wait_ge(y_free, N_EXP + 1)
            pe.wait_ge(slot_cp, 3 * N_EXP)
            for t in range(TT):
                for half in range(2):
                    for e in range(N_EXP):
                        last = nc.tensor.matmul(ps[:, 2 + 2 * t + half, :], slotT[:, e, t * P:(t + 1) * P],
                                                ys[:, e, half * 512:(half + 1) * 512], start=(e == 0), stop=(e == N_EXP - 1))
                    last.then_inc(sc_ps, 1)
            pe.wait_ge(route_done, 1)
            n_over = pe.value_load(over_i[0:1, 0:1], min_val=0, max_val=3)
            with pe.If(n_over > 0):
                with pe.Fori(0, n_over) as k:
                    e = k + N_EXP
                    ex = pe.value_load(over_i[0:1, bass.ds(k + 1, 1)], min_val=0, max_val=N_EXP - 1)
                    d = k * (EXP_UNITS // RAW) + N_EXP * (EXP_UNITS // RAW)
                    pe.wait_ge(sc_add, k + 1)
                    expert_start(e, ex, BASE_MOE, d)
                    expert_steps(e, BASE_MOE, d, False, False)
                    expert_last(e, BASE_MOE, d, False)
                    pe.wait_ge(y_free, e + 2)
                    for t in range(TT):
                        for half in range(2):
                            last = nc.tensor.matmul(ps[:, 2 + 2 * t + half, :], slotT[:, 0, t * P:(t + 1) * P],
                                                    ys[:, 0, half * 512:(half + 1) * 512], start=True, stop=True)
                    last.then_inc(ov_ps, 1)


def lay_out(inp):
    a = {k: np.asarray(v) for k, v in inp.items()}

    def by_unit(m, width):
        rows = UNIT // width
        k = m.shape[0] // (P * rows)
        u = m.reshape(k, rows, P, m.shape[1] // width, width).transpose(3, 0, 2, 1, 4)
        return u.reshape(-1, P, UNIT)

    def ffn(g, u, d):
        nb = g.shape[1] // FB
        gu = np.stack([g.reshape(D, nb, FB), u.reshape(D, nb, FB)], 2).reshape(D, nb * 2 * FB)
        gu = by_unit(gu, 2 * FB).reshape(nb, 2, P, UNIT)
        dn = by_unit(d, D)
        out = [gu[0]]
        for b in range(1, nb):
            out += [gu[b], dn[b - 1:b]]
        return out + [dn[nb - 1:nb]]

    order = ((0, 1536), (2304, 2560), (1792, 2048), (2560, 3072), (2048, 2304), (1536, 1792))
    units = []
    for L in range(DEPTH):
        w_in = np.concatenate([a["w_in"][L][:, s:e] for s, e in order], 1)
        units += [by_unit(w_in, 512), by_unit(a["w_out"][L], D)]
        if L % 2 == 0:
            units += ffn(a["dense_w_gate"][L // 2], a["dense_w_up"][L // 2], a["dense_w_down"][L // 2])
        else:
            for e in range(N_EXP):
                units += ffn(a["exp_w_gate"][L // 2, e], a["exp_w_up"][L // 2, e], a["exp_w_down"][L // 2, e])
    consts, masks = shape_constants()
    z = a["w_in"][:, :, 3072:].reshape(DEPTH, KT, P, RANK).transpose(0, 2, 1, 3)
    gate = np.concatenate([a["w_gate_lr"], a["b_gate_lr"][:, None, :]], 1)
    conv = a["conv_w"].reshape(DEPTH, 3, 2, P).transpose(3, 0, 2, 1)
    gla_gain = a["gla_norm"].reshape(DEPTH, 2, P).transpose(2, 0, 1)
    gains = np.stack([a["mix_norm"][0], a["ffn_norm"][0], a["mix_norm"][1], a["ffn_norm"][1], a["final_norm"]])
    router = a["router"][0].reshape(KT, P, N_EXP).transpose(1, 0, 2)
    return {"x": a["x"], "stream": np.concatenate(units, 0), "w_z": z, "w_gate": gate, "conv_w": conv, "gla_gain": gla_gain,
            "gains": gains, "router": router, "consts": consts, "masks": masks}


def kernel(**inputs):
    import concourse.bacc as bacc
    from concourse.bass_utils import run_bass_kernel_spmd

    nc = bacc.Bacc("TRN2", target_bir_lowering=False, num_devices=1)
    arrays, args = {}, []
    for name, v in lay_out(inputs).items():
        v = np.ascontiguousarray(v)
        arrays[f"in_{name}"] = v
        args.append(nc.dram_tensor(f"in_{name}", v.shape, mybir.dt.from_np(v.dtype), kind="ExternalInput").ap())
    out = nc.dram_tensor("out_0", (1, SEQ, D), F32, kind="ExternalOutput").ap()
    build(nc, *args, out)
    r = run_bass_kernel_spmd(nc, [arrays], core_ids=[0])
    return r.results[0]["out_0"]
```

```python
from contextlib import ExitStack

import numpy as np

import concourse.bass as bass
from concourse import mybir

F32 = mybir.dt.float32
F32R = mybir.dt.float32r
I32 = mybir.dt.int32
U32 = mybir.dt.uint32
U8 = mybir.dt.uint8
ALU = mybir.AluOpType
ACT = mybir.ActivationFunctionType
AX_X = mybir.AxisListType.X

P = 128
D = 1024
SEQ = 256
TT = SEQ // P
KT = D // P
DEPTH = 2
EPS = 1e-6
NEG = -1e30
HEADS = 8
HD = 64
BRANCHES = ((128, 1), (512, 4), (2048, 16))
ROPE_THETA = 10000.0
GH = 4
GK = 32
GV = 64
TAU = 16.0
RANK = 16
F_DENSE = 2816
N_EXP = 8
F_EXP = 3584
FB = 256

UNIT = 2048
RAW = 6
SPLIT = 3
MIX_UNITS = 16
DENSE_BLOCKS = F_DENSE // FB
EXP_BLOCKS = F_EXP // FB
DENSE_UNITS = 3 * DENSE_BLOCKS
EXP_UNITS = 3 * EXP_BLOCKS
BASE_MIX = (0, MIX_UNITS + DENSE_UNITS)
BASE_DENSE = MIX_UNITS
BASE_MOE = 2 * MIX_UNITS + DENSE_UNITS
ALL_UNITS = BASE_MOE + N_EXP * EXP_UNITS
assert DENSE_BLOCKS % 2 == 1 and EXP_BLOCKS % 2 == 0 and EXP_UNITS % RAW == 0

RSQRT_BITS = float(0x5F3759DF)
LEVELS = (128, 64, 32, 16, 8, 4, 2, 1)

C_ID, C_TRI, C_ONES, C_STRI, C_IOTA = 0, 128, 256, 384, 512
C_LNC = 640
C_ROPE = C_LNC + 3 * P
C_E8 = C_ROPE + 2 * TT * HD
C_ALL = C_E8 + 8


def shape_constants():
    c = np.zeros((P, C_ALL), np.float32)
    i = np.arange(P)
    c[:, C_ID:C_ID + P] = np.eye(P)
    c[:, C_TRI:C_TRI + P] = i[:, None] <= i[None, :]
    c[:, C_ONES:C_ONES + P] = 1.0
    c[:, C_STRI:C_STRI + P] = i[:, None] < i[None, :]
    c[:, C_IOTA:C_IOTA + P] = i[None, :]
    t = np.arange(SEQ)
    diff = t[:, None] - t[None, :]
    count = np.zeros((SEQ, SEQ))
    for window, step in BRANCHES:
        count += (diff >= 0) & (diff % step == 0) & (diff // step <= window // step)
    lnc = np.where(count > 0, np.log(np.maximum(count, 1)), NEG)
    c[:, C_LNC:C_LNC + P] = lnc[:P, :P]
    c[:, C_LNC + P:C_LNC + 3 * P] = lnc[P:]
    inv = (1.0 / (np.float32(ROPE_THETA) ** (np.arange(0, HD, 2, dtype=np.float32) / np.float32(HD)))).astype(np.float32)
    ang = (t.astype(np.float32)[:, None] * inv[None, :]).astype(np.float32).astype(np.float64)
    cos = np.concatenate([np.cos(ang), np.cos(ang)], 1)
    sin = np.concatenate([-np.sin(ang), np.sin(ang)], 1)
    rope = np.stack([cos, sin])
    c[:, C_ROPE:C_E8] = rope.reshape(2, TT, P, HD).transpose(2, 0, 1, 3).reshape(P, -1)
    c[:, C_E8:C_E8 + 8] = np.arange(8)
    m = np.zeros((P, len(LEVELS), P), np.float32)
    for n, half in enumerate(LEVELS[1:]):
        same = i[:, None] // (2 * half) == i[None, :] // (2 * half)
        m[:, n] = same & (i[:, None] % (2 * half) < half) & (i[None, :] % (2 * half) >= half)
    m[:, -1] = np.eye(P)
    return c, m


def build(nc, x, stream, w_z, w_gate, conv_w, gla_gain, gains, router, consts, masks, out):
    with ExitStack() as ctx:
        def sb(name, shape, dt=F32):
            return ctx.enter_context(nc.sbuf_tensor(name, shape, dt))

        def sem(name):
            return ctx.enter_context(nc.semaphore(name))

        ps = ctx.enter_context(nc.psum_tensor("ps", [P, 8, 512], F32))

        raw = sb("raw", [P, RAW, UNIT])
        w_hi = sb("w_hi", [P, SPLIT, UNIT], F32R)
        w_lo = sb("w_lo", [P, SPLIT, UNIT], F32R)
        h = sb("h", [P, TT, D])
        xT_hi = sb("xT_hi", [P, KT, SEQ], F32R)
        xT_lo = sb("xT_lo", [P, KT, SEQ], F32R)
        mix_hi = sb("mix_hi", [P, KT * SEQ], F32R)
        mix_lo = sb("mix_lo", [P, KT * SEQ], F32R)
        mixT_hi = mix_hi[:, :].rearrange("p (k t) -> p k t", k=KT)
        mixT_lo = mix_lo[:, :].rearrange("p (k t) -> p k t", k=KT)
        tok_hi = mix_hi[:, :].rearrange("p (t d) -> p t d", t=TT)
        tok_lo = mix_lo[:, :].rearrange("p (t d) -> p t d", t=TT)
        big = sb("big", [P, 8 * D])
        work = sb("work", [P, 2 * D])
        small = sb("small", [P, 2 * D])
        cst = sb("cst", [P, C_ALL])
        msk = sb("msk", [P, len(LEVELS), P], U8)
        gain = sb("gain", [P, D])
        gate_x = sb("gate_x", [P, 2, FB])
        act_x = sb("act_x", [P, 2, FB])
        aT_hi = sb("aT_hi", [P, 2, 2, P], F32R)
        aT_lo = sb("aT_lo", [P, 2, 2, P], F32R)
        wz = sb("wz", [P, KT, RANK])
        wz_hi = sb("wz_hi", [P, KT, RANK], F32R)
        wz_lo = sb("wz_lo", [P, KT, RANK], F32R)
        wg = sb("wg", [RANK + 1, P])
        zT = sb("zT", [RANK + 1, SEQ])
        cw = sb("cw", [P, DEPTH, 2, 3])
        gg = sb("gg", [P, DEPTH, 2])
        ss = sb("ss", [P, TT])
        rs = sb("rs", [P, 8])
        nwt = sb("nwt", [P, 8])
        mx = sb("mx", [P, 2, 2])
        nmx = sb("nmx", [P, 2, 2])
        den = sb("den", [P, 2, 2])
        rden = sb("rden", [P, 2, 2])
        gss = sb("gss", [P, 8])
        ix8 = sb("ix8", [P, TT, 8], U32)
        zero8 = sb("zero8", [P, 8])
        over_f = sb("over_f", [P, 4])
        over_i = sb("over_i", [P, 4], I32)
        rt = sb("rt", [P, KT, 8])
        rt_hi = sb("rt_hi", [P, KT, 8], F32R)
        rt_lo = sb("rt_lo", [P, KT, 8], F32R)
        w_slot = sb("w_slot", [P, 1])
        disp = sb("disp", [P, TT, P], F32R)

        ident = cst[:, C_ID:C_ID + P]
        tri = cst[:, C_TRI:C_TRI + P]
        tri_ones = cst[:, C_TRI:C_TRI + 2 * P]
        ones = cst[:, C_ONES:C_ONES + P]
        stri = cst[:, C_STRI:C_STRI + P]
        iota = cst[:, C_IOTA:C_IOTA + P]
        lnc = cst[:, C_LNC:C_LNC + 3 * P]
        rope = cst[:, C_ROPE:C_E8].rearrange("p (a t d) -> p a t d", a=2, t=TT)
        iota8 = cst[:, C_E8:C_E8 + 8]

        hn = big[:, 0:2048].rearrange("p (t d) -> p t d", t=TT)
        rope_t1 = big[:, 0:1024].rearrange("p (t n) -> p t n", t=TT)
        rope_t2 = big[:, 1024:2048].rearrange("p (t n) -> p t n", t=TT)
        ke = big[:, 0:2048].rearrange("p (l t) -> p l t", l=8)
        rot_q = big[:, 2048:3072].rearrange("p (t n) -> p t n", t=TT)
        rot_k = big[:, 3072:4096].rearrange("p (t n) -> p t n", t=TT)
        dec = big[:, 2048:4096].rearrange("p (l t) -> p l t", l=8)
        qT = big[:, 4096:5120].rearrange("p (a t) -> p a t", a=4)
        kT = big[:, 5120:6144].rearrange("p (a t) -> p a t", a=4)
        gat = big[:, 4096:5120].rearrange("p (h t q) -> p h t q", h=GH, t=TT)
        gax = big[:, 5120:5632].rearrange("p (h q) -> p h q", h=GH)
        osq = big[:, 5632:6144]
        v_sb = big[:, 6144:7168].rearrange("p (t n) -> p t n", t=TT)
        gvo = big[:, 7168:8192].rearrange("p (t n) -> p t n", t=TT)
        ys = big[:, 0:D]
        qe = work[:, :].rearrange("p (l t) -> p l t", l=8)
        z_abs = work[:, 0:256].rearrange("p (t f) -> p t f", t=TT)
        z_log = work[:, 256:512].rearrange("p (t f) -> p t f", t=TT)
        log_a = work[:, 512:768].rearrange("p (t f) -> p t f", t=TT)
        slotT = work[:, 0:SEQ]
        probs = (small[:, 0:3 * P], small[:, 3 * P:6 * P], gain[:, 0:3 * P])
        probsT = small[:, 768:1536].rearrange("p (b n) -> p b n", b=2)
        cc = small[:, 1536:2048].rearrange("p (f t) -> p f t", f=2)
        g_qk = act_x[:, :, :]
        bcum = work[:, 768:1024]
        cu = gate_x[:, :, :]
        cy = gain[:, 512:1024].rearrange("p (f t) -> p f t", f=2)

        gath = small[:, D:2 * D].rearrange("p (b n) -> p b n", b=2)
        lg = small[:, 0:16].rearrange("p (t e) -> p t e", t=TT)
        mx8 = small[:, 16:32].rearrange("p (t e) -> p t e", t=TT)
        ixf = small[:, 32:36].rearrange("p (t e) -> p t e", t=TT)
        top1 = small[:, 36:52].rearrange("p (t e) -> p t e", t=TT)
        top2 = small[:, 52:68].rearrange("p (t e) -> p t e", t=TT)
        chosen = small[:, 68:84].rearrange("p (t e) -> p t e", t=TT)
        comb = small[:, 84:100].rearrange("p (t e) -> p t e", t=TT)
        slot = small[:, 100:116].rearrange("p (t e) -> p t e", t=TT)
        tw = small[:, 116:124].rearrange("p (t e) -> p t e", t=TT)
        flag = small[:, 124:132]
        cum = small[:, 132:140]
        sel = small[:, 140:148]
        lgT = small[0:N_EXP, 256:512]

        in_x, in_gain0, in_cst, in_mask, in_small, in_gain, in_wz = (sem(n) for n in ("in_x", "in_gain0", "in_cst", "in_mask", "in_small", "in_gain", "in_wz"))
        landed = [sem(f"landed{i}") for i in range(RAW)]
        hi_done, lo_done, unit_used = sem("hi_done"), sem("lo_done"), sem("unit_used")
        dve_chain, act_chain, pool_chain = sem("dve_chain"), sem("act_chain"), sem("pool_chain")
        sq_act, hn_done, hnT_ps, hnT_hi, hnT_lo = (sem(n) for n in ("sq_act", "hn_done", "hnT_ps", "hnT_hi", "hnT_lo"))
        gain_used, first_tile, res_done = sem("gain_used"), sem("first_tile"), sem("res_done")
        wz_h, wz_l, zT_ps, zT_cp, zl_ps = (sem(n) for n in ("wz_h", "wz_l", "zT_ps", "zT_cp", "zl_ps"))
        zlog_done, loga_done, b_ps, b_cp = (sem(n) for n in ("zlog_done", "loga_done", "b_ps", "b_cp"))
        rope_mul, rope_add, qT_ps, kT_ps, qT_cp, kT_cp = (sem(n) for n in ("rope_mul", "rope_add", "qT_ps", "kT_ps", "qT_cp", "kT_cp"))
        v_cp, f_cp, t_cp = sem("v_cp"), sem("f_cp"), sem("t_cp")
        s_ps, s_max, s_exp, s_norm, pT_ps, pT_cp, att_ps, att_hi, att_lo = (
            sem(n) for n in ("s_ps", "s_max", "s_exp", "s_norm", "pT_ps", "pT_cp", "att_ps", "att_hi", "att_lo"))
        conv_u, conv_y, conv_out, conv_hi, conv_lo = (sem(n) for n in ("conv_u", "conv_y", "conv_out", "conv_hi", "conv_lo"))
        dec_sub, dec_exp, qe_done, ke_done, lv_ps, lv_cp, o_ps, o_sq, o_done, oT_ps, oT_hi, oT_lo = (
            sem(n) for n in ("dec_sub", "dec_exp", "qe_done", "ke_done", "lv_ps", "lv_cp", "o_ps", "o_sq", "o_done",
                             "oT_ps", "oT_hi", "oT_lo"))

        class FfnSems:
            def __init__(self, name):
                self.gu_first = sem(f"{name}_gu_first")
                self.silu = sem(f"{name}_silu")
                self.mul = sem(f"{name}_mul")
                self.aT_ps = sem(f"{name}_aT_ps")
                self.aT_hi = sem(f"{name}_aT_hi")
                self.aT_lo = sem(f"{name}_aT_lo")

        fd, fm = FfnSems("dense"), FfnSems("moe")
        rt_h, rt_l, lgT_ps, lgT_cp, lg_ps, lg_exp_in, lg_exp, chosen_done, pos_ps, route_done, tok_h, tok_l = (
            sem(n) for n in ("rt_h", "rt_l", "lgT_ps", "lgT_cp", "lg_ps", "lg_exp_in", "lg_exp", "chosen_done", "pos_ps", "route_done", "tok_h", "tok_l"))
        disp_done, ga_ps, ga_act, ga_dve, gaT_ps, ga_hi, ga_lo, slot_ps, slot_cp, y_free = (
            sem(n) for n in ("disp_done", "ga_ps", "ga_act", "ga_dve", "gaT_ps", "ga_hi", "ga_lo", "slot_ps", "slot_cp", "y_free"))
        sc_ps, sc_add = sem("sc_ps"), sem("sc_add")
        fin_done, out_sem = sem("fin_done"), sem("out_sem")

        def load_unit(sp, n, d=0, row=None):
            if n >= RAW:
                sp.wait_ge(lo_done, d * RAW + (n - RAW + 1))
            row = d * RAW + n if row is None else row
            src = stream[row] if isinstance(row, int) else stream[bass.ds(row, 1)].rearrange("a p c -> (a p) c")
            sp.dma_start(raw[:, n % RAW, :], src).then_inc(landed[n % RAW], 16)

        def hi_unit(act, n, d=0):
            act.wait_ge(landed[n % RAW], (d + (n // RAW + 1)) * 16)
            if n >= SPLIT:
                act.wait_ge(unit_used, d * RAW + (n - SPLIT + 1))
            nc.scalar.activation(w_hi[:, n % SPLIT, :], raw[:, n % RAW, :], ACT.Copy).then_inc(hi_done, 1)

        def lo_unit(dve, n, d=0):
            dve.wait_ge(hi_done, d * RAW + (n + 1))
            nc.vector.tensor_tensor(w_lo[:, n % SPLIT, :], raw[:, n % RAW, :], w_hi[:, n % SPLIT, :].bitcast(F32),
                                    ALU.subtract).then_inc(lo_done, 1)

        PASSES = ((0, 0), (1, 0), (0, 1))
        ALL_EXP = N_EXP * EXP_UNITS // RAW

        def w(n, part, a, b):
            return (w_hi, w_lo)[part][:, n % SPLIT, a:b]

        def used(eng, n, d=0):
            eng.wait_ge(unit_used, d * RAW + n)

        block = ctx.enter_context(nc.Block())

        @block.sync
        def _(sp):
            sp.dma_start(h[:, :, :], x.rearrange("a (t p) d -> p (a t) d", p=P)).then_inc(in_x, 16)
            sp.dma_start(gain[:, :], gains[0:1, :].to_broadcast([P, D])).then_inc(in_gain0, 16)
            sp.dma_start(cst[:, :], consts).then_inc(in_cst, 16)
            for n in range(RAW):
                load_unit(sp, n)
            for n in range(RAW, MIX_UNITS):
                load_unit(sp, n)
            with sp.Fori(0, DENSE_UNITS // RAW) as i:
                for j in range(RAW):
                    load_unit(sp, BASE_DENSE + j, i)
            for n in range(BASE_MIX[1] - DENSE_UNITS % RAW, BASE_MOE):
                load_unit(sp, n)
            with sp.Fori(0, N_EXP * EXP_UNITS // RAW) as i:
                for j in range(RAW):
                    load_unit(sp, BASE_MOE + j, i)
            sp.wait_ge(route_done, 1)
            n_over = sp.value_load(over_i[0:1, 0:1], min_val=0, max_val=3)
            with sp.If(n_over > 0):
                with sp.Fori(0, n_over) as k:
                    e = sp.value_load(over_i[0:1, bass.ds(k + 1, 1)], min_val=0, max_val=N_EXP - 1)
                    with sp.Fori(0, EXP_UNITS // RAW) as i:
                        for j in range(RAW):
                            load_unit(sp, BASE_MOE + j, k * (EXP_UNITS // RAW) + i + ALL_EXP,
                                      row=e * EXP_UNITS + i * RAW + (BASE_MOE + j))
            for t in range(TT):
                sp.wait_ge(fin_done, t + 1)
                sp.dma_start(out[0, t * P:(t + 1) * P, :], hn[:, t, :]).then_inc(out_sem, 16)
            sp.wait_ge(out_sem, 16 * TT)

        @block.gpsimd
        def _(pool):
            chain = [0]

            def link(ins):
                chain[0] += 1
                ins.then_inc(pool_chain, 1)
                pool.wait_ge(pool_chain, chain[0])

            pool.dma_start(wz[:, :, :], w_z[0]).then_inc(in_wz, 16)
            pool.dma_start(wg[:, :], w_gate[0]).then_inc(in_wz, 16)
            mask_f = big[:, 7168:8192].rearrange("p (n q) -> p n q", n=len(LEVELS))
            pool.dma_start(mask_f, masks).then_inc(in_mask, 16)
            pool.dma_start(cw[:, :, :, :], conv_w).then_inc(in_small, 16)
            pool.dma_start(gg[:, :, :], gla_gain).then_inc(in_small, 16)
            pool.dma_start(rt[:, :, :], router).then_inc(in_small, 16)
            nc.gpsimd.memset(zero8[:, :], 0.0)
            link(nc.gpsimd.memset(zT[:, :], 1.0))
            pool.wait_ge(in_mask, 16)
            link(nc.gpsimd.tensor_copy(msk[:, :, :], mask_f))
            for L in range(DEPTH):
                for n, rot in enumerate((rot_q, rot_k)):
                    pool.wait_ge(rope_mul, 2 * L + n + 1)
                    nc.gpsimd.tensor_tensor(rot[:, :, :], rope_t1[:, :, :], rope_t2[:, :, :], ALU.add).then_inc(rope_add, 1)
                pool.wait_ge(dec_exp, L + 1)
                pool.wait_ge(f_cp, 3 * L + 2)
                nc.gpsimd.tensor_tensor(ke[:, :, :], dec[:, :, :],
                                        g_qk[:, 1, :].unsqueeze(1).to_broadcast([P, 8, SEQ]), ALU.mult).then_inc(ke_done, 1)
                pool.wait_ge(pT_ps, HEADS * (L + 1))
                pool.wait_ge(conv_lo, L + 1)
                pool.dma_start(gain[:, :], gains[2 * L + 1:2 * L + 2, :].to_broadcast([P, D])).then_inc(in_gain, 16)
                pool.wait_ge(gain_used, 2 * L + 2)
                if L == 0:
                    pool.dma_start(wz[:, :, :], w_z[1]).then_inc(in_wz, 16)
                    pool.dma_start(wg[:, :], w_gate[1]).then_inc(in_wz, 16)
                pool.dma_start(gain[:, :], gains[2 * L + 2:2 * L + 3, :].to_broadcast([P, D])).then_inc(in_gain, 16)

        @block.scalar
        def _(act):
            chain = [0]

            def link(ins):
                chain[0] += 1
                ins.then_inc(act_chain, 1)
                act.wait_ge(act_chain, chain[0])

            def copy(dst, src, scale=1.0):
                return nc.scalar.activation(dst, src, ACT.Copy, scale=scale)

            def norm(i, next_unit=None):
                for t in range(TT):
                    if i == 0:
                        act.wait_ge(in_x, 16)
                    elif i < 4:
                        act.wait_ge(res_done, 2 * (i - 1) + t + 1)
                    else:
                        act.wait_ge(res_done, 2 * (i - 1) + 1)
                    nc.scalar.activation(hn[:, t, :], h[:, t, :], ACT.Square, accum_out=ss[:, t:t + 1]).then_inc(sq_act, 1)
                    if t == 0 and next_unit is not None:
                        hi_unit(act, next_unit)
                if i < 4:
                    for c in range(4):
                        if c == 2 and i == 0:
                            hi_unit(act, 0)
                            hi_unit(act, 1)
                        t, half = c // 2, c % 2
                        act.wait_ge(hnT_ps, 4 * i + c + 1)
                        copy(xT_hi[:, 4 * half:4 * half + 4, t * P:(t + 1) * P],
                             ps[:, c, :].rearrange("p (k q) -> p k q", k=4)).then_inc(hnT_hi, 1)

            def mixer(L):
                n0 = BASE_MIX[L]
                split = lambda j: hi_unit(act, n0 + j)
                if L == 0:
                    norm(0)
                act.wait_ge(in_wz, 32 * (L + 1))
                copy(wz_hi[:, :, :], wz[:, :, :]).then_inc(wz_h, 1)
                if L == 1:
                    norm(2)
                split(2)
                act.wait_ge(zT_ps, L + 1)
                if L == 0:
                    act.wait_ge(pool_chain, 1)
                copy(zT[0:RANK, :], ps[0:RANK, 7, 0:SEQ]).then_inc(zT_cp, 1)
                split(3)
                split(4)
                split(5)
                split(6)
                act.wait_ge(zl_ps, L + 1)
                link(nc.scalar.activation(z_abs[:, :, :], ps[:, 6, SEQ:2 * SEQ].rearrange("p (t f) -> p t f", t=TT), ACT.Abs))
                link(nc.scalar.activation(z_log[:, :, :], z_abs[:, :, :], ACT.Exp, scale=-1.0))
                nc.scalar.activation(z_log[:, :, :], z_log[:, :, :], ACT.Ln, bias=1.0).then_inc(zlog_done, 1)
                split(7)
                used(act, n0 + 6)
                copy(v_sb[:, :, :], ps[:, 0:2, :]).then_inc(v_cp, 1)
                split(8)
                act.wait_ge(qT_ps, L + 1)
                copy(qT[:, :, :], ps[:, 4:6, :].rearrange("p b (a t) -> p (b a) t", a=2), HD ** -0.5).then_inc(qT_cp, 1)
                used(act, n0 + 8)
                copy(g_qk[:, 0, :], ps[:, 2, 0:SEQ], GK ** -0.5).then_inc(f_cp, 1)
                copy(g_qk[:, 1, :], ps[:, 2, SEQ:2 * SEQ]).then_inc(f_cp, 1)
                copy(cc[:, :, :], ps[:, 3, :].rearrange("p (f t) -> p f t", f=2)).then_inc(f_cp, 1)
                split(9)
                split(10)
                split(11)
                act.wait_ge(dec_sub, L + 1)
                link(nc.scalar.activation(dec[:, :, :], dec[:, :, :], ACT.Abs))
                nc.scalar.activation(dec[:, :, :], dec[:, :, :], ACT.Exp, scale=-1.0 / TAU).then_inc(dec_exp, 1)
                used(act, n0 + 10)
                copy(gvo[:, :, 0:SEQ], ps[:, 0:2, 0:SEQ]).then_inc(t_cp, 1)
                nc.scalar.activation(gvo[:, :, SEQ:2 * SEQ], ps[:, 0:2, SEQ:2 * SEQ], ACT.Silu).then_inc(t_cp, 1)
                for step in range(HEADS + 4):
                    if step < HEADS:
                        b, pr = step % 2, probs[step % 3]
                        act.wait_ge(s_max, HEADS * L + step + 1)
                        nc.scalar.activation(pr[:, 0:P], pr[:, 0:P], ACT.Exp, bias=nmx[:, b, 0:1], accum_out=den[:, b, 0:1])
                        nc.scalar.activation(pr[:, P:3 * P], pr[:, P:3 * P], ACT.Exp, bias=nmx[:, b, 1:2],
                                             accum_out=den[:, b, 1:2]).then_inc(s_exp, 1)
                    if 2 <= step <= HEADS + 1:
                        hd = step - 2
                        act.wait_ge(pT_ps, HEADS * L + hd + 1)
                        if hd >= 2:
                            act.wait_ge(att_ps, HEADS * L + hd - 1)
                        copy(probsT[:, hd % 2, :], ps[:, 6 + hd % 2, 0:3 * P]).then_inc(pT_cp, 1)
                    if step in (3, 6, 8):
                        split({3: 12, 6: 13, 8: 14}[step])
                    if step >= 5 and step % 2 == 1:
                        pair = (step - 5) // 2
                        act.wait_ge(att_ps, HEADS * L + 2 * pair + 2)
                        copy(mixT_hi[:, pair, :], ps[:, pair % 2, pair // 2 * SEQ:(pair // 2 + 1) * SEQ]).then_inc(att_hi, 1)
                act.wait_ge(conv_out, L + 1)
                copy(mixT_hi[:, 4:6, :], cy[:, :, :]).then_inc(conv_hi, 1)
                act.wait_ge(o_ps, L + 1)
                nc.scalar.activation(osq, ps[:, 4, :], ACT.Square).then_inc(o_sq, 1)
                split(15)
                act.wait_ge(oT_ps, L + 1)
                for f in range(2):
                    copy(mixT_hi[:, 6 + f, :], ps[:, 5 + f, 0:SEQ], gg[:, L, f:f + 1]).then_inc(oT_hi, 1)

            def ffn_block(S, tiles, B, par, n, d=0):
                for t in range(tiles):
                    s = t if tiles == 2 else par
                    if t < tiles - 1:
                        act.wait_ge(S.gu_first, B + 1)
                    else:
                        used(act, n, d)
                    nc.scalar.activation(gate_x[:, s, :], ps[:, 4 + s, 0:FB], ACT.Silu).then_inc(S.silu, 1)

            def ffn_aT(S, tiles, B, par):
                act.wait_ge(S.aT_ps, B + 1)
                if tiles == 2:
                    copy(aT_hi[:, :, :, :], ps[:, 6 + par, :].rearrange("p (t f q) -> p t f q", t=2, f=2)).then_inc(S.aT_hi, 1)
                else:
                    copy(aT_hi[:, par, :, :], ps[:, 6 + par, 0:FB].rearrange("p (f q) -> p f q", f=2)).then_inc(S.aT_hi, 1)

            def gathered(e):
                act.wait_ge(ga_ps, e + 1)
                copy(gath[:, 0, :], ps[:, 2, :]).then_inc(ga_act, 1)

            def gather_hi(e, g):
                act.wait_ge(gaT_ps, e * 2 + (g + 1))
                copy(xT_hi[:, 4 * g:4 * g + 4, 0:P], ps[:, 2 + g, :].rearrange("p (k s) -> p k s", k=4)).then_inc(ga_hi, 1)

            def expert_start(e, n, d, split_first=True):
                gathered(e)
                for g in (0, 1):
                    gather_hi(e, g)
                    if split_first:
                        hi_unit(act, n + g, d)
                hi_unit(act, n + 2, d)
                ffn_block(fm, 1, e * EXP_BLOCKS, 0, n + 2, d)
                hi_unit(act, n + 3, d)

            def expert_middle(e, n, d):
                with act.Fori(0, (EXP_BLOCKS - 2) // 2) as i:
                    for p in range(2):
                        B = e * EXP_BLOCKS + i * 2 + p
                        m = n + 4 + 3 * p
                        hi_unit(act, m, d + i)
                        ffn_aT(fm, 1, B, p)
                        hi_unit(act, m + 1, d + i)
                        ffn_block(fm, 1, B + 1, 1 - p, m, d + i)
                        hi_unit(act, m + 2, d + i)

            def expert_end(e, n, d, follow):
                B = e * EXP_BLOCKS + (EXP_BLOCKS - 2)
                hi_unit(act, n + EXP_UNITS - 2, d)
                ffn_aT(fm, 1, B, 0)
                hi_unit(act, n + EXP_UNITS - 1, d)
                if follow:
                    gathered(e + 1)
                ffn_block(fm, 1, B + 1, 1, n + EXP_UNITS - 2, d)
                ffn_aT(fm, 1, B + 1, 1)
                if follow:
                    for g in (0, 1):
                        gather_hi(e + 1, g)
                        hi_unit(act, n + g, d + EXP_UNITS // RAW)

            def expert_out(e, n, d):
                used(act, n + EXP_UNITS, d)
                act.wait_ge(slot_cp, 3 * (e + 1))
                copy(ys, ps[:, 0:2, :].rearrange("p a d -> p (a d)"), w_slot[:, 0:1]).then_inc(y_free, 1)

            act.sem_inc(y_free, 1)
            mixer(0)
            n0 = BASE_DENSE
            hi_unit(act, n0)
            norm(1, n0 + 1)
            hi_unit(act, n0 + 2)
            ffn_block(fd, 2, 0, 0, n0 + 2)
            hi_unit(act, n0 + 3)
            with act.Fori(0, (DENSE_BLOCKS - 1) // 2) as i:
                for p in range(2):
                    B = i * 2 + p
                    m = n0 + 4 + 3 * p
                    hi_unit(act, m, i)
                    ffn_aT(fd, 2, B, p)
                    hi_unit(act, m + 1, i)
                    ffn_block(fd, 2, B + 1, 0, m, i)
                    hi_unit(act, m + 2, i)
            ffn_aT(fd, 2, DENSE_BLOCKS - 1, 0)
            hi_unit(act, BASE_MIX[1] + 1)
            mixer(1)
            act.wait_ge(in_small, 48)
            copy(rt_hi[:, :, :], rt[:, :, :]).then_inc(rt_h, 1)
            hi_unit(act, BASE_MOE)
            norm(3, BASE_MOE + 1)
            act.wait_ge(hn_done, 8)
            copy(tok_hi[:, :, :], hn[:, :, :]).then_inc(tok_h, 1)
            act.wait_ge(lg_exp_in, 1)
            nc.scalar.activation(tw[:, :, 1:2], tw[:, :, 0:1], ACT.Exp).then_inc(lg_exp, 1)
            expert_start(0, BASE_MOE, 0, split_first=False)
            with act.Fori(0, N_EXP - 1) as e:
                d = e * (EXP_UNITS // RAW)
                expert_middle(e, BASE_MOE, d)
                expert_end(e, BASE_MOE, d, True)
                expert_out(e, BASE_MOE, d)
                hi_unit(act, BASE_MOE + 2, d + EXP_UNITS // RAW)
                ffn_block(fm, 1, (e + 1) * EXP_BLOCKS, 0, BASE_MOE + 2, d + EXP_UNITS // RAW)
                hi_unit(act, BASE_MOE + 3, d + EXP_UNITS // RAW)
            last = N_EXP - 1
            expert_middle(last, BASE_MOE, last * (EXP_UNITS // RAW))
            expert_end(last, BASE_MOE, last * (EXP_UNITS // RAW), False)
            expert_out(last, BASE_MOE, last * (EXP_UNITS // RAW))
            act.wait_ge(route_done, 1)
            n_over = act.value_load(over_i[0:1, 0:1], min_val=0, max_val=3)
            with act.If(n_over > 0):
                with act.Fori(0, n_over) as k:
                    e = k + N_EXP
                    d = k * (EXP_UNITS // RAW) + N_EXP * (EXP_UNITS // RAW)
                    expert_start(e, BASE_MOE, d)
                    expert_middle(e, BASE_MOE, d)
                    expert_end(e, BASE_MOE, d, False)
                    expert_out(e, BASE_MOE, d)
            norm(4)

        @block.vector
        def _(dve):
            chain = [0]

            def link(ins):
                chain[0] += 1
                ins.then_inc(dve_chain, 1)
                dve.wait_ge(dve_chain, chain[0])

            def rsqrt_mean(src, n, width, y):
                t = nwt[:, 0:n]
                link(nc.vector.tensor_scalar(src, src, 1.0 / width, EPS, ALU.mult, ALU.add))
                link(nc.vector.tensor_scalar(y.bitcast(I32), src.bitcast(I32), -0.5, RSQRT_BITS, ALU.mult, ALU.add))
                for _ in range(3):
                    link(nc.vector.scalar_tensor_tensor(out=t, in0=y, scalar=-0.5, in1=y, op0=ALU.mult, op1=ALU.mult))
                    link(nc.vector.tensor_tensor(t, t, src, ALU.mult))
                    link(nc.vector.scalar_tensor_tensor(out=y, in0=t, scalar=1.5, in1=y, op0=ALU.add, op1=ALU.mult))

            def norm(i, end=None, next_unit=None):
                def residual(t):
                    if t == 0:
                        dve.wait_ge(first_tile, i)
                    else:
                        used(dve, end)
                    for half in range(2):
                        ins = nc.vector.tensor_tensor(h[:, t, half * 512:(half + 1) * 512], h[:, t, half * 512:(half + 1) * 512],
                                                      ps[:, 2 * t + half, :], ALU.add)
                    ins.then_inc(res_done, 1)

                def scale(t):
                    dve.wait_ge(sq_act, 2 * i + t + 1)
                    rsqrt_mean(ss[:, t:t + 1], 1, D, rs[:, t:t + 1])
                    if i == 0:
                        dve.wait_ge(in_gain0, 16)
                    else:
                        dve.wait_ge(in_gain, 16 * i)
                    ins = nc.vector.scalar_tensor_tensor(out=hn[:, t, :], in0=h[:, t, :], scalar=rs[:, t:t + 1],
                                                         in1=gain[:, :], op0=ALU.mult, op1=ALU.mult)
                    ins.then_inc(fin_done if i == 4 else hn_done, 1)

                def lo(c):
                    t, half = c // 2, c % 2
                    dve.wait_ge(hnT_hi, 4 * i + c + 1)
                    hi = xT_hi[:, 4 * half:4 * half + 4, t * P:(t + 1) * P].bitcast(F32)
                    nc.vector.tensor_tensor(xT_lo[:, 4 * half:4 * half + 4, t * P:(t + 1) * P],
                                            ps[:, c, :].rearrange("p (k q) -> p k q", k=4), hi, ALU.subtract).then_inc(hnT_lo, 1)

                if end is not None:
                    residual(0)
                scale(0)
                if end is not None:
                    residual(1)
                    lo(0)
                    lo(1)
                scale(1)
                if i == 4:
                    return
                dve.wait_ge(hn_done, 2 * (i + 1))
                dve.sem_inc(gain_used, 1)
                if end is None:
                    lo(0)
                    lo(1)
                    lo_unit(dve, 0)
                    lo_unit(dve, 1)
                if next_unit is not None:
                    lo_unit(dve, next_unit)
                lo(2)
                lo(3)

            def rope_mults(first):
                x = ps[:, first:first + 2, :].rearrange("p t (h d) -> p t h d", h=HEADS)
                t1 = rope_t1[:, :, :].rearrange("p t (h d) -> p t h d", h=HEADS)
                t2 = rope_t2[:, :, :].rearrange("p t (h d) -> p t h d", h=HEADS)
                c = rope[:, 0].unsqueeze(2).to_broadcast([P, TT, HEADS, HD])
                s = rope[:, 1].unsqueeze(2).to_broadcast([P, TT, HEADS, HD])
                half = HD // 2
                nc.vector.tensor_tensor(t1, x, c, ALU.mult)
                nc.vector.tensor_tensor(t2[:, :, :, 0:half], x[:, :, :, half:HD], s[:, :, :, 0:half], ALU.mult)
                nc.vector.tensor_tensor(t2[:, :, :, half:HD], x[:, :, :, 0:half], s[:, :, :, half:HD],
                                        ALU.mult).then_inc(rope_mul, 1)

            def mixer(L):
                n0 = BASE_MIX[L]
                split = lambda j: lo_unit(dve, n0 + j)
                if L == 0:
                    norm(0)
                dve.wait_ge(wz_h, L + 1)
                nc.vector.tensor_tensor(wz_lo[:, :, :], wz[:, :, :], wz_hi[:, :, :].bitcast(F32), ALU.subtract).then_inc(wz_l, 1)
                if L == 0:
                    dve.wait_ge(in_cst, 16)
                    dve.wait_ge(in_small, 48)
                else:
                    norm(2, BASE_MIX[1])
                split(2)
                split(3)
                used(dve, n0 + 2)
                rope_mults(0)
                split(4)
                split(5)
                zl = ps[:, 6, SEQ:2 * SEQ].rearrange("p (t f) -> p t f", t=TT)
                used(dve, n0 + 4)
                dve.wait_ge(rope_add, 2 * L + 1)
                rope_mults(2)
                split(6)
                dve.wait_ge(zlog_done, L + 1)
                nc.vector.scalar_tensor_tensor(out=log_a[:, :, :], in0=zl, scalar=0.0, in1=z_log[:, :, :], op0=ALU.min,
                                               op1=ALU.subtract).then_inc(loga_done, 1)
                split(7)
                split(8)
                dve.wait_ge(b_ps, L + 1)
                nc.vector.tensor_copy(bcum[:, :], ps[:, 7, SEQ:2 * SEQ]).then_inc(b_cp, 1)
                dve.wait_ge(kT_ps, L + 1)
                nc.vector.tensor_copy(kT[:, :, :], ps[:, 6:8, :].rearrange("p b (a t) -> p (b a) t", a=2)).then_inc(kT_cp, 1)
                split(9)
                split(10)
                dve.wait_ge(b_cp, L + 1)
                for n, half in enumerate(LEVELS):
                    b3 = bcum[:, :].rearrange("p (i j) -> p i j", j=2 * half)
                    ref = b3[:, :, half - 1:half].to_broadcast([P, SEQ // (2 * half), 2 * half])
                    ins = nc.vector.tensor_tensor(dec[:, n, :].rearrange("p (i j) -> p i j", j=2 * half), b3, ref, ALU.subtract)
                ins.then_inc(dec_sub, 1)
                split(11)
                for step in range(HEADS + 4):
                    if step < HEADS:
                        b, pr = step % 2, probs[step % 3]
                        dve.wait_ge(s_ps, HEADS * L + step + 1)
                        if step >= 3:
                            dve.wait_ge(pT_ps, HEADS * L + step - 2)
                        nc.vector.tensor_tensor_reduce(out=pr[:, 0:P], in0=ps[:, 4 + b, 0:P], in1=lnc[:, 0:P], scale=1.0,
                                                       scalar=-3e38, op0=ALU.add, op1=ALU.max, accum_out=mx[:, b, 0:1])
                        link(nc.vector.tensor_tensor_reduce(out=pr[:, P:3 * P], in0=ps[:, 4 + b, P:3 * P],
                                                            in1=lnc[:, P:3 * P], scale=1.0, scalar=-3e38, op0=ALU.add,
                                                            op1=ALU.max, accum_out=mx[:, b, 1:2]))
                        nc.vector.tensor_scalar(nmx[:, b, :], mx[:, b, :], -1.0, None, ALU.mult).then_inc(s_max, 1)
                    if step == 1:
                        dve.wait_ge(dec_exp, L + 1)
                        dve.wait_ge(f_cp, 3 * L + 1)
                        nc.vector.tensor_tensor(qe[:, :, :], dec[:, :, :], g_qk[:, 0, :].unsqueeze(1).to_broadcast([P, 8, SEQ]),
                                                ALU.mult).then_inc(qe_done, 1)
                    if 1 <= step <= HEADS:
                        hd = step - 1
                        b, pr = hd % 2, probs[hd % 3]
                        dve.wait_ge(s_exp, HEADS * L + hd + 1)
                        link(nc.vector.reciprocal(rden[:, b, :], den[:, b, :]))
                        nc.vector.tensor_scalar(pr[:, 0:P], pr[:, 0:P], rden[:, b, 0:1], None, ALU.mult)
                        nc.vector.tensor_scalar(pr[:, P:3 * P], pr[:, P:3 * P], rden[:, b, 1:2], None,
                                                ALU.mult).then_inc(s_norm, 1)
                    if step in (3, 6, 8):
                        split({3: 12, 6: 13, 8: 14}[step])
                    if step == 9:
                        used(dve, n0 + 12)
                        dve.wait_ge(f_cp, 3 * L + 3)
                        link(nc.vector.tensor_tensor(cu, cc[:, :, :], ps[:, 2, :].rearrange("p (f t) -> p f t", f=2), ALU.mult))
                        for f in range(2):
                            u, y = cu[:, f, :], cy[:, f, :]
                            link(nc.vector.tensor_scalar(y, u, cw[:, L, f, 2:3], None, ALU.mult))
                            link(nc.vector.scalar_tensor_tensor(out=y[:, 1:SEQ], in0=u[:, 0:SEQ - 1], scalar=cw[:, L, f, 1:2],
                                                                in1=y[:, 1:SEQ], op0=ALU.mult, op1=ALU.add))
                            link(nc.vector.scalar_tensor_tensor(out=y[:, 2:SEQ], in0=u[:, 0:SEQ - 2], scalar=cw[:, L, f, 0:1],
                                                                in1=y[:, 2:SEQ], op0=ALU.mult, op1=ALU.add))
                        nc.vector.tensor_tensor(cy, cy, ps[:, 3, :].rearrange("p (f t) -> p f t", f=2),
                                                ALU.mult).then_inc(conv_out, 1)
                    if step >= 5 and step % 2 == 1:
                        pair = (step - 5) // 2
                        dve.wait_ge(att_hi, 4 * L + pair + 1)
                        nc.vector.tensor_tensor(mixT_lo[:, pair, :], ps[:, pair % 2, pair // 2 * SEQ:(pair // 2 + 1) * SEQ],
                                                mixT_hi[:, pair, :].bitcast(F32), ALU.subtract).then_inc(att_lo, 1)
                dve.wait_ge(conv_hi, L + 1)
                nc.vector.tensor_tensor(mixT_lo[:, 4:6, :], cy, mixT_hi[:, 4:6, :].bitcast(F32), ALU.subtract).then_inc(conv_lo, 1)
                dve.wait_ge(pool_chain, 2)
                for n in range(9):
                    dve.wait_ge(lv_ps, 9 * L + n + 1)
                    if n:
                        dve.wait_ge(lv_cp, 9 * L + n)
                    b0 = 4 - n % 2 * 4
                    src = ps[:, b0:b0 + 4, 0:SEQ].rearrange("p h (t q) -> p h t q", t=TT)
                    if n == 8:
                        nc.vector.tensor_copy(gax[:, :, :], src[:, :, 0, :]).then_inc(lv_cp, 1)
                        continue
                    for t in range(TT):
                        if n == 0:
                            m = msk[:, 7, :].unsqueeze(1).to_broadcast([P, GH, P])
                            ins = nc.vector.tensor_tensor(gat[:, :, t, :], src[:, :, t, :], m, ALU.mult)
                        else:
                            m = msk[:, n - 1, :].unsqueeze(1).to_broadcast([P, GH, P])
                            ins = nc.vector.copy_predicated(gat[:, :, t, :], m, src[:, :, t, :])
                        if t == 0:
                            continue
                        ins.then_inc(lv_cp, 1)
                dve.wait_ge(o_sq, L + 1)
                link(nc.vector.tensor_reduce(gss[:, :], osq.rearrange("p (g d) -> p g d", d=GV), AX_X, ALU.add))
                rsqrt_mean(gss[:, :], 8, GV, rs[:, :])
                og = cc[:, :, :].rearrange("p t (g d) -> p (t g) d", d=GV)
                link(nc.vector.tensor_tensor(og, ps[:, 4, :].rearrange("p (g d) -> p g d", d=GV),
                                             rs[:, :].unsqueeze(2).to_broadcast([P, 8, GV]), ALU.mult))
                dve.wait_ge(t_cp, 2 * (L + 1))
                nc.vector.tensor_tensor(cc[:, :, :], cc[:, :, :], gvo[:, :, SEQ:2 * SEQ], ALU.mult).then_inc(o_done, 1)
                split(15)
                for f in range(2):
                    dve.wait_ge(oT_hi, 2 * L + f + 1)
                    nc.vector.scalar_tensor_tensor(out=mixT_lo[:, 6 + f, :], in0=ps[:, 5 + f, 0:SEQ],
                                                   scalar=gg[:, L, f:f + 1], in1=mixT_hi[:, 6 + f, :].bitcast(F32),
                                                   op0=ALU.mult, op1=ALU.subtract).then_inc(oT_lo, 1)

            def ffn_block(S, tiles, B, par, n, d=0):
                for t in range(tiles):
                    s = t if tiles == 2 else par
                    dve.wait_ge(S.silu, B * tiles + (t + 1))
                    nc.vector.tensor_tensor(act_x[:, s, :], gate_x[:, s, :], ps[:, 4 + s, FB:2 * FB], ALU.mult).then_inc(S.mul, 1)

            def ffn_aT(S, tiles, B, par):
                dve.wait_ge(S.aT_hi, B + 1)
                if tiles == 2:
                    dst, hi = aT_lo[:, :, :, :], aT_hi[:, :, :, :]
                    src = ps[:, 6 + par, :].rearrange("p (t f q) -> p t f q", t=2, f=2)
                else:
                    dst, hi = aT_lo[:, par, :, :], aT_hi[:, par, :, :]
                    src = ps[:, 6 + par, 0:FB].rearrange("p (f q) -> p f q", f=2)
                nc.vector.tensor_tensor(dst, src, hi.bitcast(F32), ALU.subtract).then_inc(S.aT_lo, 1)

            def dispatch(e, over):
                for t in range(TT):
                    s = slot[:, t, e:e + 1] if isinstance(e, int) else slot[:, t, bass.ds(e, 1)]
                    ins = nc.vector.tensor_scalar(disp[:, t, :], iota, 128.0 if over else 0.0, s, ALU.add, ALU.is_equal)
                ins.then_inc(disp_done, 1)

            def gathered(e):
                dve.wait_ge(ga_ps, e + 1)
                nc.vector.tensor_copy(gath[:, 1, :], ps[:, 3, :]).then_inc(ga_dve, 1)

            def gather_lo(e, g):
                dve.wait_ge(ga_hi, e * 2 + (g + 1))
                nc.vector.tensor_tensor(xT_lo[:, 4 * g:4 * g + 4, 0:P], ps[:, 2 + g, :].rearrange("p (k s) -> p k s", k=4),
                                        xT_hi[:, 4 * g:4 * g + 4, 0:P].bitcast(F32), ALU.subtract).then_inc(ga_lo, 1)

            def slots(e):
                dve.wait_ge(slot_ps, e + 1)
                nc.vector.tensor_copy(slotT, ps[:, 2, 0:SEQ]).then_inc(slot_cp, 2)
                dve.wait_ge(y_free, e + 1)
                nc.vector.tensor_copy(w_slot[:, :], ps[:, 3, 0:1]).then_inc(slot_cp, 1)

            def scatter_add(e, t):
                dve.wait_ge(sc_ps, e * 2 + (t + 1))
                for half in range(2):
                    ins = nc.vector.tensor_tensor(h[:, t, half * 512:(half + 1) * 512], h[:, t, half * 512:(half + 1) * 512],
                                                  ps[:, 2 + half, :], ALU.add)
                ins.then_inc(sc_add, 1)

            def expert_start(e, n, d):
                gathered(e)
                for g in (0, 1):
                    gather_lo(e, g)
                lo_unit(dve, n + 2, d)
                ffn_block(fm, 1, e * EXP_BLOCKS, 0, n + 2, d)
                lo_unit(dve, n + 3, d)

            def expert_first(e, n, d, scatter):
                B = e * EXP_BLOCKS
                if scatter:
                    scatter_add(e - 1, 0)
                for p in range(2):
                    m = n + 4 + 3 * p
                    lo_unit(dve, m, d)
                    ffn_aT(fm, 1, B + p, p)
                    lo_unit(dve, m + 1, d)
                    ffn_block(fm, 1, B + p + 1, 1 - p, m, d)
                    if p == 0 and scatter:
                        scatter_add(e - 1, 1)
                    if p == 1:
                        slots(e)
                    lo_unit(dve, m + 2, d)

            def expert_rest(e, n, d):
                with dve.Fori(1, (EXP_BLOCKS - 2) // 2) as i:
                    for p in range(2):
                        B = e * EXP_BLOCKS + i * 2 + p
                        m = n + 4 + 3 * p
                        lo_unit(dve, m, d + i)
                        ffn_aT(fm, 1, B, p)
                        lo_unit(dve, m + 1, d + i)
                        ffn_block(fm, 1, B + 1, 1 - p, m, d + i)
                        lo_unit(dve, m + 2, d + i)

            def expert_end(e, n, d, follow):
                B = e * EXP_BLOCKS + (EXP_BLOCKS - 2)
                if follow:
                    dve.wait_ge(slot_ps, e + 1)
                    dispatch(e + 1, False)
                lo_unit(dve, n + EXP_UNITS - 2, d)
                ffn_aT(fm, 1, B, 0)
                lo_unit(dve, n + EXP_UNITS - 1, d)
                if follow:
                    gathered(e + 1)
                ffn_block(fm, 1, B + 1, 1, n + EXP_UNITS - 2, d)
                ffn_aT(fm, 1, B + 1, 1)
                if follow:
                    for g in (0, 1):
                        gather_lo(e + 1, g)
                        lo_unit(dve, n + g, d + EXP_UNITS // RAW)

            mixer(0)
            n0 = BASE_DENSE
            lo_unit(dve, n0)
            norm(1, BASE_DENSE, n0 + 1)
            lo_unit(dve, n0 + 2)
            ffn_block(fd, 2, 0, 0, n0 + 2)
            lo_unit(dve, n0 + 3)
            with dve.Fori(0, (DENSE_BLOCKS - 1) // 2) as i:
                for p in range(2):
                    B = i * 2 + p
                    m = n0 + 4 + 3 * p
                    lo_unit(dve, m, i)
                    ffn_aT(fd, 2, B, p)
                    lo_unit(dve, m + 1, i)
                    ffn_block(fd, 2, B + 1, 0, m, i)
                    lo_unit(dve, m + 2, i)
            ffn_aT(fd, 2, DENSE_BLOCKS - 1, 0)
            lo_unit(dve, BASE_MIX[1] + 1)
            mixer(1)
            lo_unit(dve, BASE_MOE)
            dve.wait_ge(rt_h, 1)
            nc.vector.tensor_tensor(rt_lo[:, :, :], rt[:, :, :], rt_hi[:, :, :].bitcast(F32), ALU.subtract).then_inc(rt_l, 1)
            norm(3, BASE_MOE, BASE_MOE + 1)
            dve.wait_ge(tok_h, 1)
            nc.vector.tensor_tensor(tok_lo[:, :, :], hn[:, :, :], tok_hi[:, :, :].bitcast(F32), ALU.subtract).then_inc(tok_l, 1)
            dve.wait_ge(lgT_ps, 1)
            nc.vector.tensor_copy(lgT, ps[0:N_EXP, 7, 0:SEQ]).then_inc(lgT_cp, 1)
            dve.wait_ge(lg_ps, 1)
            link(nc.vector.tensor_copy(lg[:, :, :], ps[:, 6, 0:16].rearrange("p (t e) -> p t e", t=TT)))
            for t in range(TT):
                link(nc.vector.max(mx8[:, t, :], lg[:, t, :]))
            for t in range(TT):
                ins = nc.vector.max_index(ix8[:, t, :], mx8[:, t, :], lg[:, t, :])
            link(ins)
            nc.vector.tensor_tensor(tw[:, :, 0:1], mx8[:, :, 1:2], mx8[:, :, 0:1], ALU.subtract).then_inc(lg_exp_in, 1)
            link(nc.vector.tensor_copy(ixf[:, :, :], ix8[:, :, 0:2]))
            for n, top in enumerate((top1, top2)):
                for t in range(TT):
                    ins = nc.vector.tensor_scalar(top[:, t, :], iota8, ixf[:, t, n:n + 1], None, ALU.is_equal)
            link(ins)
            nc.vector.tensor_tensor(chosen[:, :, :], top1[:, :, :], top2[:, :, :], ALU.add).then_inc(chosen_done, 1)
            dve.wait_ge(lg_exp, 1)
            link(nc.vector.tensor_scalar(tw[:, :, 2:3], tw[:, :, 1:2], 1.0, None, ALU.add))
            link(nc.vector.reciprocal(tw[:, :, 2:3], tw[:, :, 2:3]))
            link(nc.vector.tensor_tensor(tw[:, :, 3:4], tw[:, :, 1:2], tw[:, :, 2:3], ALU.mult))
            for t in range(TT):
                ins = nc.vector.tensor_scalar(comb[:, t, :], top1[:, t, :], tw[:, t, 2:3], None, ALU.mult)
            link(ins)
            for t in range(TT):
                ins = nc.vector.scalar_tensor_tensor(out=comb[:, t, :], in0=top2[:, t, :], scalar=tw[:, t, 3:4],
                                                     in1=comb[:, t, :], op0=ALU.mult, op1=ALU.add)
            link(ins)
            dve.wait_ge(chosen_done, 1)
            dve.wait_ge(pos_ps, 1)
            link(nc.vector.scalar_tensor_tensor(out=slot[:, :, :], in0=ps[:, 7, 0:16].rearrange("p (t e) -> p t e", t=TT),
                                                scalar=1.0, in1=chosen[:, :, :], op0=ALU.add, op1=ALU.mult))
            link(nc.vector.tensor_scalar(slot[:, :, :], slot[:, :, :], -1.0, None, ALU.add))
            link(nc.vector.tensor_scalar(flag[:, :], ps[:, 7, 16:24], float(P), None, ALU.is_gt))
            dispatch(0, False)
            link(nc.vector.tensor_tensor_scan(cum[:, :], flag[:, :], zero8[:, :], 0.0, ALU.add, ALU.add))
            link(nc.vector.tensor_copy(over_f[:, 0:1], cum[:, 7:8]))
            for k in range(3):
                link(nc.vector.scalar_tensor_tensor(out=sel[:, :], in0=cum[:, :], scalar=float(k + 1), in1=flag[:, :],
                                                    op0=ALU.is_equal, op1=ALU.mult))
                link(nc.vector.tensor_tensor_reduce(out=sel[:, :], in0=sel[:, :], in1=iota8, scale=1.0, scalar=0.0,
                                                    op0=ALU.mult, op1=ALU.add, accum_out=over_f[:, k + 1:k + 2]))
            nc.vector.tensor_copy(over_i[:, :], over_f[:, :]).then_inc(route_done, 1)
            expert_start(0, BASE_MOE, 0)
            expert_first(0, BASE_MOE, 0, False)
            with dve.Fori(0, N_EXP - 1) as e:
                d = e * (EXP_UNITS // RAW)
                expert_rest(e, BASE_MOE, d)
                expert_end(e, BASE_MOE, d, True)
                lo_unit(dve, BASE_MOE + 2, d + EXP_UNITS // RAW)
                ffn_block(fm, 1, (e + 1) * EXP_BLOCKS, 0, BASE_MOE + 2, d + EXP_UNITS // RAW)
                lo_unit(dve, BASE_MOE + 3, d + EXP_UNITS // RAW)
                expert_first(e + 1, BASE_MOE, d + EXP_UNITS // RAW, True)
            last = N_EXP - 1
            expert_rest(last, BASE_MOE, last * (EXP_UNITS // RAW))
            expert_end(last, BASE_MOE, last * (EXP_UNITS // RAW), False)
            for t in range(TT):
                scatter_add(last, t)
            dve.wait_ge(sc_add, 2 * N_EXP)
            dve.wait_ge(route_done, 1)
            n_over = dve.value_load(over_i[0:1, 0:1], min_val=0, max_val=3)
            with dve.If(n_over > 0):
                with dve.Fori(0, n_over) as k:
                    e = k + N_EXP
                    ex = dve.value_load(over_i[0:1, bass.ds(k + 1, 1)], min_val=0, max_val=N_EXP - 1)
                    d = k * (EXP_UNITS // RAW) + N_EXP * (EXP_UNITS // RAW)
                    dve.wait_ge(slot_ps, e)
                    dispatch(ex, True)
                    gathered(e)
                    for g in (0, 1):
                        gather_lo(e, g)
                        lo_unit(dve, BASE_MOE + g, d)
                    lo_unit(dve, BASE_MOE + 2, d)
                    ffn_block(fm, 1, e * EXP_BLOCKS, 0, BASE_MOE + 2, d)
                    lo_unit(dve, BASE_MOE + 3, d)
                    expert_first(e, BASE_MOE, d, False)
                    expert_rest(e, BASE_MOE, d)
                    expert_end(e, BASE_MOE, d, False)
                    for t in range(TT):
                        scatter_add(e, t)
                    dve.wait_ge(sc_add, e * 2 + 2)
            dve.sem_inc(res_done, 1)
            norm(4)

        @block.tensor
        def _(pe):
            def unit_ready(n, d=0):
                pe.wait_ge(lo_done, d * RAW + (n + 1))

            def norm(i, t):
                pe.wait_ge(hn_done, 2 * i + t + 1)
                for half in range(2):
                    for kk in range(4):
                        k = 4 * half + kk
                        last = nc.tensor.transpose(ps[:, 2 * t + half, kk * P:(kk + 1) * P], hn[:, t, k * P:(k + 1) * P], ident)
                    last.then_inc(hnT_ps, 1)

            def first_block(i, n, bank, first_done=None):
                norm(i, 0)
                for t in range(TT):
                    for half in range(2):
                        pe.wait_ge(hnT_lo, 4 * i + 2 * t + half + 1)
                        unit_ready(n + half)
                        for kk in range(4):
                            k = 4 * half + kk
                            for xp, wp in PASSES:
                                last = nc.tensor.matmul(ps[:, bank + t, :], (xT_hi, xT_lo)[xp][:, k, t * P:(t + 1) * P],
                                                        w(n + half, wp, kk * 512, (kk + 1) * 512),
                                                        start=(k == 0 and xp == wp), stop=(k == KT - 1 and wp == 1))
                        if t == 1:
                            last.then_inc(unit_used, 1)
                        elif half == 0:
                            norm(i, 1)
                        elif first_done is not None:
                            last.then_inc(first_done, 1)

            def narrow(dst, hi, lo):
                for k in range(KT):
                    for xp, wp in PASSES:
                        last = nc.tensor.matmul(dst, (hi, lo)[wp][:, k, :], (xT_hi, xT_lo)[xp][:, k, :],
                                                start=(k == 0 and xp == wp), stop=(k == KT - 1 and wp == 1))
                return last

            def tokens_first(n, half, bank):
                unit_ready(n)
                for t in range(TT):
                    for kk in range(4):
                        k = 4 * half + kk
                        for xp, wp in PASSES:
                            last = nc.tensor.matmul(ps[:, bank + t, :], (xT_hi, xT_lo)[xp][:, k, t * P:(t + 1) * P],
                                                    w(n, wp, kk * 512, (kk + 1) * 512),
                                                    start=(k == 0 and xp == wp), stop=(k == KT - 1 and wp == 1))
                last.then_inc(unit_used, 1)

            def features_first(n, half, bank):
                unit_ready(n)
                for kk in range(4):
                    k = 4 * half + kk
                    for f in range(4):
                        for xp, wp in PASSES:
                            last = nc.tensor.matmul(ps[:, bank + f // 2, f % 2 * SEQ:(f % 2 + 1) * SEQ],
                                                    w(n, wp, kk * 512 + f * P, kk * 512 + (f + 1) * P),
                                                    (xT_hi, xT_lo)[xp][:, k, :],
                                                    start=(k == 0 and f % 2 == 0 and xp == wp),
                                                    stop=(k == KT - 1 and wp == 1), skip_group_check=True)
                last.then_inc(unit_used, 1)

            def w_in_block(fn, n, bank):
                fn(n, 0, bank)
                fn(n + 1, 1, bank)

            def scores(L, hd):
                b, r, a = hd % 2, hd % 2 * HD, hd // 2
                if hd >= 2:
                    pe.wait_ge(s_max, HEADS * L + hd - 1)
                for t in range(TT):
                    last = nc.tensor.matmul(ps[:, 4 + b, P * t:P * t + (t + 1) * P], qT[r:r + HD, a, t * P:(t + 1) * P],
                                            kT[r:r + HD, a, 0:(t + 1) * P], start=True, stop=True)
                last.then_inc(s_ps, 1)

            def probs_T(L, hd):
                b, pr = hd % 2, probs[hd % 3]
                pe.wait_ge(s_norm, HEADS * L + hd + 1)
                if hd >= 2:
                    pe.wait_ge(pT_cp, HEADS * L + hd - 1)
                for c in range(3):
                    last = nc.tensor.transpose(ps[:, 6 + b, c * P:(c + 1) * P], pr[:, c * P:(c + 1) * P], ident)
                last.then_inc(pT_ps, 1)

            def weigh(L, hd):
                b, r, a = hd % 2, hd % 2 * HD, hd // 2
                pe.wait_ge(pT_cp, HEADS * L + hd + 1)
                if a >= 2:
                    pe.wait_ge(att_lo, 4 * L + a - 1)
                o = ps[r:r + HD, a % 2, a // 2 * SEQ:(a // 2 + 1) * SEQ]
                nc.tensor.matmul(o, v_sb[:, 0, hd * HD:(hd + 1) * HD], probsT[:, b, 0:SEQ], start=True, stop=True)
                nc.tensor.matmul(o[:, P:SEQ], v_sb[:, 1, hd * HD:(hd + 1) * HD], probsT[:, b, SEQ:3 * P], start=False,
                                 stop=True, skip_group_check=True).then_inc(att_ps, 1)

            def w_out(n, j, tiles=range(TT)):
                unit_ready(n)
                for kk in range(2):
                    k = 2 * j + kk
                    for t in tiles:
                        for half in range(2):
                            for xp, wp in PASSES:
                                last = nc.tensor.matmul(ps[:, 2 * t + half, :], (mixT_hi, mixT_lo)[xp][:, k, t * P:(t + 1) * P],
                                                        w(n, wp, kk * D + half * 512, kk * D + (half + 1) * 512),
                                                        start=(k == 0 and xp == wp), stop=(k == KT - 1 and wp == 1))
                if TT - 1 in tiles:
                    last.then_inc(unit_used, 1)
                return last

            def mixer(L):
                n0 = BASE_MIX[L]
                first_block(2 * L, n0, 0)
                pe.wait_ge(wz_l, L + 1)
                narrow(ps[0:RANK, 7, 0:SEQ], wz_hi, wz_lo).then_inc(zT_ps, 1)
                w_in_block(tokens_first, n0 + 2, 2)
                pe.wait_ge(zT_cp, L + 1)
                for t in range(TT):
                    last = nc.tensor.matmul(ps[:, 6, SEQ + t * P:SEQ + (t + 1) * P], zT[:, t * P:(t + 1) * P], wg[:, :],
                                            start=True, stop=True)
                last.then_inc(zl_ps, 1)
                pe.wait_ge(rope_mul, 2 * L + 1)
                w_in_block(tokens_first, n0 + 4, 0)
                pe.wait_ge(loga_done, L + 1)
                nc.tensor.matmul(ps[:, 7, SEQ:2 * SEQ], log_a[:, 0, :], tri_ones, start=True, stop=True)
                nc.tensor.matmul(ps[:, 7, SEQ + P:2 * SEQ], log_a[:, 1, :], tri, start=False, stop=True,
                                 skip_group_check=True).then_inc(b_ps, 1)
                pe.wait_ge(rope_mul, 2 * L + 2)
                w_in_block(features_first, n0 + 6, 2)
                for n, (rot, bank, done) in enumerate(((rot_q, 4, qT_ps), (rot_k, 6, kT_ps))):
                    pe.wait_ge(rope_add, 2 * L + n + 1)
                    if n:
                        pe.wait_ge(b_cp, L + 1)
                    for a in range(4):
                        for t in range(TT):
                            last = nc.tensor.transpose(ps[:, bank + a // 2, a % 2 * SEQ + t * P:a % 2 * SEQ + (t + 1) * P],
                                                       rot[:, t, a * P:(a + 1) * P], ident)
                    last.then_inc(done, 1)
                pe.wait_ge(v_cp, L + 1)
                w_in_block(tokens_first, n0 + 8, 0)
                pe.wait_ge(qT_cp, L + 1)
                pe.wait_ge(kT_cp, L + 1)
                for step in range(HEADS + 3):
                    if step < HEADS:
                        scores(L, step)
                    if step == 1:
                        pe.wait_ge(f_cp, 3 * (L + 1))
                        features_first(n0 + 10, 0, 2)
                    if step == 3:
                        features_first(n0 + 11, 1, 2)
                    if 2 <= step <= HEADS + 1:
                        probs_T(L, step - 2)
                    if step >= 3:
                        if step == 3:
                            pe.wait_ge(t_cp, 2 * (L + 1))
                        weigh(L, step - 3)
                for n in range(9):
                    if n == 0:
                        pe.wait_ge(pT_cp, HEADS * (L + 1))
                        pe.wait_ge(f_cp, 3 * L + 2)
                    if n == 1:
                        pe.wait_ge(att_lo, 4 * (L + 1))
                        pe.wait_ge(conv_out, L + 1)
                        pe.wait_ge(qe_done, L + 1)
                        pe.wait_ge(ke_done, L + 1)
                    if n >= 2:
                        pe.wait_ge(lv_cp, 9 * L + n - 1)
                    for hh in range(GH):
                        r = slice(GK * hh, GK * (hh + 1))
                        for t in range(1 if n == 8 else TT):
                            if n == 0:
                                lhsT, rhs = g_qk[r, 1, t * P:(t + 1) * P], g_qk[r, 0, t * P:(t + 1) * P]
                            elif n == 8:
                                lhsT, rhs = ke[r, 0, 0:P], qe[r, 0, P:2 * P]
                            else:
                                lhsT, rhs = ke[r, n, t * P:(t + 1) * P], qe[r, n, t * P:(t + 1) * P]
                            last = nc.tensor.matmul(ps[:, 4 - n % 2 * 4 + hh, t * P:(t + 1) * P], lhsT, rhs, start=True, stop=True,
                                                    tile_position=(GK * hh, 0))
                    last.then_inc(lv_ps, 1)
                pe.wait_ge(lv_cp, 9 * L + 8)
                w_out(n0 + 12, 0)
                pe.wait_ge(lv_cp, 9 * (L + 1))
                for t in range(TT):
                    for hh in range(GH):
                        o = ps[:, 4, t * SEQ + hh * GV:t * SEQ + (hh + 1) * GV]
                        last = nc.tensor.matmul(o, gat[:, hh, t, :], gvo[:, t, hh * GV:(hh + 1) * GV], start=True, stop=(t == 0))
                        if t == 1:
                            last = nc.tensor.matmul(o, gax[:, hh, :], gvo[:, 0, hh * GV:(hh + 1) * GV], start=False, stop=True)
                last.then_inc(o_ps, 1)
                w_out(n0 + 13, 1)
                pe.wait_ge(o_done, L + 1)
                for f in range(2):
                    for t in range(TT):
                        last = nc.tensor.transpose(ps[:, 5 + f, t * P:(t + 1) * P], cc[:, t, f * P:(f + 1) * P], ident)
                last.then_inc(oT_ps, 1)
                pe.wait_ge(conv_lo, L + 1)
                w_out(n0 + 14, 2, (0,))
                pe.wait_ge(oT_lo, 2 * (L + 1))
                w_out(n0 + 15, 3, (0,)).then_inc(first_tile, 1)
                w_out(n0 + 14, 2, (1,))
                w_out(n0 + 15, 3, (1,))

            def gate_up(S, tiles, B, par, n, d, wait_mul=True, slots_of=None):
                for half in range(2):
                    if slots_of is not None:
                        pe.wait_ge(ga_lo, slots_of * 2 + (half + 1))
                    unit_ready(n + half, d)
                    for t in range(tiles):
                        s = t if tiles == 2 else par
                        if half == 0 and wait_mul:
                            pe.wait_ge(S.mul, (B - 1) * 2 + (t + 1) if tiles == 2 else B - 1)
                        for kk in range(4):
                            k = 4 * half + kk
                            for xp, wp in PASSES:
                                last = nc.tensor.matmul(ps[:, 4 + s, :], (xT_hi, xT_lo)[xp][:, k, t * P:(t + 1) * P],
                                                        w((n + half), wp, kk * 512, (kk + 1) * 512),
                                                        start=(k == 0 and xp == wp), stop=(k == KT - 1 and wp == 1))
                        if half == 1 and t < tiles - 1:
                            last.then_inc(S.gu_first, 1)
                    last.then_inc(unit_used, 1)
                    if half == 0:
                        yield

            def act_T(S, tiles, B, par):
                pe.wait_ge(S.mul, (B + 1) * tiles)
                for t in range(tiles):
                    s = t if tiles == 2 else par
                    for f in range(2):
                        c = t * FB + f * P
                        last = nc.tensor.transpose(ps[:, 6 + par, c:c + P], act_x[:, s, f * P:(f + 1) * P], ident)
                last.then_inc(S.aT_ps, 1)

            def down(S, tiles, B, par, n, d, first, final):
                unit_ready(n, d)
                pe.wait_ge(S.aT_lo, B + 1)
                by_tile = final and tiles == 2
                for t, f in [(t, f) for t in range(tiles) for f in range(2)] if by_tile else \
                        [(t, f) for f in range(2) for t in range(tiles)]:
                    s = t if tiles == 2 else par
                    for half in range(2):
                        for xp, wp in PASSES:
                            last = nc.tensor.matmul(ps[:, 2 * t + half, :], (aT_hi, aT_lo)[xp][:, s, f, :],
                                                    w(n, wp, f * D + half * 512, f * D + (half + 1) * 512),
                                                    start=(first and f == 0 and xp == wp),
                                                    stop=(final and f == 1 and wp == 1), skip_group_check=True)
                    if by_tile and (t, f) == (0, 1):
                        last.then_inc(first_tile, 1)
                last.then_inc(unit_used, 1)

            def step(S, tiles, B, p, n, d, first, final=False, wait_mul=True, gather_for=None):
                gu = gate_up(S, tiles, B + 1, 1 - p, n, d, wait_mul)
                next(gu)
                if gather_for is not None:
                    gather(gather_for)
                act_T(S, tiles, B, p)
                for _ in gu:
                    pass
                down(S, tiles, B, p, n + 2, d, first, final)

            def gather(e):
                pe.wait_ge(disp_done, e + 1)
                if not isinstance(e, int) or e > 0:
                    pe.wait_ge(slot_cp, e * 3)
                for half in range(2):
                    for t in range(TT):
                        for part, src in enumerate((tok_hi, tok_lo)):
                            last = nc.tensor.matmul(ps[:, 2 + half, :], disp[:, t, :], src[:, t, half * 512:(half + 1) * 512],
                                                    start=(t + part == 0), stop=(t + part == TT))
                last.then_inc(ga_ps, 1)

            def gather_T(e):
                pe.wait_ge(ga_act, e + 1)
                pe.wait_ge(ga_dve, e + 1)
                for half in range(2):
                    for kk in range(4):
                        last = nc.tensor.transpose(ps[:, 2 + half, kk * P:(kk + 1) * P], gath[:, half, kk * P:(kk + 1) * P],
                                                   ident)
                    last.then_inc(gaT_ps, 1)

            def slot_tables(e, col):
                for t in range(TT):
                    nc.tensor.transpose(ps[:, 2, t * P:(t + 1) * P], disp[:, t, :].bitcast(F32), ident)
                for t in range(TT):
                    c = comb[:, t, col:col + 1] if isinstance(col, int) else comb[:, t, bass.ds(col, 1)]
                    last = nc.tensor.matmul(ps[:, 3, 0:1], disp[:, t, :].bitcast(F32), c, start=(t == 0),
                                            stop=(t == TT - 1))
                last.then_inc(slot_ps, 1)

            def scatter(e, t):
                for half in range(2):
                    last = nc.tensor.matmul(ps[:, 2 + half, :], slotT[:, t * P:(t + 1) * P], ys[:, half * 512:(half + 1) * 512],
                                            start=True, stop=True)
                last.then_inc(sc_ps, 1)

            def expert_start(e, n, d):
                gather(e)
                gather_T(e)
                for _ in gate_up(fm, 1, e * EXP_BLOCKS, 0, n, d, wait_mul=False, slots_of=e):
                    pass

            def expert_first(e, col, n, d, scatter_before):
                B0 = e * EXP_BLOCKS
                pe.wait_ge(y_free, e + 1)
                if scatter_before:
                    scatter(e - 1, 0)
                step(fm, 1, B0, 0, n + 2, d, True, wait_mul=False)
                if scatter_before:
                    pe.wait_ge(sc_add, e * 2 - 1)
                    scatter(e - 1, 1)
                step(fm, 1, B0 + 1, 1, n + 5, d, False)
                if scatter_before:
                    pe.wait_ge(sc_add, e * 2)
                slot_tables(e, col)

            def expert_rest(e, n, d, follow):
                B0 = e * EXP_BLOCKS
                with pe.Fori(1, (EXP_BLOCKS - 2) // 2) as i:
                    for p in range(2):
                        step(fm, 1, B0 + i * 2 + p, p, n + 2 + 3 * p, d + i, False)
                step(fm, 1, B0 + (EXP_BLOCKS - 2), 0, n + EXP_UNITS - 4, d, False, gather_for=e + 1 if follow else None)

            def expert_last(e, n, d, follow):
                B = e * EXP_BLOCKS + (EXP_BLOCKS - 1)
                act_T(fm, 1, B, 1)
                if follow:
                    gather_T(e + 1)
                down(fm, 1, B, 1, n + EXP_UNITS - 1, d, False, True)

            pe.wait_ge(in_cst, 16)
            mixer(0)
            n0 = BASE_DENSE
            first_block(1, n0, 4, fd.gu_first)
            step(fd, 2, 0, 0, n0 + 2, 0, True)
            step(fd, 2, 1, 1, n0 + 5, 0, False)
            with pe.Fori(1, (DENSE_BLOCKS - 1) // 2) as i:
                for p in range(2):
                    step(fd, 2, i * 2 + p, p, n0 + 2 + 3 * p, i, False)
            act_T(fd, 2, DENSE_BLOCKS - 1, 0)
            down(fd, 2, DENSE_BLOCKS - 1, 0, n0 + DENSE_UNITS - 1, 0, False, True)
            mixer(1)
            norm(3, 0)
            norm(3, 1)
            pe.wait_ge(hnT_lo, 16)
            pe.wait_ge(rt_l, 1)
            narrow(ps[0:N_EXP, 7, 0:SEQ], rt_hi, rt_lo).then_inc(lgT_ps, 1)
            pe.wait_ge(lgT_cp, 1)
            for t in range(TT):
                last = nc.tensor.transpose(ps[:, 6, t * N_EXP:(t + 1) * N_EXP], lgT[:, t * P:(t + 1) * P], ident[0:N_EXP, 0:N_EXP])
            last.then_inc(lg_ps, 1)
            pe.wait_ge(chosen_done, 1)
            nc.tensor.matmul(ps[:, 7, 0:8], stri, chosen[:, 0, :], start=True, stop=True)
            nc.tensor.matmul(ps[:, 7, 8:16], ones, chosen[:, 0, :], start=True, stop=False)
            nc.tensor.matmul(ps[:, 7, 8:16], stri, chosen[:, 1, :], start=False, stop=True)
            nc.tensor.matmul(ps[:, 7, 16:24], ones, chosen[:, 0, :], start=True, stop=False)
            nc.tensor.matmul(ps[:, 7, 16:24], ones, chosen[:, 1, :], start=False, stop=True).then_inc(pos_ps, 1)
            pe.wait_ge(tok_l, 1)
            expert_start(0, BASE_MOE, 0)
            expert_first(0, 0, BASE_MOE, 0, False)
            with pe.Fori(0, N_EXP - 1) as e:
                d = e * (EXP_UNITS // RAW)
                expert_rest(e, BASE_MOE, d, True)
                expert_last(e, BASE_MOE, d, True)
                for _ in gate_up(fm, 1, (e + 1) * EXP_BLOCKS, 0, BASE_MOE, d + EXP_UNITS // RAW, wait_mul=False,
                                 slots_of=e + 1):
                    pass
                expert_first(e + 1, e + 1, BASE_MOE, d + EXP_UNITS // RAW, True)
            last_e = N_EXP - 1
            expert_rest(last_e, BASE_MOE, last_e * (EXP_UNITS // RAW), False)
            expert_last(last_e, BASE_MOE, last_e * (EXP_UNITS // RAW), False)
            pe.wait_ge(y_free, N_EXP + 1)
            scatter(last_e, 0)
            pe.wait_ge(sc_add, 2 * N_EXP - 1)
            scatter(last_e, 1)
            pe.wait_ge(route_done, 1)
            n_over = pe.value_load(over_i[0:1, 0:1], min_val=0, max_val=3)
            with pe.If(n_over > 0):
                with pe.Fori(0, n_over) as k:
                    e = k + N_EXP
                    ex = pe.value_load(over_i[0:1, bass.ds(k + 1, 1)], min_val=0, max_val=N_EXP - 1)
                    d = k * (EXP_UNITS // RAW) + N_EXP * (EXP_UNITS // RAW)
                    pe.wait_ge(sc_add, e * 2)
                    expert_start(e, BASE_MOE, d)
                    expert_first(e, ex, BASE_MOE, d, False)
                    expert_rest(e, BASE_MOE, d, False)
                    expert_last(e, BASE_MOE, d, False)
                    pe.wait_ge(y_free, e + 2)
                    scatter(e, 0)
                    pe.wait_ge(sc_add, e * 2 + 1)
                    scatter(e, 1)


def lay_out(inp):
    a = {k: np.asarray(v) for k, v in inp.items()}

    def by_unit(m, width):
        rows = UNIT // width
        k = m.shape[0] // (P * rows)
        u = m.reshape(k, rows, P, m.shape[1] // width, width).transpose(3, 0, 2, 1, 4)
        return u.reshape(-1, P, UNIT)

    def ffn(g, u, d):
        nb = g.shape[1] // FB
        gu = np.stack([g.reshape(D, nb, FB), u.reshape(D, nb, FB)], 2).reshape(D, nb * 2 * FB)
        gu = by_unit(gu, 2 * FB).reshape(nb, 2, P, UNIT)
        dn = by_unit(d, D)
        out = [gu[0]]
        for b in range(1, nb):
            out += [gu[b], dn[b - 1:b]]
        return out + [dn[nb - 1:nb]]

    order = ((0, 1536), (2304, 2560), (1792, 2048), (2560, 3072), (2048, 2304), (1536, 1792))
    units = []
    for L in range(DEPTH):
        w_in = np.concatenate([a["w_in"][L][:, s:e] for s, e in order], 1)
        units += [by_unit(w_in, 512), by_unit(a["w_out"][L], D)]
        if L % 2 == 0:
            units += ffn(a["dense_w_gate"][L // 2], a["dense_w_up"][L // 2], a["dense_w_down"][L // 2])
        else:
            for e in range(N_EXP):
                units += ffn(a["exp_w_gate"][L // 2, e], a["exp_w_up"][L // 2, e], a["exp_w_down"][L // 2, e])
    consts, masks = shape_constants()
    z = a["w_in"][:, :, 3072:].reshape(DEPTH, KT, P, RANK).transpose(0, 2, 1, 3)
    gate = np.concatenate([a["w_gate_lr"], a["b_gate_lr"][:, None, :]], 1)
    conv = a["conv_w"].reshape(DEPTH, 3, 2, P).transpose(3, 0, 2, 1)
    gla_gain = a["gla_norm"].reshape(DEPTH, 2, P).transpose(2, 0, 1)
    gains = np.stack([a["mix_norm"][0], a["ffn_norm"][0], a["mix_norm"][1], a["ffn_norm"][1], a["final_norm"]])
    router = a["router"][0].reshape(KT, P, N_EXP).transpose(1, 0, 2)
    return {"x": a["x"], "stream": np.concatenate(units, 0), "w_z": z, "w_gate": gate, "conv_w": conv, "gla_gain": gla_gain,
            "gains": gains, "router": router, "consts": consts, "masks": masks}


def kernel(**inputs):
    import concourse.bacc as bacc
    from concourse.bass_utils import run_bass_kernel_spmd

    nc = bacc.Bacc("TRN2", target_bir_lowering=False, num_devices=1)
    arrays, args = {}, []
    for name, v in lay_out(inputs).items():
        v = np.ascontiguousarray(v)
        arrays[f"in_{name}"] = v
        args.append(nc.dram_tensor(f"in_{name}", v.shape, mybir.dt.from_np(v.dtype), kind="ExternalInput").ap())
    out = nc.dram_tensor("out_0", (1, SEQ, D), F32, kind="ExternalOutput").ap()
    build(nc, *args, out)
    r = run_bass_kernel_spmd(nc, [arrays], core_ids=[0])
    return r.results[0]["out_0"]
```
